# Optimizing a Trainium2 kernel written in Bass

```python
import math
import jax, jax.numpy as jnp
from jax import lax
import numpy as np

D_MODEL = 1024
BATCH = 1
SEQ = 1024
DEPTH = 1

N_META = 16
BLOCK_Q = 128
HEAD_DIM = 64
N_HEADS_DIFF = 8
DIFF_V_DIM = 2 * HEAD_DIM
D_QK_DIFF = 2 * N_HEADS_DIFF * HEAD_DIM
D_DIFF = N_HEADS_DIFF * DIFF_V_DIM
N_HEADS_SB = 16
D_SB = N_HEADS_SB * HEAD_DIM
D_FF = 4 * D_MODEL
ROPE_THETA = 10000.0
EPS = 1e-6
IN_SIZES = [D_QK_DIFF, D_QK_DIFF, D_DIFF, D_SB, D_SB, D_SB, D_MODEL, D_MODEL]
D_IN = sum(IN_SIZES)

kernel_name = "hybrid_diffattn_stickbreaking_gated"

def lambda_init_fn(layer_idx):
    return 0.8 - 0.6 * math.exp(-0.3 * layer_idx)

def rmsnorm(x, g):
    xf = x.astype(jnp.float32)
    y = xf * lax.rsqrt(jnp.mean(xf * xf, axis=-1, keepdims=True) + EPS)
    return (y * g.astype(jnp.float32)).astype(x.dtype)

def rope(x, pos):
    d = x.shape[-1]
    inv = ROPE_THETA ** (-jnp.arange(0, d, 2, dtype=jnp.float32) / d)
    ang = pos.astype(jnp.float32)[:, None] * inv[None, :]
    cos, sin = jnp.cos(ang), jnp.sin(ang)
    xf = x.astype(jnp.float32)
    x1, x2 = xf[..., : d // 2], xf[..., d // 2:]
    out = jnp.concatenate([x1 * cos - x2 * sin, x2 * cos + x1 * sin], axis=-1)
    return out.astype(x.dtype)

def block_bounds():
    bounds = [(0, N_META)]
    for s in range(0, SEQ, BLOCK_Q):
        bounds.append((N_META + s, N_META + min(SEQ, s + BLOCK_Q)))
    return bounds

def diff_attn_block(qa, ka, va, lam, start, end):
    B = qa.shape[0]
    tq = end - start
    s = jnp.einsum('bhqd,bhkd->bhqk', qa[:, :, start:end], ka[:, :, :end]).astype(jnp.float32)
    s = s / math.sqrt(HEAD_DIM)
    causal = jnp.arange(start, end)[:, None] >= jnp.arange(end)[None, :]
    p = jax.nn.softmax(jnp.where(causal, s, -jnp.inf), axis=-1)
    p = p.reshape(B, N_HEADS_DIFF, 2, tq, end)
    a = p[:, :, 0] - lam * p[:, :, 1]
    return jnp.einsum('bhqk,bhkd->bhqd', a.astype(va.dtype), va[:, :, :end])

def stick_breaking_block(qb, kb, vb, start, end):
    z = jnp.einsum('bhqd,bhkd->bhqk', qb[:, :, start:end], kb[:, :, :end]).astype(jnp.float32)
    z = z / math.sqrt(HEAD_DIM)
    strict = jnp.arange(end)[None, :] < jnp.arange(start, end)[:, None]
    log_1m = jnp.where(strict, jax.nn.log_sigmoid(-z), 0.0)
    rcum = lax.cumsum(log_1m, axis=3, reverse=True)
    excl = jnp.concatenate([rcum[..., 1:], jnp.zeros_like(rcum[..., :1])], axis=-1)
    log_a = jax.nn.log_sigmoid(z) + excl
    a = jnp.where(strict, jnp.exp(log_a), 0.0)
    return jnp.einsum('bhqk,bhkd->bhqd', a.astype(vb.dtype), vb[:, :, :end])

def setup_inputs(seed: int = 0) -> dict:
    key = jax.random.key(seed)
    ks = jax.random.split(key, 16)
    nrm = jax.random.normal
    f32 = jnp.float32
    return {
        "x": nrm(ks[0], (BATCH, SEQ, D_MODEL), f32),
        "meta_tokens": nrm(ks[1], (N_META, D_MODEL), f32),
        "norm_mix_g": 1.0 + 0.02 * nrm(ks[2], (DEPTH, D_MODEL), f32),
        "w_in": nrm(ks[3], (DEPTH, D_MODEL, D_IN), f32) * D_MODEL ** -0.5,
        "lambda_q1": 0.1 * nrm(ks[4], (DEPTH, HEAD_DIM), f32),
        "lambda_k1": 0.1 * nrm(ks[5], (DEPTH, HEAD_DIM), f32),
        "lambda_q2": 0.1 * nrm(ks[6], (DEPTH, HEAD_DIM), f32),
        "lambda_k2": 0.1 * nrm(ks[7], (DEPTH, HEAD_DIM), f32),
        "subln_g": 1.0 + 0.02 * nrm(ks[8], (DEPTH, DIFF_V_DIM), f32),
        "w_out_a": nrm(ks[9], (DEPTH, D_DIFF, D_MODEL), f32) * D_DIFF ** -0.5,
        "w_out_b": nrm(ks[10], (DEPTH, D_SB, D_MODEL), f32) * D_SB ** -0.5,
        "w_out": nrm(ks[11], (DEPTH, D_MODEL, D_MODEL), f32) * D_MODEL ** -0.5,
        "norm_mlp_g": 1.0 + 0.02 * nrm(ks[12], (DEPTH, D_MODEL), f32),
        "w_up": nrm(ks[13], (DEPTH, D_MODEL, D_FF), f32) * D_MODEL ** -0.5,
        "w_down": nrm(ks[14], (DEPTH, D_FF, D_MODEL), f32) * D_FF ** -0.5,
        "norm_final_g": 1.0 + 0.02 * nrm(ks[15], (D_MODEL,), f32),
    }

def reference(x, meta_tokens, norm_mix_g, w_in, lambda_q1, lambda_k1, lambda_q2, lambda_k2,
              subln_g, w_out_a, w_out_b, w_out, norm_mlp_g, w_up, w_down, norm_final_g):
    B = x.shape[0]
    meta = jnp.broadcast_to(meta_tokens.astype(x.dtype)[None], (B, N_META, D_MODEL))
    h = jnp.concatenate([meta, x], axis=1)
    L = h.shape[1]
    pos = jnp.arange(L, dtype=jnp.int32)
    split_idx = list(np.cumsum(IN_SIZES)[:-1])
    bounds = block_bounds()

    for layer in range(DEPTH):
        lam_init = lambda_init_fn(layer)
        hn = rmsnorm(h, norm_mix_g[layer])
        proj = hn @ w_in[layer]
        qa, ka, va, qb, kb, vb, ga, gb = jnp.split(proj, split_idx, axis=-1)
        qa = rope(qa.reshape(B, L, 2 * N_HEADS_DIFF, HEAD_DIM).transpose(0, 2, 1, 3), pos)
        ka = rope(ka.reshape(B, L, 2 * N_HEADS_DIFF, HEAD_DIM).transpose(0, 2, 1, 3), pos)
        va = va.reshape(B, L, N_HEADS_DIFF, DIFF_V_DIM).transpose(0, 2, 1, 3)
        qb = qb.reshape(B, L, N_HEADS_SB, HEAD_DIM).transpose(0, 2, 1, 3)
        kb = kb.reshape(B, L, N_HEADS_SB, HEAD_DIM).transpose(0, 2, 1, 3)
        vb = vb.reshape(B, L, N_HEADS_SB, HEAD_DIM).transpose(0, 2, 1, 3)
        lam = (jnp.exp(jnp.sum(lambda_q1[layer].astype(jnp.float32) * lambda_k1[layer].astype(jnp.float32)))
               - jnp.exp(jnp.sum(lambda_q2[layer].astype(jnp.float32) * lambda_k2[layer].astype(jnp.float32)))
               + lam_init)

        outs_a, outs_b = [], []
        for (s0, e0) in bounds:
            outs_a.append(diff_attn_block(qa, ka, va, lam, s0, e0))
            outs_b.append(stick_breaking_block(qb, kb, vb, s0, e0))
        oa = jnp.concatenate(outs_a, axis=2)
        ob = jnp.concatenate(outs_b, axis=2)
        oa = rmsnorm(oa, subln_g[layer]) * (1.0 - lam_init)
        oa = oa.transpose(0, 2, 1, 3).reshape(B, L, D_DIFF)
        ob = ob.transpose(0, 2, 1, 3).reshape(B, L, D_SB)
        ua = oa @ w_out_a[layer]
        ub = ob @ w_out_b[layer]
        merged = jax.nn.sigmoid(ga) * ua + jax.nn.sigmoid(gb) * ub
        h = h + merged @ w_out[layer]
        hm = rmsnorm(h, norm_mlp_g[layer])
        h = h + jnp.square(jax.nn.relu(hm @ w_up[layer])) @ w_down[layer]

    h = rmsnorm(h, norm_final_g)
    return h[:, N_META:]


_drawn_inputs = setup_inputs


def setup_inputs(seed=0):
    import zlib

    import numpy as np

    out = dict(_drawn_inputs(seed))
    spreads = {}
    factors = {'norm_mix_g': 3.14,
     'lambda_k1': 4.285,
     'lambda_q2': 4.548,
     'subln_g': 18.262,
     'norm_mlp_g': 10.147,
     'norm_final_g': 22.929}
    for name, (base, spread) in spreads.items():
        noise = np.random.default_rng([zlib.crc32(name.encode()), seed]).standard_normal(out[name].shape)
        drawn = base * np.exp(spread * noise) if base else spread * noise
        out[name] = __import__('jax').numpy.asarray(drawn.astype(out[name].dtype))
    for name, factor in factors.items():
        out[name] = (out[name] * factor).astype(out[name].dtype)
    return out
```

```python
from contextlib import ExitStack
import math

import numpy as np
import concourse.bass as bass
from concourse import mybir

F32 = mybir.dt.float32
F32R = mybir.dt.float32r
ALU = mybir.AluOpType
ACT = mybir.ActivationFunctionType
AXX = mybir.AxisListType.X

P = 128
BANK = 512
D = 1024
KT = D // P
META = 16
SEQ = 1024
L = META + SEQ
HD = 64
UNITS = 8
D_FF = 4 * D
EPS = 1e-6
LAM_INIT = 0.8 - 0.6 * math.exp(-0.3 * 0)
SCALE = 1.0 / math.sqrt(HD)
NEG = -1.0e30
ROPE_THETA = 10000.0

QA_COL, KA_COL, VA_COL = 0, D, 2 * D
QB_COL, KB_COL, VB_COL = 3 * D, 4 * D, 5 * D
GA_COL, GB_COL = 6 * D, 7 * D

Q_CHUNKS = [(META, 512), (META + 512, 512)]
K_CHUNKS = [(0, 352), (352, 344), (696, 344)]
QT = SEQ // P
KEY_TILES = QT + 1


def words(ap):
    return ap.bitcast(F32)


class Scratch:

    def __init__(self, nc):
        self.nc, self.ctx, self.used = nc, ExitStack(), []

    def __enter__(self):
        return self

    def __exit__(self, *a):
        if self.used and a[0] is None:
            self.nc.clear_and_free_semaphores(self.used)
            self.nc.all_engine_barrier()
        return self.ctx.__exit__(*a)

    def sb(self, name, shape, dt=F32):
        return self.ctx.enter_context(self.nc.sbuf_tensor(name, shape, dt))

    def sem(self, name):
        self.used.append(self.nc.alloc_semaphore(name))
        return self.used[-1]

    def sems(self, name, n):
        return [self.sem(f"{name}{i}") for i in range(n)]


def stage_norm(nc, ps, x, meta, norm_g, ident, hn_hi, hn_lo):
    with Scratch(nc) as s:
        xt = s.sb("n_xt", [P, QT + 1, D])
        sq = s.sb("n_sq", [P, D])
        ssum = s.sb("n_ssum", [P, QT + 1])
        rstd = s.sb("n_rstd", [P, QT + 1])
        g = s.sb("n_g", [P, KT])
        loaded = s.sems("n_loaded", QT + 1)
        g_loaded = s.sem("n_g_loaded")
        zeroed = s.sem("n_zeroed")
        summed, mean_eps, rooted = s.sem("n_summed"), s.sem("n_mean_eps"), s.sem("n_rooted")
        inverted, scaled = s.sem("n_inverted"), s.sem("n_scaled")
        turned, hi_done, lo_done = s.sem("n_turned"), s.sem("n_hi_done"), s.sem("n_lo_done")
        groups = []
        for kt in range(KT):
            groups.append((kt, 0, META, [QT]))
            groups.append((kt, META, 512, [0, 1, 2, 3]))
            groups.append((kt, META + 512, 512, [4, 5, 6, 7]))
        groups.sort(key=lambda q: q[1])
        with nc.Block() as block:
            @block.sync
            def _(sp):
                sp.dma_start(xt[0:META, QT, :], meta).then_inc(loaded[QT], 16)
                for t in range(QT):
                    sp.dma_start(xt[:, t, :], x[0, t * P:(t + 1) * P, :]).then_inc(loaded[t], 16)
                    if t == 0:
                        sp.dma_start(g[:, :], norm_g.rearrange("o (k p) -> p (o k)", p=P),
                                     allow_slow_non_contiguous=True).then_inc(g_loaded, 16)

            order = [QT] + list(range(QT))

            @block.scalar
            def _(act):
                for n, t in enumerate(order):
                    m = META if t == QT else P
                    act.wait_ge(loaded[t], 16)
                    if n:
                        act.wait_ge(summed, n)
                    act.activation(sq[0:m, :], xt[0:m, t, :], ACT.Square,
                                   accum_out=ssum[0:m, t:t + 1]).then_inc(summed, 1)
                    act.wait_ge(mean_eps, n + 1)
                    act.activation(rstd[0:m, t:t + 1], ssum[0:m, t:t + 1], ACT.Sqrt).then_inc(rooted, 1)
                act.wait_ge(g_loaded, 16)
                for n, (kt, c0, w, tiles) in enumerate(groups):
                    act.wait_ge(turned, n + 1)
                    act.activation(hn_hi[:, kt, c0:c0 + w], ps[n % 8][:, 0:w], ACT.Copy,
                                   scale=g[:, kt:kt + 1]).then_inc(hi_done, 1)

            @block.vector
            def _(dve):
                for n, t in enumerate(order):
                    m = META if t == QT else P
                    dve.wait_ge(summed, n + 1)
                    dve.tensor_scalar(ssum[0:m, t:t + 1], ssum[0:m, t:t + 1], 1.0 / D, EPS,
                                      ALU.mult, ALU.add).then_inc(mean_eps, 1)
                    dve.wait_ge(rooted, n + 1)
                    dve.reciprocal(rstd[0:m, t:t + 1], rstd[0:m, t:t + 1]).then_inc(inverted, 1)
                    dve.wait_ge(inverted, n + 1)
                    dve.tensor_scalar(xt[0:m, t, :], xt[0:m, t, :], rstd[0:m, t:t + 1], None,
                                      ALU.mult).then_inc(scaled, 1)
                dve.wait_ge(g_loaded, 16)
                for n, (kt, c0, w, tiles) in enumerate(groups):
                    dve.wait_ge(hi_done, n + 1)
                    dve.scalar_tensor_tensor(out=hn_lo[:, kt, c0:c0 + w], in0=ps[n % 8][:, 0:w],
                                             scalar=g[:, kt:kt + 1], in1=hn_hi[:, kt, c0:c0 + w],
                                             op0=ALU.mult, op1=ALU.subtract).then_inc(lo_done, 1)

            @block.tensor
            def _(pe):
                for n, (kt, c0, w, tiles) in enumerate(groups):
                    if n >= 8:
                        pe.wait_ge(lo_done, n - 7)
                    pe.wait_ge(scaled, order.index(tiles[-1]) + 1)
                    for i, t in enumerate(tiles):
                        m = META if t == QT else P
                        mm = pe.transpose(ps[n % 8][:, i * P:i * P + m], xt[0:m, t, kt * P:(kt + 1) * P],
                                          ident[0:m, 0:m])
                    mm.then_inc(turned, 1)


def product3(pe, bank, w_hi, w_lo, x_hi, x_lo, kts, first=True, last=True):
    for n, kt in enumerate(kts):
        pe.matmul(bank, w_lo(kt), x_hi(kt), start=(first and n == 0), stop=False)
        pe.matmul(bank, w_hi(kt), x_lo(kt), start=False, stop=False)
        mm = pe.matmul(bank, w_hi(kt), x_hi(kt), start=False, stop=(last and n == len(kts) - 1))
    return mm


def stage_channels(nc, ps, tag, w_in, cols, chunk_lists, hn_hi, hn_lo, rope, store, gate=None):
    chunks = [(w, t0, n) for w in range(2) for (t0, n) in chunk_lists[w]]
    C = len(chunks)
    first_of = [0, len(chunk_lists[0])]
    wv = w_in.rearrange("(k p) n -> p k n", p=P)
    with Scratch(nc) as s:
        w_raw = [s.sb(f"{tag}_w_raw{i}", [P, KT, P]) for i in range(2)]
        w_hi = [s.sb(f"{tag}_w_hi{i}", [P, KT, P], F32R) for i in range(2)]
        w_lo = [s.sb(f"{tag}_w_lo{i}", [P, KT, P], F32R) for i in range(2)]
        o_hi = s.sb(f"{tag}_o_hi", [P, C, BANK], F32 if gate else F32R)
        o_lo = None if gate else s.sb(f"{tag}_o_lo", [P, C, BANK], F32R)
        if rope:
            cos, sin = s.sb(f"{tag}_cos", [P, L]), s.sb(f"{tag}_sin", [P, L])
            swp = s.sb(f"{tag}_swp", [P, C, BANK])
            rot = s.sb(f"{tag}_rot", [P, C, BANK])
            rot2 = s.sb(f"{tag}_rot2", [P, C, BANK])
        w_loaded = s.sems(f"{tag}_w_loaded", 2)
        w_hi_done, w_lo_done = s.sems(f"{tag}_w_hi_done", 2), s.sems(f"{tag}_w_lo_done", 2)
        tables = s.sem(f"{tag}_tables")
        mm_done = s.sem(f"{tag}_mm_done")
        swapped, sin_done, cos_done, added = (s.sem(f"{tag}_swapped"), s.sem(f"{tag}_sin_done"),
                                              s.sem(f"{tag}_cos_done"), s.sem(f"{tag}_added"))
        hi_done, lo_done = s.sem(f"{tag}_hi_done"), s.sem(f"{tag}_lo_done")
        hi_stored, lo_stored = s.sems(f"{tag}_hi_stored", C), s.sems(f"{tag}_lo_stored", C)
        n_st = 1 if gate else 2

        with nc.Block() as block:
            @block.sync
            def _(sp):
                def load(u, w):
                    sp.dma_start(w_raw[w][:, :, :], wv[:, :, bass.ds(u * P + cols[w], P)]).then_inc(w_loaded[w], 16)

                if rope:
                    sp.dma_start(cos[:, :], rope[0]).then_inc(tables, 16)
                    sp.dma_start(sin[:, :], rope[1]).then_inc(tables, 16)
                load(0, 0)
                load(0, 1)

                def body(u, last):
                    for w in range(2):
                        if not last:
                            sp.wait_ge(w_lo_done[w], u + 1)
                            load(u + 1, w)
                    for c, (w, t0, n) in enumerate(chunks):
                        if gate:
                            sp.wait_ge(hi_done, u * C + (c + 1))
                            for dst, p0, m in store(u, w, 0, t0, n):
                                sp.dma_start(dst, words(o_hi[p0:p0 + m, c, 0:n])).then_inc(hi_stored[c], 16)
                        else:
                            sp.wait_ge(lo_done, u * C + (c + 1))
                            for dst, p0, m in store(u, w, 0, t0, n):
                                sp.dma_start(dst, words(o_hi[p0:p0 + m, c, 0:n])).then_inc(hi_stored[c], 16)
                            for dst, p0, m in store(u, w, 1, t0, n):
                                sp.dma_start(dst, words(o_lo[p0:p0 + m, c, 0:n])).then_inc(lo_stored[c], 16)

                with sp.Fori(0, UNITS - 1) as u:
                    body(u, False)
                body(UNITS - 1, True)
                for c in range(C):
                    sp.wait_ge(hi_stored[c], 16 * n_st * (UNITS + 1))
                    if not gate:
                        sp.wait_ge(lo_stored[c], 16 * n_st * (UNITS + 1))

            @block.scalar
            def _(act):
                def split(u, w):
                    act.wait_ge(w_loaded[w], u * 16 + 16)
                    act.wait_ge(mm_done, u * C + (first_of[w] + len(chunk_lists[w])))
                    act.activation(w_hi[w][:, :, :], w_raw[w][:, :, :], ACT.Copy).then_inc(w_hi_done[w], 1)

                def swap(u, c):
                    w, t0, n = chunks[c]
                    act.wait_ge(mm_done, (u + 1) * C + (c + 1))
                    act.wait_ge(added, u * C + (c + 1))
                    for q in range(4):
                        o, i = 32 * q, 32 * (q ^ 1)
                        last = act.activation(swp[o:o + 32, c, 0:n], ps[c][i:i + 32, 0:n], ACT.Copy)
                    last.then_inc(swapped, 1)

                def high(u, c):
                    w, t0, n = chunks[c]
                    act.wait_ge(hi_stored[c], (u + 1) * 16 * n_st)
                    if rope:
                        act.wait_ge(added, (u + 1) * C + (c + 1))
                        act.activation(o_hi[:, c, 0:n], rot[:, c, 0:n], ACT.Copy).then_inc(hi_done, 1)
                    else:
                        act.wait_ge(mm_done, (u + 1) * C + (c + 1))
                        act.activation(o_hi[:, c, 0:n], ps[c][:, 0:n],
                                       ACT.Sigmoid if gate else ACT.Copy).then_inc(hi_done, 1)

                def body(u, last):
                    split(u, 1)
                    for c in range(C + 1):
                        if rope and c < C:
                            swap(u, c)
                        if c == first_of[1] and not last:
                            split(u + 1, 0)
                        if rope and c >= 1:
                            high(u, c - 1)
                        if not rope and c < C:
                            high(u, c)

                act.sem_inc(mm_done, C)
                for c in range(C):
                    act.sem_inc(hi_stored[c], 16 * n_st)
                if rope:
                    act.sem_inc(added, C)
                split(0, 0)
                with act.Fori(0, UNITS - 1) as u:
                    body(u, False)
                body(UNITS - 1, True)

            @block.gpsimd
            def _(pool):
                def body(u):
                    for c, (w, t0, n) in enumerate(chunks):
                        pool.wait_ge(swapped, u * C + (c + 1))
                        pool.tensor_tensor(rot2[:, c, 0:n], swp[:, c, 0:n], sin[:, t0:t0 + n],
                                           ALU.mult).then_inc(sin_done, 1)
                if rope:
                    pool.wait_ge(tables, 32)
                    with pool.Fori(0, UNITS) as u:
                        body(u)

            @block.vector
            def _(dve):
                def split(u, w):
                    dve.wait_ge(w_hi_done[w], u + 1)
                    dve.tensor_tensor(w_lo[w][:, :, :], w_raw[w][:, :, :], w_hi[w][:, :, :],
                                      ALU.subtract).then_inc(w_lo_done[w], 1)

                def times_cos(u, c):
                    w, t0, n = chunks[c]
                    dve.wait_ge(swapped, u * C + (c + 1))
                    dve.wait_ge(hi_done, (u + 1) * C - C + c + 1)
                    dve.tensor_tensor(rot[:, c, 0:n], ps[c][:, 0:n], cos[:, t0:t0 + n],
                                      ALU.mult).then_inc(cos_done, 1)

                def add(u, c):
                    w, t0, n = chunks[c]
                    dve.wait_ge(sin_done, u * C + (c + 1))
                    dve.wait_ge(cos_done, u * C + (c + 1))
                    dve.tensor_tensor(rot[:, c, 0:n], rot[:, c, 0:n], rot2[:, c, 0:n], ALU.add).then_inc(added, 1)

                def low(u, c):
                    w, t0, n = chunks[c]
                    dve.wait_ge(lo_stored[c], (u + 1) * 16 * n_st)
                    dve.wait_ge(hi_done, (u + 1) * C + (c + 1) if rope else u * C + (c + 1))
                    src = rot[:, c, 0:n] if rope else ps[c][:, 0:n]
                    dve.tensor_tensor(o_lo[:, c, 0:n], src, o_hi[:, c, 0:n], ALU.subtract).then_inc(lo_done, 1)

                def body(u, last):
                    split(u, 1)
                    for c in range(C + 2):
                        if rope and c < C:
                            times_cos(u, c)
                        if c == first_of[1] and not last:
                            split(u + 1, 0)
                        if rope and 1 <= c <= C:
                            add(u, c - 1)
                        if rope and c >= 2:
                            low(u, c - 2)
                        if not rope and not gate and c < C:
                            low(u, c)

                if not gate:
                    for c in range(C):
                        dve.sem_inc(lo_stored[c], 16 * n_st)
                if rope:
                    dve.wait_ge(tables, 32)
                    dve.sem_inc(hi_done, C)
                split(0, 0)
                with dve.Fori(0, UNITS - 1) as u:
                    body(u, False)
                body(UNITS - 1, True)

            @block.tensor
            def _(pe):
                bank_free = cos_done if rope else (hi_done if gate else lo_done)

                def body(u, first):
                    for c, (w, t0, n) in enumerate(chunks):
                        if c in first_of:
                            pe.wait_ge(w_lo_done[w], u + 1)
                        if not first:
                            pe.wait_ge(bank_free, u * C - C + c + 1)
                        mm = product3(pe, ps[c][:, 0:n],
                                      lambda k: w_hi[w][:, k, :], lambda k: w_lo[w][:, k, :],
                                      lambda k: hn_hi[:, k, t0:t0 + n], lambda k: hn_lo[:, k, t0:t0 + n], range(KT))
                        mm.then_inc(mm_done, 1)

                body(0, True)
                with pe.Fori(1, UNITS) as u:
                    body(u, False)


def stage_values(nc, ps, w_in, hn_hi, hn_lo, v_dram):
    T = QT + 1
    GROUPS = 2
    UPG = BANK // P
    with Scratch(nc) as s:
        w_raw = s.sb("v_w_raw", [P, KT, BANK])
        w_hi, w_lo = s.sb("v_w_hi", [P, KT, BANK], F32R), s.sb("v_w_lo", [P, KT, BANK], F32R)
        out = s.sb("v_out", [P, T, UPG, 2 * P], F32R)
        w_loaded = s.sem("v_w_loaded")
        w_hi_done, w_lo_done = s.sem("v_w_hi_done"), s.sem("v_w_lo_done")
        mm_done, hi_done, lo_done = s.sem("v_mm_done"), s.sem("v_hi_done"), s.sem("v_lo_done")
        stored = s.sems("v_stored", T)
        wv = w_in.rearrange("(k p) n -> p k n", p=P)
        vd = v_dram.rearrange("(g u) t c -> g t u c", u=UPG)

        def rows(t):
            return (0, META) if t == QT else (META + t * P, P)

        with nc.Block() as block:
            @block.sync
            def _(sp):
                for b, col in enumerate((VA_COL, VB_COL)):
                    with sp.Fori(0, GROUPS) as g:
                        sp.wait_ge(w_lo_done, (b * GROUPS + g + 1) * KT)
                        sp.dma_start(w_raw[:, :, :], wv[:, :, bass.ds(g * BANK + col, BANK)]).then_inc(w_loaded, 16)
                        for t in range(T):
                            t0, m = rows(t)
                            if t < QT:
                                sp.wait_ge(lo_done, (b * GROUPS + g) * T + (t + 1 + (t == QT - 1)))
                            sp.dma_start(vd[g + b * GROUPS, t0:t0 + m, :, :],
                                         words(out[0:m, t, :, :])).then_inc(stored[t], 16)
                for t in range(T):
                    sp.wait_ge(stored[t], 16 * (2 * GROUPS + 1))

            @block.scalar
            def _(act):
                act.sem_inc(mm_done, T)
                for t in range(T):
                    act.sem_inc(stored[t], 16)
                for b in range(2):
                    with act.Fori(0, GROUPS) as g:
                        n = b * GROUPS + g
                        act.wait_ge(w_loaded, n * 16 + 16)
                        act.wait_ge(mm_done, n * T + T)
                        for k in range(KT):
                            act.activation(w_hi[:, k, :], w_raw[:, k, :], ACT.Copy).then_inc(w_hi_done, 1)
                        for t in range(T):
                            t0, m = rows(t)
                            act.wait_ge(mm_done, n * T + (T + t + 1))
                            act.wait_ge(stored[t], n * 16 + 16)
                            src = ps[t % 8][0:m, :].rearrange("p (u c) -> p u c", c=P)
                            act.activation(out[0:m, t, :, 0:HD], src[:, :, 0:HD], ACT.Copy)
                            act.activation(out[0:m, t, :, 3 * HD:4 * HD], src[:, :, HD:P], ACT.Copy).then_inc(hi_done, 1)

            @block.vector
            def _(dve):
                dve.sem_inc(w_lo_done, KT)
                for b in range(2):
                    with dve.Fori(0, GROUPS) as g:
                        n = b * GROUPS + g
                        for k in range(KT):
                            dve.wait_ge(w_hi_done, n * KT + (k + 1))
                            dve.tensor_tensor(w_lo[:, k, :], w_raw[:, k, :], w_hi[:, k, :],
                                              ALU.subtract).then_inc(w_lo_done, 1)
                        for t in range(T):
                            t0, m = rows(t)
                            dve.wait_ge(hi_done, n * T + (t + 1))
                            src = ps[t % 8][0:m, :].rearrange("p (u c) -> p u c", c=P)
                            dve.tensor_tensor(out[0:m, t, :, HD:2 * HD], src[:, :, 0:HD],
                                              out[0:m, t, :, 0:HD], ALU.subtract)
                            dve.tensor_tensor(out[0:m, t, :, 2 * HD:3 * HD], src[:, :, HD:P],
                                              out[0:m, t, :, 3 * HD:4 * HD], ALU.subtract).then_inc(lo_done, 1)

            @block.tensor
            def _(pe):
                def body(n, first):
                    for t in range(T):
                        t0, m = rows(t)
                        if t == 8:
                            pe.wait_ge(lo_done, n * T + 1)
                        elif t == 0 and not first:
                            pe.wait_ge(lo_done, n * T)
                        elif not first:
                            pe.wait_ge(lo_done, n * T - T + t + 1)
                        for k in range(KT):
                            if t == 0:
                                pe.wait_ge(w_lo_done, n * KT + (KT + k + 1))
                            pe.matmul(ps[t % 8][0:m, :], hn_hi[:, k, t0:t0 + m], w_lo[:, k, :],
                                      start=(k == 0), stop=False)
                            pe.matmul(ps[t % 8][0:m, :], hn_lo[:, k, t0:t0 + m], w_hi[:, k, :],
                                      start=False, stop=False)
                            mm = pe.matmul(ps[t % 8][0:m, :], hn_hi[:, k, t0:t0 + m], w_hi[:, k, :],
                                           start=False, stop=(k == KT - 1))
                        mm.then_inc(mm_done, 1)

                body(0, True)
                with pe.Fori(1, 2 * GROUPS) as n:
                    body(n, False)


def score_chunks(i):
    w = META + P * (i + 1)
    return {1: [(0, w)], 2: [(0, w // 2), (w // 2, w - w // 2)], 3: K_CHUNKS}[-(-w // BANK)]


def turn_groups(i):
    tiles = list(range(i + 2))
    return [tiles[n:n + 4] for n in range(0, len(tiles), 4)]


CHUNKS_BEFORE = [sum(len(score_chunks(j)) for j in range(i)) for i in range(QT + 1)]
GROUPS_BEFORE = [sum(len(turn_groups(j)) for j in range(i)) for i in range(QT + 1)]
CPU = 2 * CHUNKS_BEFORE[QT]
GPH = GROUPS_BEFORE[QT]


def key_col(tile):
    return 0 if tile == 0 else META + P * (tile - 1)


def chunk_no(i, h, c):
    return 2 * CHUNKS_BEFORE[i] + h * len(score_chunks(i)) + c


class UnitBuffers:

    def __init__(self, s, tag, v_parts):
        self.v_parts = v_parts
        self.LOADS = 2 + 8 + 2 * len(v_parts)
        self.q = [[s.sb(f"{tag}_q{p}{h}", [P, SEQ], F32R) for h in range(2)] for p in range(2)]
        self.k = [[[s.sb(f"{tag}_k{p}{h}{x}", [P, L], F32R) for x in range(2)] for h in range(2)] for p in range(2)]
        self.v = [s.sb(f"{tag}_v{p}", [P, KEY_TILES, 2 * P], F32R) for p in range(2)]
        self.loaded = s.sems(f"{tag}_loaded", 2)

    def zero_meta(self, dve, done):
        for p in range(2):
            dve.memset(self.v[p][:, 0, :].bitcast(F32), 0.0).then_inc(done, 1)

    def load(self, sp, u, p, q_dram, k_dram, v_dram, v_unit0):
        for h in range(2):
            sp.dma_start(words(self.q[p][h][:, :]), q_dram[u, h]).then_inc(self.loaded[p], 16)
            for x in range(2):
                for half in range(2):
                    sp.dma_start(words(self.k[p][h][x][half * HD:(half + 1) * HD, :]), k_dram[u, h, x]).then_inc(self.loaded[p], 16)
        for a, b, n in self.v_parts:
            sp.dma_start(words(self.v[p][0:META, 0, b:b + n]),
                         v_dram[u + v_unit0, 0:META, a:a + n]).then_inc(self.loaded[p], 16)
            sp.dma_start(words(self.v[p][:, 1:KEY_TILES, b:b + n]),
                         v_dram[u + v_unit0, META:L, a:a + n].rearrange("(j p) c -> p j c", p=P)).then_inc(self.loaded[p], 16)


def stage_diff(nc, ps, q_dram, k_dram, v_dram, o_dram, lams, subln_g, ident, ident_r, mask_r):
    LAG, RING = 2, 4
    S_BANKS, T_BANKS, PV_BANK, SUM_BANK = ps[0:4], ps[4:6], ps[6], ps[7]
    with Scratch(nc) as s:
        ub = UnitBuffers(s, "d", [(0, 0, HD), (3 * HD, HD, HD), (HD, P, P)])
        probs = s.sb("d_probs", [P, RING, 2, L])
        at_hi, at_lo = s.sb("d_at_hi", [P, KEY_TILES, 2 * P], F32R), s.sb("d_at_lo", [P, KEY_TILES, 2 * P], F32R)
        mx = s.sb("d_mx", [P, RING, 2, 4])
        neg_max = s.sb("d_neg_max", [P, RING, 2])
        row_sum = s.sb("d_row_sum", [P, RING, 2])
        weight = s.sb("d_weight", [P, RING, 2])
        coef = s.sb("d_coef", [P, RING])
        o_raw = s.sb("d_o_raw", [P, SEQ])
        o_sq = s.sb("d_o_sq", [P, BANK])
        o_rstd = s.sb("d_o_rstd", [P, BANK])
        o_norm = s.sb("d_o_norm", [P, BANK])
        o_hi, o_lo = s.sb("d_o_hi", [P, 2, BANK], F32R), s.sb("d_o_lo", [P, 2, BANK], F32R)
        ones = s.sb("d_ones", [P, P])
        lam_in = s.sb("d_lam_in", [1, 4, HD])
        lam_t = s.sb("d_lam_t", [1, HD])
        lam_s = s.sb("d_lam_s", [1, 8])
        neg_lam = s.sb("d_neg_lam", [P, 1])
        g8 = s.sb("d_g8", [P, 1])
        eps = s.sb("d_eps", [P, 1])
        small_loaded, prep = s.sem("d_small_loaded"), s.sem("d_prep")
        prep_exp, lam_ready, lam_spread = s.sem("d_prep_exp"), s.sem("d_lam_ready"), s.sem("d_lam_spread")
        scored, copied, shifted, exped = s.sem("d_scored"), s.sem("d_copied"), s.sem("d_shifted"), s.sem("d_exped")
        inverted, coef_done, scaled, mixed = s.sem("d_inverted"), s.sem("d_coef_done"), s.sem("d_scaled"), s.sem("d_mixed")
        turned, at_hi_done, at_lo_done = s.sem("d_turned"), s.sem("d_at_hi_done"), s.sem("d_at_lo_done")
        pv_done, o_copied, squared, summed = s.sem("d_pv_done"), s.sem("d_o_copied"), s.sem("d_squared"), s.sem("d_summed")
        normed = s.sem("d_normed")
        o_chain, o_hi_done, o_lo_done = s.sem("d_o_chain"), s.sem("d_o_hi_done"), s.sem("d_o_lo_done")
        o_stored = s.sems("d_o_stored", 2)

        def run(eng, unit, flush):
            unit(0, 0, 0, True)
            unit(0, 1, 1, False)
            with eng.Fori(1, UNITS // 2) as v:
                unit(v, 0, v * 2, False)
                unit(v, 1, v * 2 + 1, False)
            flush(UNITS - 1)

        with nc.Block() as block:
            @block.sync
            def _(sp):
                for n, l in enumerate(lams):
                    sp.dma_start(lam_in[:, n, :], l).then_inc(small_loaded, 16)
                sp.dma_start(g8[:, :], subln_g.rearrange("o p -> p o"), allow_slow_non_contiguous=True).then_inc(small_loaded, 16)
                sp.wait_ge(prep, 2)
                ub.load(sp, 0, 0, q_dram, k_dram, v_dram, 0)
                ub.load(sp, 1, 1, q_dram, k_dram, v_dram, 0)

                def stores(u):
                    for half in range(2):
                        sp.wait_ge(o_lo_done, u * 2 + (half + 3))
                        for x, src in enumerate((o_hi, o_lo)):
                            sp.dma_start(o_dram[x, bass.ds(u * P, P), half * BANK:(half + 1) * BANK],
                                         words(src[:, half, :])).then_inc(o_stored[half], 16)

                with sp.Fori(0, UNITS // 2 - 1) as v:
                    for p in range(2):
                        sp.wait_ge(pv_done, (v * 2 + (p + 1)) * 4 + 1)
                        ub.load(sp, v * 2 + (p + 2), p, q_dram, k_dram, v_dram, 0)
                        stores(v * 2 + p)
                for p in range(2):
                    stores(UNITS - 2 + p)
                for half in range(2):
                    sp.wait_ge(o_stored[half], 32 * (UNITS + 1))

            @block.tensor
            def _(pe):
                def scores(v, p, u, i):
                    for h in range(2):
                        for c, (k0, n) in enumerate(score_chunks(i)):
                            no = chunk_no(i, h, c)
                            bank = S_BANKS[no % 4]
                            pe.wait_ge(copied, u * CPU + (no + 1))
                            q = ub.q[p][h][:, i * P:(i + 1) * P]
                            last = c == len(score_chunks(i)) - 1
                            pe.matmul(bank[:, 0:n], q, ub.k[p][h][1][:, k0:k0 + n], start=True, stop=False)
                            mm = pe.matmul(bank[:, 0:n], q, ub.k[p][h][0][:, k0:k0 + n], start=False, stop=not last)
                            if last:
                                mm = pe.matmul(bank[:, n - P:n], ident_r[:, :], mask_r[:, :], start=False, stop=True)
                            mm.then_inc(scored, 1)

                def turn(u, i):
                    pe.wait_ge(mixed, u * QT + (i + 1))
                    for n, tiles in enumerate(turn_groups(i)):
                        no = GROUPS_BEFORE[i] + n
                        pe.wait_ge(at_lo_done, u * GPH + (no + 1))
                        for x, t in enumerate(tiles):
                            mm = pe.transpose(T_BANKS[no % 2][:, x * P:(x + 1) * P],
                                              probs[:, i % RING, 0, key_col(t):key_col(t) + P], ident[:, :])
                        mm.then_inc(turned, 1)

                def values(p, u, sp_):
                    pe.wait_ge(at_lo_done, u * GPH + (2 + GROUPS_BEFORE[2 * sp_ + 2]))
                    pe.wait_ge(o_copied, u * 4 + (sp_ + 1))
                    n_t = 2 * sp_ + 3
                    for t in range(n_t):
                        q0 = P if t == n_t - 1 else 0
                        v_hi, v_lo = ub.v[p][:, t, 0:P], ub.v[p][:, t, P:2 * P]
                        o = PV_BANK[:, q0:2 * P]
                        pe.matmul(o, v_lo, at_hi[:, t, q0:2 * P], start=(t == 0), stop=False)
                        pe.matmul(o, v_hi, at_lo[:, t, q0:2 * P], start=False, stop=False)
                        mm = pe.matmul(o, v_hi, at_hi[:, t, q0:2 * P], start=False, stop=(t == n_t - 1))
                    mm.then_inc(pv_done, 1)

                def sums(u, half):
                    pe.wait_ge(squared, u * 2 + (half + 1))
                    pe.wait_ge(o_lo_done, u * 2 + (half + 2))
                    pe.matmul(SUM_BANK[:, :], ones[:, :], o_sq[:, :], start=True, stop=True).then_inc(summed, 1)

                def lagged(p, u, i):
                    if i % 2 == 0 and i > 0:
                        values(p, u, i // 2 - 1)
                    turn(u, i)
                    if i == 5:
                        sums(u, 0)

                def unit(v, p, u, first):
                    pe.wait_ge(ub.loaded[p], (v + 1) * (16 * ub.LOADS))
                    for i in range(QT):
                        scores(v, p, u, i)
                        if i >= LAG:
                            lagged(p, u, i - LAG)
                        elif not first:
                            lagged(1 - p, u - 1, QT - LAG + i)
                            if i == LAG - 1:
                                values(1 - p, u - 1, 3)
                        if i == LAG and not first:
                            sums(u - 1, 1)

                def flush(u):
                    for i in range(QT - LAG, QT):
                        lagged(u % 2, u, i)
                    values(u % 2, u, 3)
                    sums(u, 1)

                pe.wait_ge(prep, 5)
                run(pe, unit, flush)

            @block.vector
            def _(dve):
                def copy_scores(u, i):
                    r = i % RING
                    for h in range(2):
                        for c, (k0, n) in enumerate(score_chunks(i)):
                            no = chunk_no(i, h, c)
                            dve.wait_ge(scored, u * CPU + (no + 1))
                            if c:
                                dve.wait_ge(copied, u * CPU + (no + 4))
                            dve.tensor_scalar(probs[:, r, h, k0:k0 + n], S_BANKS[no % 4][:, 0:n], 1.0,
                                              mx[:, r, h, c - 1:c] if c else None, ALU.mult, ALU.max,
                                              accum_out=mx[:, r, h, c:c + 1]).then_inc(copied, 1)
                        c = len(score_chunks(i)) - 1
                        dve.wait_ge(copied, u * CPU + (chunk_no(i, h, c) + 5))
                        dve.tensor_scalar(neg_max[:, r, h:h + 1], mx[:, r, h, c:c + 1], -SCALE, None,
                                          ALU.mult).then_inc(shifted, 1)

                def mix(u, i):
                    r, w = i % RING, META + P * (i + 1)
                    dve.wait_ge(exped, (u * QT + (i + 1)) * 2)
                    dve.reciprocal(weight[:, r, :], row_sum[:, r, :]).then_inc(inverted, 1)
                    dve.wait_ge(inverted, u * QT + (i + 1))
                    dve.tensor_scalar(coef[:, r:r + 1], weight[:, r, 1:2], neg_lam[:, 0:1], None,
                                      ALU.mult).then_inc(coef_done, 1)
                    dve.wait_ge(coef_done, u * QT + (i + 1))
                    dve.wait_ge(scaled, u * QT + (i + 1))
                    dve.scalar_tensor_tensor(out=probs[:, r, 0, 0:w], in0=probs[:, r, 1, 0:w],
                                             scalar=coef[:, r:r + 1], in1=probs[:, r, 0, 0:w],
                                             op0=ALU.mult, op1=ALU.add).then_inc(mixed, 1)

                def low(u, i):
                    for n, tiles in enumerate(turn_groups(i)):
                        no = GROUPS_BEFORE[i] + n
                        m, q0 = len(tiles), (i % 2) * P
                        dve.wait_ge(at_hi_done, u * GPH + (no + 1))
                        dve.tensor_tensor(at_lo[:, tiles[0]:tiles[0] + m, q0:q0 + P],
                                          T_BANKS[no % 2][:, 0:m * P].rearrange("p (t c) -> p t c", c=P),
                                          at_hi[:, tiles[0]:tiles[0] + m, q0:q0 + P],
                                          ALU.subtract).then_inc(at_lo_done, 1)

                def square(u, half):
                    dve.wait_ge(o_copied, u * 4 + (2 * half + 3))
                    dve.tensor_tensor(o_sq[:, :], o_raw[:, half * BANK:(half + 1) * BANK],
                                      o_raw[:, half * BANK:(half + 1) * BANK], ALU.mult).then_inc(squared, 1)

                def normalise(u, half):
                    dve.wait_ge(o_chain, (u * 2 + half) * 2 + 2)
                    dve.scalar_tensor_tensor(out=o_norm[:, :], in0=o_raw[:, half * BANK:(half + 1) * BANK],
                                             scalar=g8[:, 0:1], in1=o_rstd[:, :], op0=ALU.mult,
                                             op1=ALU.mult).then_inc(normed, 1)
                    dve.wait_ge(o_hi_done, u * 2 + (half + 1))
                    dve.wait_ge(o_stored[half], u * 32 + 32)
                    dve.tensor_tensor(o_lo[:, half, :], o_norm[:, :], o_hi[:, half, :], ALU.subtract).then_inc(o_lo_done, 1)

                def unit(v, p, u, first):
                    for i in range(QT):
                        copy_scores(u, i)
                        if i >= 1:
                            mix(u, i - 1)
                        elif not first:
                            mix(u - 1, QT - 1)
                        if i >= LAG:
                            low(u, i - LAG)
                        elif not first:
                            low(u - 1, QT - LAG + i)
                        if i == 6:
                            square(u, 0)
                        if i == 7:
                            normalise(u, 0)
                        if i == 2 and not first:
                            square(u - 1, 1)
                        if i == 3 and not first:
                            normalise(u - 1, 1)

                def flush(u):
                    mix(u, QT - 1)
                    for i in range(QT - LAG, QT):
                        low(u, i)
                    square(u, 1)
                    normalise(u, 1)

                ub.zero_meta(dve, prep)
                dve.memset(ones[:, :], 1.0).then_inc(prep, 1)
                dve.memset(eps[:, :], EPS).then_inc(prep, 1)
                dve.wait_ge(small_loaded, 16 * 5)
                dve.tensor_scalar(g8[:, :], g8[:, :], 1.0 - LAM_INIT, None, ALU.mult).then_inc(prep, 1)
                for n in range(2):
                    dve.tensor_tensor(lam_in[:, 2 * n, :], lam_in[:, 2 * n, :], lam_in[:, 2 * n + 1, :],
                                      ALU.mult).then_inc(lam_ready, 1)
                    dve.wait_ge(lam_ready, 2 * n + 1)
                    dve.reduce_sum(lam_s[:, n:n + 1], lam_in[:, 2 * n, :], AXX).then_inc(lam_ready, 1)
                dve.wait_ge(prep_exp, 1)
                dve.tensor_scalar(lam_s[:, 4:5], lam_s[:, 2:3], LAM_INIT, None, ALU.add).then_inc(lam_ready, 1)
                dve.wait_ge(lam_ready, 5)
                dve.tensor_tensor(lam_s[:, 5:6], lam_s[:, 3:4], lam_s[:, 4:5], ALU.subtract).then_inc(lam_ready, 1)
                dve.wait_ge(lam_spread, 1)
                dve.sem_inc(copied, 4)
                dve.sem_inc(at_lo_done, 2)
                dve.sem_inc(o_lo_done, 2)
                run(dve, unit, flush)

            @block.scalar
            def _(act):
                def exp(u, i):
                    r, w = i % RING, META + P * (i + 1)
                    for h in range(2):
                        act.wait_ge(shifted, (u * QT + i) * 2 + (h + 1))
                        act.activation(probs[:, r, h, 0:w], probs[:, r, h, 0:w], ACT.Exp, bias=neg_max[:, r, h:h + 1],
                                       scale=SCALE, accum_out=row_sum[:, r, h:h + 1]).then_inc(exped, 1)

                def high(u, i):
                    for n, tiles in enumerate(turn_groups(i)):
                        no = GROUPS_BEFORE[i] + n
                        m, q0 = len(tiles), (i % 2) * P
                        if n == 0 and i % 2 == 0:
                            act.wait_ge(pv_done, u * 4 + (i // 2 + 1))
                        act.wait_ge(turned, u * GPH + (no + 1))
                        act.activation(at_hi[:, tiles[0]:tiles[0] + m, q0:q0 + P],
                                       T_BANKS[no % 2][:, 0:m * P].rearrange("p (t c) -> p t c", c=P),
                                       ACT.Copy).then_inc(at_hi_done, 1)

                def copy_out(u, q):
                    act.wait_ge(pv_done, u * 4 + (q + 2))
                    act.wait_ge(o_lo_done, u * 2 + (q // 2 + 1))
                    act.activation(o_raw[:, q * 2 * P:(q + 1) * 2 * P], PV_BANK[:, 0:2 * P], ACT.Copy).then_inc(o_copied, 1)

                def out_rstd(u, half):
                    act.wait_ge(summed, u * 2 + (half + 1))
                    act.wait_ge(normed, u * 2 + (half + 1))
                    act.activation(o_rstd[:, :], SUM_BANK[:, :], ACT.Ln, bias=eps[:, 0:1], scale=1.0 / P).then_inc(o_chain, 1)
                    act.wait_ge(o_chain, (u * 2 + half) * 2 + 1)
                    act.activation(o_rstd[:, :], o_rstd[:, :], ACT.Exp, scale=-0.5).then_inc(o_chain, 1)

                def out_high(u, half):
                    act.wait_ge(normed, u * 2 + (half + 2))
                    act.wait_ge(o_stored[half], u * 32 + 32)
                    act.activation(o_hi[:, half, :], o_norm[:, :], ACT.Copy).then_inc(o_hi_done, 1)

                def lagged(u, i):
                    if i % 2 == 0 and i > 0:
                        copy_out(u, i // 2 - 1)
                    high(u, i)

                def unit(v, p, u, first):
                    for i in range(QT):
                        exp(u, i)
                        if i >= LAG:
                            lagged(u, i - LAG)
                        elif not first:
                            lagged(u - 1, QT - LAG + i)
                        if i == LAG - 1 and not first:
                            copy_out(u - 1, 3)
                        if i == 7:
                            out_rstd(u, 0)
                            out_high(u, 0)
                        if i == 3 and not first:
                            out_rstd(u - 1, 1)
                            out_high(u - 1, 1)

                def flush(u):
                    for i in range(QT - LAG, QT):
                        lagged(u, i)
                    copy_out(u, 3)
                    out_rstd(u, 1)
                    out_high(u, 1)

                act.sem_inc(pv_done, 1)
                act.sem_inc(o_copied, 1)
                act.sem_inc(normed, 1)
                act.wait_ge(lam_ready, 4)
                act.wait_ge(prep, 5)
                act.activation(lam_s[:, 2:4], lam_s[:, 0:2], ACT.Exp).then_inc(prep_exp, 1)
                for half in range(2):
                    act.sem_inc(o_stored[half], 32)
                run(act, unit, flush)

            @block.gpsimd
            def _(pool):
                pool.wait_ge(lam_ready, 6)
                pool.partition_broadcast(neg_lam[:, :], lam_s[0:1, 5:6]).then_inc(lam_spread, 1)
                with pool.Fori(0, UNITS) as u:
                    for i in range(QT):
                        r, w = i % RING, META + P * (i + 1)
                        pool.wait_ge(inverted, u * QT + (i + 1))
                        pool.tensor_tensor(probs[:, r, 0, 0:w], probs[:, r, 0, 0:w], weight[:, r, 0:1].broadcast_to([P, w]),
                                           ALU.mult).then_inc(scaled, 1)


def stage_stick(nc, ps, q_dram, k_dram, v_dram, o_dram, ident, ident_r, mask_r):
    ITEMS = 2 * QT
    LAG, RING = 3, 4
    S_BANKS, T_BANKS, PV_BANKS = ps[0:4], ps[4:6], ps[6:8]
    GPU = 2 * GPH
    with Scratch(nc) as s:
        ub = UnitBuffers(s, "s", [(0, 0, 2 * P)])
        take = s.sb("s_take", [P, RING, L])
        leave = s.sb("s_leave", [P, RING, L])
        one = s.sb("s_one", [P, L])
        at_hi = s.sb("s_at_hi", [P, 2, KEY_TILES, 2 * P], F32R)
        at_lo = s.sb("s_at_lo", [P, 2, KEY_TILES, 2 * P], F32R)
        o_low = s.sb("s_o_low", [P, 2 * P])
        o_sum = s.sb("s_o_sum", [P, 2 * P])
        o_hi, o_lo = s.sb("s_o_hi", [P, 4, 2 * P], F32R), s.sb("s_o_lo", [P, 4, 2 * P], F32R)
        prep = s.sem("s_prep")
        scored, split = s.sem("s_scored"), s.sem("s_split")
        scanned, taken = s.sem("s_scanned"), s.sem("s_taken")
        turned, at_hi_done, at_lo_done = s.sem("s_turned"), s.sem("s_at_hi_done"), s.sem("s_at_lo_done")
        pv_done, o_low_done, o_summed = s.sem("s_pv_done"), s.sem("s_o_low_done"), s.sem("s_o_summed")
        o_hi_done, o_lo_done = s.sem("s_o_hi_done"), s.sem("s_o_lo_done")
        o_stored = s.sems("s_o_stored", 4)

        def group_no(n, g):
            i, h = n // 2, n % 2
            return 2 * GROUPS_BEFORE[i] + h * len(turn_groups(i)) + g

        def run(eng, unit, flush):
            unit(0, 0, 0, True)
            unit(0, 1, 1, False)
            with eng.Fori(1, UNITS // 2) as v:
                unit(v, 0, v * 2, False)
                unit(v, 1, v * 2 + 1, False)
            flush(UNITS - 1)

        with nc.Block() as block:
            @block.sync
            def _(sp):
                sp.wait_ge(prep, 2)
                ub.load(sp, 0, 0, q_dram, k_dram, v_dram, UNITS)
                ub.load(sp, 1, 1, q_dram, k_dram, v_dram, UNITS)

                def stores(u):
                    for q in range(4):
                        sp.wait_ge(o_lo_done, u * 4 + (q + 2))
                        for x, src in enumerate((o_hi, o_lo)):
                            sp.dma_start(o_dram[x, bass.ds(u * P, P), q * 2 * P:(q + 1) * 2 * P],
                                         words(src[:, q, :])).then_inc(o_stored[q], 16)

                with sp.Fori(0, UNITS // 2 - 1) as v:
                    for p in range(2):
                        sp.wait_ge(pv_done, (v * 2 + (p + 1)) * 8 + 2)
                        ub.load(sp, v * 2 + (p + 2), p, q_dram, k_dram, v_dram, UNITS)
                        stores(v * 2 + p)
                for p in range(2):
                    stores(UNITS - 2 + p)
                for q in range(4):
                    sp.wait_ge(o_stored[q], 32 * (UNITS + 1))

            @block.tensor
            def _(pe):
                def scores(p, u, n_item):
                    i, h = n_item // 2, n_item % 2
                    for c, (k0, n) in enumerate(score_chunks(i)):
                        no = chunk_no(i, h, c)
                        bank = S_BANKS[no % 4]
                        pe.wait_ge(split, u * CPU + (no + 1))
                        q = ub.q[p][h][:, i * P:(i + 1) * P]
                        last = c == len(score_chunks(i)) - 1
                        pe.matmul(bank[:, 0:n], q, ub.k[p][h][1][:, k0:k0 + n], start=True, stop=False)
                        mm = pe.matmul(bank[:, 0:n], q, ub.k[p][h][0][:, k0:k0 + n], start=False, stop=not last)
                        if last:
                            mm = pe.matmul(bank[:, n - P:n], ident_r[:, :], mask_r[:, :], start=False, stop=True)
                        mm.then_inc(scored, 1)

                def turn(u, n_item):
                    i = n_item // 2
                    pe.wait_ge(taken, u * ITEMS + (n_item + 1))
                    for g, tiles in enumerate(turn_groups(i)):
                        no = group_no(n_item, g)
                        pe.wait_ge(at_lo_done, u * GPU + (no + 1))
                        for x, t in enumerate(tiles):
                            mm = pe.transpose(T_BANKS[no % 2][:, x * P:(x + 1) * P],
                                              take[:, n_item % RING, key_col(t):key_col(t) + P], ident[:, :])
                        mm.then_inc(turned, 1)

                def values(p, u, s_, h):
                    last_item = 4 * s_ + 2 + h
                    pe.wait_ge(at_lo_done, u * GPU + (2 + group_no(last_item, len(turn_groups(2 * s_ + 1)) - 1) + 1))
                    pe.wait_ge(o_summed, u * 4 + (s_ + 1))
                    n_t = 2 * s_ + 3
                    for t in range(n_t):
                        q0 = P if t == n_t - 1 else 0
                        w = ub.v[p][:, t, h * P:(h + 1) * P]
                        o = PV_BANKS[h][:, q0:2 * P]
                        pe.matmul(o, w, at_lo[:, h, t, q0:2 * P], start=(t == 0), stop=False)
                        mm = pe.matmul(o, w, at_hi[:, h, t, q0:2 * P], start=False, stop=(t == n_t - 1))
                    mm.then_inc(pv_done, 1)

                def lagged(p, u, n):
                    turn(u, n)
                    if n % 4 == 3:
                        values(p, u, n // 4, 0)
                    if n % 4 == 0 and n > 0:
                        values(p, u, n // 4 - 1, 1)

                def unit(v, p, u, first):
                    pe.wait_ge(ub.loaded[p], (v + 1) * (16 * ub.LOADS))
                    for n in range(ITEMS):
                        scores(p, u, n)
                        if n >= LAG:
                            lagged(p, u, n - LAG)
                            if n == LAG and not first:
                                values(1 - p, u - 1, 3, 1)
                        elif not first:
                            lagged(1 - p, u - 1, ITEMS - LAG + n)

                def flush(u):
                    for n in range(ITEMS - LAG, ITEMS):
                        lagged(u % 2, u, n)
                    values(u % 2, u, 3, 1)

                run(pe, unit, flush)

            @block.scalar
            def _(act):
                def sigmoids(u, n_item):
                    i, h = n_item // 2, n_item % 2
                    for c, (k0, n) in enumerate(score_chunks(i)):
                        no = chunk_no(i, h, c)
                        act.wait_ge(scored, u * CPU + (no + 1))
                        act.activation(leave[:, n_item % RING, k0:k0 + n], S_BANKS[no % 4][:, 0:n], ACT.Sigmoid,
                                       scale=-SCALE)
                        act.activation(take[:, n_item % RING, k0:k0 + n], S_BANKS[no % 4][:, 0:n], ACT.Sigmoid,
                                       scale=SCALE).then_inc(split, 1)

                def high(u, n_item):
                    i, h = n_item // 2, n_item % 2
                    q0 = (i % 2) * P
                    for g, tiles in enumerate(turn_groups(i)):
                        no, m = group_no(n_item, g), len(tiles)
                        if g == 0 and i % 2 == 0:
                            act.wait_ge(pv_done, (u * 4 + i // 2) * 2 + (h + 1))
                        act.wait_ge(turned, u * GPU + (no + 1))
                        act.activation(at_hi[:, h, tiles[0]:tiles[0] + m, q0:q0 + P],
                                       T_BANKS[no % 2][:, 0:m * P].rearrange("p (t c) -> p t c", c=P),
                                       ACT.Copy).then_inc(at_hi_done, 1)

                def out_low(u, s_):
                    act.wait_ge(pv_done, (u * 4 + s_) * 2 + 4)
                    act.wait_ge(o_summed, u * 4 + (s_ + 1))
                    act.activation(o_low[0:HD, :], PV_BANKS[0][HD:P, 0:2 * P], ACT.Copy)
                    act.activation(o_low[HD:P, :], PV_BANKS[1][0:HD, 0:2 * P], ACT.Copy).then_inc(o_low_done, 1)

                def out_high(u, s_):
                    act.wait_ge(o_summed, u * 4 + (s_ + 2))
                    act.wait_ge(o_stored[s_], u * 32 + 32)
                    act.activation(o_hi[:, s_, :], o_sum[:, :], ACT.Copy).then_inc(o_hi_done, 1)

                def lagged(u, n):
                    high(u, n)
                    if n % 4 == 1 and n > 1:
                        out_low(u, n // 4 - 1)
                    if n % 4 == 3 and n > 3:
                        out_high(u, n // 4 - 1)

                def unit(v, p, u, first):
                    for n in range(ITEMS):
                        sigmoids(u, n)
                        if n >= LAG:
                            lagged(u, n - LAG)
                        elif not first:
                            lagged(u - 1, ITEMS - LAG + n)
                        if n == LAG + 1 and not first:
                            out_low(u - 1, 3)
                        if n == LAG + 3 and not first:
                            out_high(u - 1, 3)

                def flush(u):
                    for n in range(ITEMS - LAG, ITEMS):
                        lagged(u, n)
                    out_low(u, 3)
                    out_high(u, 3)

                for q in range(4):
                    act.sem_inc(o_stored[q], 32)
                act.sem_inc(split, 4)
                act.sem_inc(pv_done, 2)
                run(act, unit, flush)

            @block.vector
            def _(dve):
                def scan(u, n_item):
                    i, h = n_item // 2, n_item % 2
                    w = META + P * (i + 1)
                    no = chunk_no(i, h, len(score_chunks(i)) - 1)
                    dve.wait_ge(split, u * CPU + (no + 5))
                    r = leave[:, n_item % RING, w - 1::-1] if w == L else leave[:, n_item % RING, 0:w][:, ::-1]
                    dve.tensor_tensor_scan(r, r, one[:, 0:w], 1.0, ALU.mult, ALU.mult).then_inc(scanned, 1)

                def low(u, n_item):
                    i, h = n_item // 2, n_item % 2
                    q0 = (i % 2) * P
                    for g, tiles in enumerate(turn_groups(i)):
                        no, m = group_no(n_item, g), len(tiles)
                        dve.wait_ge(at_hi_done, u * GPU + (no + 1))
                        dve.tensor_tensor(at_lo[:, h, tiles[0]:tiles[0] + m, q0:q0 + P],
                                          T_BANKS[no % 2][:, 0:m * P].rearrange("p (t c) -> p t c", c=P),
                                          at_hi[:, h, tiles[0]:tiles[0] + m, q0:q0 + P],
                                          ALU.subtract).then_inc(at_lo_done, 1)

                def out_sum(u, s_):
                    dve.wait_ge(o_low_done, u * 4 + (s_ + 1))
                    dve.wait_ge(o_lo_done, u * 4 + (s_ + 1))
                    for h in range(2):
                        a, b = h * HD, (h + 1) * HD
                        last = dve.tensor_tensor(o_sum[a:b, :], PV_BANKS[h][a:b, 0:2 * P], o_low[a:b, :], ALU.add)
                    last.then_inc(o_summed, 1)

                def out_lo(u, s_):
                    dve.wait_ge(o_hi_done, u * 4 + (s_ + 1))
                    dve.wait_ge(o_stored[s_], u * 32 + 32)
                    dve.tensor_tensor(o_lo[:, s_, :], o_sum[:, :], o_hi[:, s_, :], ALU.subtract).then_inc(o_lo_done, 1)

                def lagged(u, n):
                    low(u, n)
                    if n % 4 == 1 and n > 1:
                        out_sum(u, n // 4 - 1)
                    if n % 4 == 3 and n > 3:
                        out_lo(u, n // 4 - 1)

                def unit(v, p, u, first):
                    for n in range(ITEMS):
                        scan(u, n)
                        if n >= LAG:
                            lagged(u, n - LAG)
                        elif not first:
                            lagged(u - 1, ITEMS - LAG + n)
                        if n == LAG + 1 and not first:
                            out_sum(u - 1, 3)
                        if n == LAG + 3 and not first:
                            out_lo(u - 1, 3)

                def flush(u):
                    for n in range(ITEMS - LAG, ITEMS):
                        lagged(u, n)
                    out_sum(u, 3)
                    out_lo(u, 3)

                ub.zero_meta(dve, prep)
                dve.memset(one[:, :], 1.0).then_inc(prep, 1)
                dve.wait_ge(prep, 3)
                dve.sem_inc(at_lo_done, 2)
                dve.sem_inc(o_summed, 1)
                dve.sem_inc(o_lo_done, 1)
                run(dve, unit, flush)

            @block.gpsimd
            def _(pool):
                with pool.Fori(0, UNITS) as u:
                    for n in range(ITEMS):
                        w, r = META + P * (n // 2 + 1), n % RING
                        pool.wait_ge(scanned, u * ITEMS + (n + 1))
                        pool.tensor_tensor(take[:, r, 0:w - 1], take[:, r, 0:w - 1], leave[:, r, 1:w],
                                           ALU.mult).then_inc(taken, 1)


def stage_constants(nc, ident, ident_r, causal_r, strict_r):
    with Scratch(nc) as s:
        masks = s.sb("c_masks", [P, 2, P])
        zeroed, selected, done = s.sem("c_zeroed"), s.sem("c_selected"), s.sem("c_done")
        with nc.Block() as block:
            @block.gpsimd
            def _(pool):
                pool.memset(ident[:, :], 0.0).then_inc(zeroed, 1)
                pool.memset(masks[:, :, :], 0.0).then_inc(zeroed, 1)
                pool.wait_ge(zeroed, 2)
                pool.affine_select(out=ident[:, :], in_=ident[:, :], pattern=[[-1, P]], compare_op=ALU.not_equal,
                                   fill=1.0, base=0, channel_multiplier=1).then_inc(selected, 1)
                for m in range(2):
                    pool.affine_select(out=masks[:, m, :], in_=masks[:, m, :], pattern=[[-1, P]],
                                       compare_op=ALU.is_ge, fill=NEG, base=-m,
                                       channel_multiplier=1).then_inc(selected, 1)

            @block.vector
            def _(dve):
                dve.wait_ge(selected, 3)
                dve.tensor_copy(ident_r[:, :], ident[:, :]).then_inc(done, 1)
                dve.tensor_copy(causal_r[:, :], masks[:, 0, :]).then_inc(done, 1)
                dve.tensor_copy(strict_r[:, :], masks[:, 1, :]).then_inc(done, 1)
                dve.wait_ge(done, 3)


def stage_merge(nc, ps, w_out_a, w_out_b, oa_dram, ob_dram, gate_dram, m_dram):
    CH = 2
    with Scratch(nc) as s:
        o = [[s.sb(f"m_o{b}{x}", [P, KT, SEQ], F32R) for x in range(2)] for b in range(2)]
        w_raw = [s.sb(f"m_w_raw{b}", [P, KT, P]) for b in range(2)]
        w_hi = [s.sb(f"m_w_hi{b}", [P, KT, P], F32R) for b in range(2)]
        w_lo = [s.sb(f"m_w_lo{b}", [P, KT, P], F32R) for b in range(2)]
        gates = [s.sb(f"m_gate{b}", [P, SEQ]) for b in range(2)]
        part = s.sb("m_part", [P, CH, BANK])
        m_hi, m_lo = s.sb("m_hi", [P, CH, BANK], F32R), s.sb("m_lo", [P, CH, BANK], F32R)
        o_loaded = [[s.sem(f"m_o_loaded{b}{c}") for c in range(CH)] for b in range(2)]
        w_loaded, g_loaded = s.sems("m_w_loaded", 2), s.sems("m_g_loaded", 2)
        w_hi_done, w_lo_done = s.sems("m_w_hi_done", 2), s.sems("m_w_lo_done", 2)
        mm_done, gated, added = s.sem("m_mm_done"), s.sem("m_gated"), s.sem("m_added")
        hi_done, lo_done, stored = s.sem("m_hi_done"), s.sem("m_lo_done"), s.sems("m_stored", CH)
        wv = [w.rearrange("o (k p) n -> p (o k) n", p=P) for w in (w_out_a, w_out_b)]
        ov = [x.rearrange("x (k p) t -> x p k t", p=P) for x in (oa_dram, ob_dram)]
        with nc.Block() as block:
            @block.sync
            def _(sp):
                def load_w(u, b):
                    sp.dma_start(w_raw[b][:, :, :], wv[b][:, :, bass.ds(u * P, P)]).then_inc(w_loaded[b], 16)

                def load_g(u, b):
                    sp.dma_start(gates[b][:, :], gate_dram[b, bass.ds(u * P, P), :]).then_inc(g_loaded[b], 16)

                load_w(0, 0)
                for b in range(2):
                    for c in range(CH):
                        for x in range(2):
                            sp.dma_start(words(o[b][x][:, :, c * BANK:(c + 1) * BANK]),
                                         ov[b][x, :, :, c * BANK:(c + 1) * BANK]).then_inc(o_loaded[b][c], 16)
                    if b == 0:
                        load_w(0, 1)
                        load_g(0, 0)
                        load_g(0, 1)

                def body(u, last):
                    if not last:
                        for b in range(2):
                            sp.wait_ge(w_lo_done[b], u + 1)
                            load_w(u + 1, b)
                    for c in range(CH):
                        sp.wait_ge(lo_done, u * CH + (c + 1))
                        for x, src in enumerate((m_hi, m_lo)):
                            sp.dma_start(m_dram[x, bass.ds(u * P, P), c * BANK:(c + 1) * BANK],
                                         words(src[:, c, :])).then_inc(stored[c], 16)
                    if not last:
                        for b in range(2):
                            sp.wait_ge(gated, (u + 1) * 4)
                            load_g(u + 1, b)

                with sp.Fori(0, KT - 1) as u:
                    body(u, False)
                body(KT - 1, True)
                for c in range(CH):
                    sp.wait_ge(stored[c], 32 * (KT + 1))

            @block.scalar
            def _(act):
                def body(u):
                    for b in range(2):
                        act.wait_ge(w_loaded[b], u * 16 + 16)
                        act.wait_ge(mm_done, u * 4 + (2 * b + 2))
                        act.activation(w_hi[b][:, :, :], w_raw[b][:, :, :], ACT.Copy).then_inc(w_hi_done[b], 1)
                        if b == 0:
                            pass
                    for c in range(CH):
                        act.wait_ge(added, u * CH + (c + 1))
                        act.wait_ge(stored[c], u * 32 + 32)
                        act.activation(m_hi[:, c, :], part[:, c, :], ACT.Copy).then_inc(hi_done, 1)

                act.sem_inc(mm_done, 4)
                for c in range(CH):
                    act.sem_inc(stored[c], 32)
                with act.Fori(0, KT) as u:
                    body(u)

            @block.vector
            def _(dve):
                with dve.Fori(0, KT) as u:
                    for b in range(2):
                        dve.wait_ge(w_hi_done[b], u + 1)
                        dve.tensor_tensor(w_lo[b][:, :, :], w_raw[b][:, :, :], w_hi[b][:, :, :],
                                          ALU.subtract).then_inc(w_lo_done[b], 1)
                        dve.wait_ge(g_loaded[b], u * 16 + 16)
                        if b == 0:
                            for c in range(CH):
                                dve.wait_ge(mm_done, u * 4 + (c + 5))
                                dve.tensor_tensor(part[:, c, :], ps[c][:, :], gates[0][:, c * BANK:(c + 1) * BANK],
                                                  ALU.mult).then_inc(gated, 1)
                    for c in range(CH):
                        dve.wait_ge(mm_done, u * 4 + (c + 7))
                        dve.tensor_tensor(gates[1][:, c * BANK:(c + 1) * BANK], ps[2 + c][:, :],
                                          gates[1][:, c * BANK:(c + 1) * BANK], ALU.mult).then_inc(gated, 1)
                        dve.wait_ge(gated, u * 4 + (c + 3))
                        dve.tensor_tensor(part[:, c, :], part[:, c, :], gates[1][:, c * BANK:(c + 1) * BANK],
                                          ALU.add).then_inc(added, 1)
                    for c in range(CH):
                        dve.wait_ge(hi_done, u * CH + (c + 1))
                        dve.wait_ge(stored[c], u * 32 + 32)
                        dve.tensor_tensor(m_lo[:, c, :], part[:, c, :], m_hi[:, c, :],
                                          ALU.subtract).then_inc(lo_done, 1)

            @block.tensor
            def _(pe):
                def body(u, first):
                    for b in range(2):
                        pe.wait_ge(w_lo_done[b], u + 1)
                        for c in range(CH):
                            if first:
                                pe.wait_ge(o_loaded[b][c], 32)
                            else:
                                pe.wait_ge(gated, u * 4 - 4 + (2 * b + c + 1))
                            product3(pe, ps[2 * b + c][:, :], lambda k: w_hi[b][:, k, :], lambda k: w_lo[b][:, k, :],
                                     lambda k: o[b][0][:, k, c * BANK:(c + 1) * BANK],
                                     lambda k: o[b][1][:, k, c * BANK:(c + 1) * BANK], range(KT)).then_inc(mm_done, 1)

                body(0, True)
                with pe.Fori(1, KT) as u:
                    body(u, False)


def stage_residual(nc, ps, x, w_out, mlp_g, m_dram, ident, h2, hm_hi, hm_lo):
    with Scratch(nc) as s:
        w_raw = s.sb("r_w_raw", [P, KT, BANK])
        w_hi, w_lo = s.sb("r_w_hi", [P, KT, D], F32R), s.sb("r_w_lo", [P, KT, D], F32R)
        m = [[s.sb(f"r_m{p}{q}", [P, KT, P], F32R) for q in range(2)] for p in range(2)]
        sq = s.sb("r_sq", [P, D])
        ssum, rstd = s.sb("r_ssum", [P, 2]), s.sb("r_rstd", [P, 2])
        y = s.sb("r_y", [P, 2, D])
        g = s.sb("r_g", [P, KT])
        w_loaded, x_loaded, m_loaded, g_loaded = (s.sem("r_w_loaded"), s.sem("r_x_loaded"),
                                                  s.sems("r_m_loaded", 2), s.sem("r_g_loaded"))
        w_hi_done, w_lo_done = s.sem("r_w_hi_done"), s.sem("r_w_lo_done")
        mm_done, added, squared, scaled = s.sem("r_mm_done"), s.sem("r_added"), s.sem("r_squared"), s.sem("r_scaled")
        mean_eps, rooted, inverted = s.sem("r_mean_eps"), s.sem("r_rooted"), s.sem("r_inverted")
        turned, hi_done, lo_done = s.sem("r_turned"), s.sem("r_hi_done"), s.sem("r_lo_done")
        wv = w_out.rearrange("o (k p) n -> p (o k) n", p=P)
        mv = m_dram.rearrange("x (k p) t -> x p k t", p=P)
        TP = QT // 2
        with nc.Block() as block:
            @block.sync
            def _(sp):
                def load_m(t, p):
                    for q in range(2):
                        sp.dma_start(words(m[p][q][:, :, :]), mv[q, :, :, bass.ds(t * P, P)]).then_inc(m_loaded[p], 16)

                sp.dma_start(w_raw[:, :, :], wv[:, :, 0:BANK]).then_inc(w_loaded, 16)
                load_m(0, 0)
                sp.wait_ge(w_lo_done, KT)
                sp.dma_start(w_raw[:, :, :], wv[:, :, BANK:D]).then_inc(w_loaded, 16)
                sp.dma_start(h2[:, :, :], x[0].rearrange("(t p) c -> p t c", p=P)).then_inc(x_loaded, 16)
                sp.dma_start(g[:, :], mlp_g.rearrange("o (k p) -> p (o k)", p=P),
                             allow_slow_non_contiguous=True).then_inc(g_loaded, 16)
                load_m(1, 1)
                with sp.Fori(0, TP - 1) as v:
                    for p in range(2):
                        sp.wait_ge(mm_done, (v * 2 + p) * 2 + 2)
                        load_m(v * 2 + (p + 2), p)

            @block.scalar
            def _(act):
                def square(t, p):
                    act.wait_ge(added, t * 2 + 2)
                    act.activation(sq[:, :], h2[:, bass.ds(t, 1), :].rearrange("p o c -> p (o c)"), ACT.Square,
                                   accum_out=ssum[:, p:p + 1]).then_inc(squared, 1)
                    act.wait_ge(mean_eps, t + 1)
                    act.activation(rstd[:, p:p + 1], ssum[:, p:p + 1], ACT.Sqrt).then_inc(rooted, 1)

                def high(t):
                    for k in range(KT):
                        if k % 4 == 0:
                            act.wait_ge(turned, t * 2 + (k // 4 + 1))
                        act.activation(hm_hi[:, k, bass.ds(t * P, P)], ps[4 + k // 4][:, (k % 4) * P:(k % 4 + 1) * P],
                                       ACT.Copy, scale=g[:, k:k + 1]).then_inc(hi_done, 1)

                for half in range(2):
                    act.wait_ge(w_loaded, 16 * (half + 1))
                    for k in range(KT):
                        act.activation(w_hi[:, k, half * BANK:(half + 1) * BANK], w_raw[:, k, :],
                                       ACT.Copy).then_inc(w_hi_done, 1)
                act.wait_ge(g_loaded, 16)
                square(0, 0)
                with act.Fori(0, TP - 1) as v:
                    square(v * 2 + 1, 1)
                    high(v * 2)
                    square(v * 2 + 2, 0)
                    high(v * 2 + 1)
                square(QT - 1, 1)
                high(QT - 2)
                high(QT - 1)

            @block.vector
            def _(dve):
                def add(t):
                    for half in range(2):
                        dve.wait_ge(mm_done, t * 2 + (half + 1))
                        dst = h2[:, bass.ds(t, 1), half * BANK:(half + 1) * BANK].rearrange("p o c -> p (o c)")
                        dve.tensor_tensor(dst, ps[half][:, :], dst, ALU.add).then_inc(added, 1)

                def scale(t, p):
                    dve.wait_ge(squared, t + 1)
                    dve.tensor_scalar(ssum[:, p:p + 1], ssum[:, p:p + 1], 1.0 / D, EPS, ALU.mult, ALU.add).then_inc(mean_eps, 1)
                    dve.wait_ge(rooted, t + 1)
                    dve.reciprocal(rstd[:, p:p + 1], rstd[:, p:p + 1]).then_inc(inverted, 1)
                    dve.wait_ge(inverted, t + 1)
                    dve.tensor_scalar(y[:, p, :], h2[:, bass.ds(t, 1), :].rearrange("p o c -> p (o c)"),
                                      rstd[:, p:p + 1], None, ALU.mult).then_inc(scaled, 1)

                def low(t):
                    for k in range(KT):
                        if k % 4 == 0:
                            dve.wait_ge(hi_done, t * KT + (k + 4))
                        dve.scalar_tensor_tensor(out=hm_lo[:, k, bass.ds(t * P, P)],
                                                 in0=ps[4 + k // 4][:, (k % 4) * P:(k % 4 + 1) * P],
                                                 scalar=g[:, k:k + 1], in1=hm_hi[:, k, bass.ds(t * P, P)],
                                                 op0=ALU.mult, op1=ALU.subtract).then_inc(lo_done, 1)

                for half in range(2):
                    for k in range(KT):
                        dve.wait_ge(w_hi_done, half * KT + k + 1)
                        dve.tensor_tensor(w_lo[:, k, half * BANK:(half + 1) * BANK], w_raw[:, k, :],
                                          w_hi[:, k, half * BANK:(half + 1) * BANK], ALU.subtract).then_inc(w_lo_done, 1)
                dve.wait_ge(x_loaded, 16)
                dve.wait_ge(g_loaded, 16)
                add(0)
                scale(0, 0)
                with dve.Fori(0, TP - 1) as v:
                    add(v * 2 + 1)
                    scale(v * 2 + 1, 1)
                    low(v * 2)
                    add(v * 2 + 2)
                    scale(v * 2 + 2, 0)
                    low(v * 2 + 1)
                add(QT - 1)
                scale(QT - 1, 1)
                low(QT - 2)
                low(QT - 1)

            @block.tensor
            def _(pe):
                def product(v, t, p, first):
                    pe.wait_ge(m_loaded[p], (v + 1) * 32)
                    for half in range(2):
                        if first:
                            pe.wait_ge(w_lo_done, KT * (half + 1))
                        else:
                            pe.wait_ge(added, t * 2 - 2 + (half + 1))
                        product3(pe, ps[half][:, :], lambda k: m[p][0][:, k, :], lambda k: m[p][1][:, k, :],
                                 lambda k: w_hi[:, k, half * BANK:(half + 1) * BANK],
                                 lambda k: w_lo[:, k, half * BANK:(half + 1) * BANK], range(KT)).then_inc(mm_done, 1)

                def turn(t, p, first=False):
                    pe.wait_ge(scaled, t + 1)
                    if not first:
                        pe.wait_ge(lo_done, t * KT)
                    for k in range(KT):
                        mm = pe.transpose(ps[4 + k // 4][:, (k % 4) * P:(k % 4 + 1) * P], y[:, p, k * P:(k + 1) * P],
                                          ident[:, :])
                        if k % 4 == 3:
                            mm.then_inc(turned, 1)

                product(0, 0, 0, True)
                product(0, 1, 1, False)
                turn(0, 0, True)
                with pe.Fori(1, TP) as v:
                    product(v, v * 2, 0, False)
                    turn(v * 2 - 1, 1)
                    product(v, v * 2 + 1, 1, False)
                    turn(v * 2, 0)
                turn(QT - 1, 1)


def stage_mlp(nc, ps, w_up, w_down, h2, hm_hi, hm_lo):
    FT = 4
    GROUPS = D_FF // (FT * P)
    CH = 2
    with Scratch(nc) as s:
        u_raw = [s.sb(f"f_u_raw{i}", [P, KT, P]) for i in range(2)]
        u_hi = [s.sb(f"f_u_hi{i}", [P, KT, P], F32R) for i in range(2)]
        u_lo = [s.sb(f"f_u_lo{i}", [P, KT, P], F32R) for i in range(2)]
        d_raw = s.sb("f_d_raw", [P, FT, BANK])
        d_hi = [s.sb(f"f_d_hi{i}", [P, FT, BANK], F32R) for i in range(2)]
        d_lo = [s.sb(f"f_d_lo{i}", [P, FT, BANK], F32R) for i in range(2)]
        relu = s.sb("f_relu", [P, 2, BANK])
        sq = s.sb("f_sq", [P, 2, BANK])
        r_hi, r_lo = s.sb("f_r_hi", [P, FT, SEQ], F32R), s.sb("f_r_lo", [P, FT, SEQ], F32R)
        u_loaded, d_loaded = s.sems("f_u_loaded", 2), s.sem("f_d_loaded")
        u_hi_done, u_lo_done, d_hi_done, d_lo_done = (s.sem("f_u_hi_done"), s.sem("f_u_lo_done"),
                                                      s.sem("f_d_hi_done"), s.sem("f_d_lo_done"))
        up_done, relued, sqd, r_hi_done, r_lo_done = (s.sem("f_up_done"), s.sem("f_relued"), s.sem("f_sqd"),
                                                      s.sem("f_r_hi_done"), s.sem("f_r_lo_done"))
        down_done, added = s.sem("f_down_done"), s.sem("f_added")
        uv = w_up.rearrange("o (k p) n -> p (o k) n", p=P)
        dv = w_down.rearrange("o (g k p) n -> (o g) p k n", p=P, k=FT)
        UC = FT * CH
        DC = QT * 2
        with nc.Block() as block:
            @block.sync
            def _(sp):
                def load_u(g, f):
                    sp.dma_start(u_raw[f % 2][:, :, :], uv[:, :, bass.ds((g * FT + f) * P, P)]).then_inc(u_loaded[f % 2], 16)

                def body(g, last):
                    for f in range(FT):
                        if f < FT - 2 or not last:
                            sp.wait_ge(u_lo_done, g * FT + (f + 1))
                            load_u(g + 1 if f >= FT - 2 else g, (f + 2) % FT)
                        if f == 0:
                            sp.wait_ge(d_lo_done, g * 2 + 2)
                            sp.dma_start(d_raw[:, :, :], dv[g, :, :, 0:BANK]).then_inc(d_loaded, 16)
                        if f == 2:
                            sp.wait_ge(d_lo_done, g * 2 + 3)
                            sp.dma_start(d_raw[:, :, :], dv[g, :, :, BANK:D]).then_inc(d_loaded, 16)

                load_u(0, 0)
                load_u(0, 1)
                with sp.Fori(0, GROUPS - 1) as g:
                    body(g, False)
                body(GROUPS - 1, True)

            @block.scalar
            def _(act):
                def split_u(g, f):
                    act.wait_ge(u_loaded[f % 2], (g * 2 + (f // 2 + 1)) * 16)
                    act.wait_ge(up_done, (g * FT + f) * CH + 2)
                    act.activation(u_hi[f % 2][:, :, :], u_raw[f % 2][:, :, :], ACT.Copy).then_inc(u_hi_done, 1)

                def split_d(g, half):
                    act.wait_ge(d_loaded, (g * 2 + (half + 1)) * 16)
                    act.wait_ge(down_done, (g + 1) * DC)
                    act.activation(d_hi[half][:, :, :], d_raw[:, :, :], ACT.Copy).then_inc(d_hi_done, 1)

                def rectify(g, n):
                    act.wait_ge(up_done, g * UC + (n + 5))
                    act.wait_ge(sqd, g * UC + (n + 1))
                    act.activation(relu[:, n % 2, :], ps[n % 4][:, :], ACT.Relu).then_inc(relued, 1)

                def high(g, n):
                    f, c = n // CH, n % CH
                    act.wait_ge(sqd, g * UC + (n + 3))
                    act.activation(r_hi[:, f, c * BANK:(c + 1) * BANK], sq[:, n % 2, :], ACT.Copy).then_inc(r_hi_done, 1)

                act.sem_inc(up_done, 4)
                act.sem_inc(down_done, DC)
                act.sem_inc(sqd, 2)

                def body(g):
                    split_u(g, 0)
                    split_u(g, 1)
                    for n in range(UC):
                        rectify(g, n)
                        high(g, n)
                        if n in (1, 3):
                            split_u(g, n // 2 + 2)
                        if n in (2, 5):
                            split_d(g, n // 3)

                with act.Fori(0, GROUPS) as g:
                    body(g)

            @block.vector
            def _(dve):
                def split_u(g, f):
                    dve.wait_ge(u_hi_done, g * FT + (f + 1))
                    dve.tensor_tensor(u_lo[f % 2][:, :, :], u_raw[f % 2][:, :, :], u_hi[f % 2][:, :, :],
                                      ALU.subtract).then_inc(u_lo_done, 1)

                def split_d(g, half):
                    dve.wait_ge(d_hi_done, g * 2 + (half + 1))
                    dve.tensor_tensor(d_lo[half][:, :, :], d_raw[:, :, :], d_hi[half][:, :, :],
                                      ALU.subtract).then_inc(d_lo_done, 1)

                def square(g, n):
                    dve.wait_ge(relued, g * UC + (n + 1))
                    dve.scalar_tensor_tensor(out=sq[:, n % 2, :], in0=ps[n % 4][:, :], scalar=0.0,
                                             in1=relu[:, n % 2, :], op0=ALU.max, op1=ALU.mult).then_inc(sqd, 1)

                def low(g, n):
                    f, c = n // CH, n % CH
                    dve.wait_ge(r_hi_done, g * UC + (n + 1))
                    dve.tensor_tensor(r_lo[:, f, c * BANK:(c + 1) * BANK], sq[:, n % 2, :],
                                      r_hi[:, f, c * BANK:(c + 1) * BANK], ALU.subtract).then_inc(r_lo_done, 1)

                def add(g, n):
                    t, half = n // 2, n % 2
                    dve.wait_ge(down_done, g * DC + (DC + n + 1))
                    dst = h2[:, t, half * BANK:(half + 1) * BANK]
                    dve.tensor_tensor(dst, ps[4 + n % 4][:, :], dst, ALU.add).then_inc(added, 1)

                dve.sem_inc(added, 4)
                dve.sem_inc(d_lo_done, 2)
                with dve.Fori(0, GROUPS) as g:
                    split_u(g, 0)
                    split_u(g, 1)
                    for n in range(UC):
                        square(g, n)
                        low(g, n)
                        if n in (1, 3):
                            split_u(g, n // 2 + 2)
                        if n in (2, 5):
                            split_d(g, n // 3)
                    for n in range(DC):
                        add(g, n)

            @block.tensor
            def _(pe):
                def body(g, first):
                    for n in range(UC):
                        f, c = n // CH, n % CH
                        if c == 0:
                            pe.wait_ge(u_lo_done, g * FT + (f + 1))
                        if not (first and n < 4):
                            pe.wait_ge(sqd, g * UC + (n - 1))
                        product3(pe, ps[n % 4][:, :], lambda k: u_hi[f % 2][:, k, :], lambda k: u_lo[f % 2][:, k, :],
                                 lambda k: hm_hi[:, k, c * BANK:(c + 1) * BANK],
                                 lambda k: hm_lo[:, k, c * BANK:(c + 1) * BANK], range(KT)).then_inc(up_done, 1)
                    for n in range(DC):
                        t, half = n // 2, n % 2
                        if n < 2:
                            pe.wait_ge(d_lo_done, g * 2 + (half + 3))
                        pe.wait_ge(added, g * DC + (n + 1))
                        for k in range(FT):
                            if n == 0:
                                pe.wait_ge(r_lo_done, g * UC + (k + 1) * CH)
                            x = lambda a: a[:, k, t * P:(t + 1) * P]
                            o = ps[4 + n % 4][:, :]
                            pe.matmul(o, x(r_lo), d_hi[half][:, k, :], start=(k == 0), stop=False)
                            pe.matmul(o, x(r_hi), d_lo[half][:, k, :], start=False, stop=False)
                            mm = pe.matmul(o, x(r_hi), d_hi[half][:, k, :], start=False, stop=(k == FT - 1))
                        mm.then_inc(down_done, 1)

                body(0, True)
                with pe.Fori(1, GROUPS) as g:
                    body(g, False)


def stage_final(nc, final_g, h2, out):
    with Scratch(nc) as s:
        g = s.sb("z_g", [P, D])
        sq = s.sb("z_sq", [P, 2, D])
        ssum, rstd = s.sb("z_ssum", [P, QT]), s.sb("z_rstd", [P, QT])
        g_loaded, squared, normed, stored = s.sem("z_g_loaded"), s.sem("z_squared"), s.sem("z_normed"), s.sem("z_stored")
        mean_eps, rooted, inverted = s.sem("z_mean_eps"), s.sem("z_rooted"), s.sem("z_inverted")
        with nc.Block() as block:
            @block.sync
            def _(sp):
                sp.dma_start(g[:, :], final_g.rearrange("(o c) -> o c", o=1).broadcast_to([P, D])).then_inc(g_loaded, 16)
                for t in range(QT):
                    sp.wait_ge(normed, t + 1)
                    sp.dma_start(out[0, t * P:(t + 1) * P, :], h2[:, t, :]).then_inc(stored, 16)
                sp.wait_ge(stored, 16 * QT)

            @block.scalar
            def _(act):
                for t in range(QT):
                    if t >= 2:
                        act.wait_ge(squared, t - 1)
                    act.activation(sq[:, t % 2, :], h2[:, t, :], ACT.Square,
                                   accum_out=ssum[:, t:t + 1]).then_inc(squared, 1)
                    act.wait_ge(mean_eps, t + 1)
                    act.activation(rstd[:, t:t + 1], ssum[:, t:t + 1], ACT.Sqrt).then_inc(rooted, 1)

            @block.vector
            def _(dve):
                dve.wait_ge(g_loaded, 16)
                for t in range(QT):
                    dve.wait_ge(squared, t + 1)
                    dve.tensor_scalar(ssum[:, t:t + 1], ssum[:, t:t + 1], 1.0 / D, EPS, ALU.mult, ALU.add).then_inc(mean_eps, 1)
                    dve.wait_ge(rooted, t + 1)
                    dve.reciprocal(rstd[:, t:t + 1], rstd[:, t:t + 1]).then_inc(inverted, 1)
                    dve.wait_ge(inverted, t + 1)
                    dve.scalar_tensor_tensor(out=h2[:, t, :], in0=h2[:, t, :], scalar=rstd[:, t:t + 1], in1=g[:, :],
                                             op0=ALU.mult, op1=ALU.mult).then_inc(normed, 1)


def layer(nc, a, cos, sin, out):
    with ExitStack() as keep:
        def sb(name, shape, dt=F32):
            return keep.enter_context(nc.sbuf_tensor(name, shape, dt))

        ps = [keep.enter_context(nc.psum_tensor(f"bank{i}", [P, BANK], F32)) for i in range(8)]
        ident, ident_r = sb("ident", [P, P]), sb("ident_r", [P, P], F32R)
        causal_r, strict_r = sb("causal_r", [P, P], F32R), sb("strict_r", [P, P], F32R)
        q_dram = [nc.dram_tensor(f"q_scratch{b}", (UNITS, 2, 2, HD, SEQ), F32).ap() for b in range(2)]
        k_dram = [nc.dram_tensor(f"k_scratch{b}", (UNITS, 2, 2, HD, L), F32).ap() for b in range(2)]
        v_dram = nc.dram_tensor("v_scratch", (2 * UNITS, L, 2 * P), F32).ap()
        o_dram = [nc.dram_tensor(f"o_scratch{b}", (2, D, SEQ), F32).ap() for b in range(2)]
        m_dram = nc.dram_tensor("m_scratch", (2, D, SEQ), F32).ap()
        gate_dram = nc.dram_tensor("gate_scratch", (2, D, SEQ), F32).ap()
        w_in = a["w_in"].rearrange("o k n -> (o k) n")

        stage_constants(nc, ident, ident_r, causal_r, strict_r)
        with Scratch(nc) as s:
            hn_hi, hn_lo = s.sb("hn_hi", [P, KT, L], F32R), s.sb("hn_lo", [P, KT, L], F32R)
            stage_norm(nc, ps, a["x"], a["meta_tokens"], a["norm_mix_g"], ident, hn_hi, hn_lo)

            def place_qk(b):
                def place(u, w, part, t0, n):
                    if w == 0:
                        return [(q_dram[b][u, h, part, :, t0 - META:t0 - META + n], h * HD, HD) for h in range(2)]
                    return [(k_dram[b][u, h, part, :, t0:t0 + n], h * HD, HD) for h in range(2)]
                return place

            def place_gate(u, w, part, t0, n):
                return [(gate_dram[w, bass.ds(u * P, P), t0 - META:t0 - META + n], 0, P)]

            stage_channels(nc, ps, "pa", w_in, (QA_COL, KA_COL), (Q_CHUNKS, K_CHUNKS), hn_hi, hn_lo,
                           (cos, sin), place_qk(0))
            stage_channels(nc, ps, "pb", w_in, (QB_COL, KB_COL), (Q_CHUNKS, K_CHUNKS), hn_hi, hn_lo,
                           None, place_qk(1))
            stage_channels(nc, ps, "pg", w_in, (GA_COL, GB_COL), (Q_CHUNKS, Q_CHUNKS), hn_hi, hn_lo,
                           None, place_gate, gate=True)
            stage_values(nc, ps, w_in, hn_hi, hn_lo, v_dram)
        stage_diff(nc, ps, q_dram[0], k_dram[0], v_dram, o_dram[0],
                   [a["lambda_q1"], a["lambda_k1"], a["lambda_q2"], a["lambda_k2"]], a["subln_g"],
                   ident, ident_r, causal_r)
        stage_stick(nc, ps, q_dram[1], k_dram[1], v_dram, o_dram[1], ident, ident_r, strict_r)
        stage_merge(nc, ps, a["w_out_a"], a["w_out_b"], o_dram[0], o_dram[1], gate_dram, m_dram)
        h2 = sb("h2", [P, QT, D])
        with Scratch(nc) as s:
            hm_hi, hm_lo = s.sb("hm_hi", [P, KT, SEQ], F32R), s.sb("hm_lo", [P, KT, SEQ], F32R)
            stage_residual(nc, ps, a["x"], a["w_out"], a["norm_mlp_g"], m_dram, ident, h2, hm_hi, hm_lo)
            stage_mlp(nc, ps, a["w_up"], a["w_down"], h2, hm_hi, hm_lo)
        stage_final(nc, a["norm_final_g"], h2, out)


INPUTS = ["x", "meta_tokens", "norm_mix_g", "w_in", "lambda_q1", "lambda_k1", "lambda_q2", "lambda_k2", "subln_g",
          "w_out_a", "w_out_b", "w_out", "norm_mlp_g", "w_up", "w_down", "norm_final_g"]


def rope_tables():
    inv = (np.float32(ROPE_THETA) ** (-np.arange(0, HD, 2, dtype=np.float32) / np.float32(HD))).astype(np.float32)
    ang = inv[:, None] * np.arange(L, dtype=np.float32)[None, :]
    cos, sin = np.cos(ang).astype(np.float32), np.sin(ang).astype(np.float32)
    return np.concatenate([cos] * 4, axis=0), np.concatenate([-sin, sin, -sin, sin], axis=0)


def kernel(**inputs):
    import concourse.bacc as _bacc
    from concourse.bass_utils import run_bass_kernel_spmd as _run

    nc = _bacc.Bacc("TRN2", target_bir_lowering=False, num_devices=1)
    arrays, aps = {}, {}
    for name in INPUTS:
        arrays[f"in_{name}"] = np.ascontiguousarray(inputs[name])
        aps[name] = nc.dram_tensor(f"in_{name}", arrays[f"in_{name}"].shape, F32, kind="ExternalInput").ap()
    tables = []
    for name, table in zip(("rope_cos", "rope_sin"), rope_tables()):
        arrays[name] = table
        tables.append(nc.dram_tensor(name, table.shape, F32, kind="ExternalInput").ap())
    out = nc.dram_tensor("out_0", (1, SEQ, D), F32, kind="ExternalOutput").ap()
    layer(nc, aps, tables[0], tables[1], out)
    r = _run(nc, [arrays], core_ids=[0])
    return r.results[0]["out_0"]
```

```python
from contextlib import ExitStack
import math

import numpy as np
import concourse.bass as bass
from concourse import mybir

F32 = mybir.dt.float32
F32R = mybir.dt.float32r
ALU = mybir.AluOpType
ACT = mybir.ActivationFunctionType
AXX = mybir.AxisListType.X

P = 128
BANK = 512
D = 1024
KT = D // P
META = 16
SEQ = 1024
L = META + SEQ
HD = 64
UNITS = 8
D_FF = 4 * D
EPS = 1e-6
LAM_INIT = 0.8 - 0.6 * math.exp(-0.3 * 0)
SCALE = 1.0 / math.sqrt(HD)
NEG = -1.0e30
ROPE_THETA = 10000.0

QA_COL, KA_COL, VA_COL = 0, D, 2 * D
QB_COL, KB_COL, VB_COL = 3 * D, 4 * D, 5 * D
GA_COL, GB_COL = 6 * D, 7 * D

Q_CHUNKS = [(META, 512), (META + 512, 512)]
K_CHUNKS = [(0, 352), (352, 344), (696, 344)]
QT = SEQ // P
KEY_TILES = QT + 1


def words(ap):
    return ap.bitcast(F32)


class Scratch:

    def __init__(self, nc):
        self.nc, self.ctx, self.used = nc, ExitStack(), []

    def __enter__(self):
        return self

    def __exit__(self, *a):
        if self.used and a[0] is None:
            self.nc.clear_and_free_semaphores(self.used)
            self.nc.all_engine_barrier()
        return self.ctx.__exit__(*a)

    def sb(self, name, shape, dt=F32):
        return self.ctx.enter_context(self.nc.sbuf_tensor(name, shape, dt))

    def sem(self, name):
        self.used.append(self.nc.alloc_semaphore(name))
        return self.used[-1]

    def sems(self, name, n):
        return [self.sem(f"{name}{i}") for i in range(n)]


def stage_norm(nc, ps, x, meta, norm_g, ident, hn_hi, hn_lo):
    with Scratch(nc) as s:
        xt = s.sb("n_xt", [P, QT + 1, D])
        sq = s.sb("n_sq", [P, D])
        ssum = s.sb("n_ssum", [P, QT + 1])
        rstd = s.sb("n_rstd", [P, QT + 1])
        g = s.sb("n_g", [P, KT])
        loaded = s.sems("n_loaded", QT + 1)
        g_loaded = s.sem("n_g_loaded")
        zeroed = s.sem("n_zeroed")
        summed, mean_eps, rooted = s.sem("n_summed"), s.sem("n_mean_eps"), s.sem("n_rooted")
        inverted, scaled = s.sem("n_inverted"), s.sem("n_scaled")
        turned, hi_done, lo_done = s.sem("n_turned"), s.sem("n_hi_done"), s.sem("n_lo_done")
        groups = []
        for kt in range(KT):
            groups.append((kt, 0, META, [QT]))
            groups.append((kt, META, 512, [0, 1, 2, 3]))
            groups.append((kt, META + 512, 512, [4, 5, 6, 7]))
        groups.sort(key=lambda q: q[1])
        with nc.Block() as block:
            @block.sync
            def _(sp):
                sp.dma_start(xt[0:META, QT, :], meta).then_inc(loaded[QT], 16)
                for t in range(QT):
                    sp.dma_start(xt[:, t, :], x[0, t * P:(t + 1) * P, :]).then_inc(loaded[t], 16)
                    if t == 0:
                        sp.dma_start(g[:, :], norm_g.rearrange("o (k p) -> p (o k)", p=P),
                                     allow_slow_non_contiguous=True).then_inc(g_loaded, 16)

            order = [QT] + list(range(QT))

            @block.scalar
            def _(act):
                for n, t in enumerate(order):
                    m = META if t == QT else P
                    act.wait_ge(loaded[t], 16)
                    if n:
                        act.wait_ge(summed, n)
                    act.activation(sq[0:m, :], xt[0:m, t, :], ACT.Square,
                                   accum_out=ssum[0:m, t:t + 1]).then_inc(summed, 1)
                    act.wait_ge(mean_eps, n + 1)
                    act.activation(rstd[0:m, t:t + 1], ssum[0:m, t:t + 1], ACT.Sqrt).then_inc(rooted, 1)
                act.wait_ge(g_loaded, 16)
                for n, (kt, c0, w, tiles) in enumerate(groups):
                    act.wait_ge(turned, n + 1)
                    act.activation(hn_hi[:, kt, c0:c0 + w], ps[n % 8][:, 0:w], ACT.Copy,
                                   scale=g[:, kt:kt + 1]).then_inc(hi_done, 1)

            @block.vector
            def _(dve):
                for n, t in enumerate(order):
                    m = META if t == QT else P
                    dve.wait_ge(summed, n + 1)
                    dve.tensor_scalar(ssum[0:m, t:t + 1], ssum[0:m, t:t + 1], 1.0 / D, EPS,
                                      ALU.mult, ALU.add).then_inc(mean_eps, 1)
                    dve.wait_ge(rooted, n + 1)
                    dve.reciprocal(rstd[0:m, t:t + 1], rstd[0:m, t:t + 1]).then_inc(inverted, 1)
                    dve.wait_ge(inverted, n + 1)
                    dve.tensor_scalar(xt[0:m, t, :], xt[0:m, t, :], rstd[0:m, t:t + 1], None,
                                      ALU.mult).then_inc(scaled, 1)
                dve.wait_ge(g_loaded, 16)
                for n, (kt, c0, w, tiles) in enumerate(groups):
                    dve.wait_ge(hi_done, n + 1)
                    dve.scalar_tensor_tensor(out=hn_lo[:, kt, c0:c0 + w], in0=ps[n % 8][:, 0:w],
                                             scalar=g[:, kt:kt + 1], in1=hn_hi[:, kt, c0:c0 + w],
                                             op0=ALU.mult, op1=ALU.subtract).then_inc(lo_done, 1)

            @block.tensor
            def _(pe):
                for n, (kt, c0, w, tiles) in enumerate(groups):
                    if n >= 8:
                        pe.wait_ge(lo_done, n - 7)
                    pe.wait_ge(scaled, order.index(tiles[-1]) + 1)
                    for i, t in enumerate(tiles):
                        m = META if t == QT else P
                        mm = pe.transpose(ps[n % 8][:, i * P:i * P + m], xt[0:m, t, kt * P:(kt + 1) * P],
                                          ident[0:m, 0:m])
                    mm.then_inc(turned, 1)


def product3(pe, bank, w_hi, w_lo, x_hi, x_lo, kts, first=True, last=True):
    for n, kt in enumerate(kts):
        pe.matmul(bank, w_lo(kt), x_hi(kt), start=(first and n == 0), stop=False)
        pe.matmul(bank, w_hi(kt), x_lo(kt), start=False, stop=False)
        mm = pe.matmul(bank, w_hi(kt), x_hi(kt), start=False, stop=(last and n == len(kts) - 1))
    return mm


def stage_channels(nc, ps, tag, w_in, cols, chunk_lists, hn_hi, hn_lo, rope, store, gate=None):
    chunks = [(w, t0, n) for w in range(2) for (t0, n) in chunk_lists[w]]
    C = len(chunks)
    first_of = [0, len(chunk_lists[0])]
    wv = w_in.rearrange("(k p) n -> p k n", p=P)
    with Scratch(nc) as s:
        w_raw = [s.sb(f"{tag}_w_raw{i}", [P, KT, P]) for i in range(2)]
        w_hi = [s.sb(f"{tag}_w_hi{i}", [P, KT, P], F32R) for i in range(2)]
        w_lo = [s.sb(f"{tag}_w_lo{i}", [P, KT, P], F32R) for i in range(2)]
        o_hi = s.sb(f"{tag}_o_hi", [P, C, BANK], F32 if gate else F32R)
        o_lo = None if gate else s.sb(f"{tag}_o_lo", [P, C, BANK], F32R)
        if rope:
            cos, sin = s.sb(f"{tag}_cos", [P, L]), s.sb(f"{tag}_sin", [P, L])
            swp = s.sb(f"{tag}_swp", [P, C, BANK])
            rot = s.sb(f"{tag}_rot", [P, C, BANK])
            rot2 = s.sb(f"{tag}_rot2", [P, C, BANK])
        w_loaded = s.sems(f"{tag}_w_loaded", 2)
        w_hi_done, w_lo_done = s.sems(f"{tag}_w_hi_done", 2), s.sems(f"{tag}_w_lo_done", 2)
        tables = s.sem(f"{tag}_tables")
        mm_done = s.sem(f"{tag}_mm_done")
        swapped, sin_done, cos_done, added = (s.sem(f"{tag}_swapped"), s.sem(f"{tag}_sin_done"),
                                              s.sem(f"{tag}_cos_done"), s.sem(f"{tag}_added"))
        hi_done, lo_done = s.sem(f"{tag}_hi_done"), s.sem(f"{tag}_lo_done")
        hi_stored, lo_stored = s.sems(f"{tag}_hi_stored", C), s.sems(f"{tag}_lo_stored", C)
        n_st = 1 if gate else 2

        with nc.Block() as block:
            @block.sync
            def _(sp):
                def load(u, w):
                    sp.dma_start(w_raw[w][:, :, :], wv[:, :, bass.ds(u * P + cols[w], P)]).then_inc(w_loaded[w], 16)

                if rope:
                    sp.dma_start(cos[:, :], rope[0]).then_inc(tables, 16)
                    sp.dma_start(sin[:, :], rope[1]).then_inc(tables, 16)
                load(0, 0)
                load(0, 1)

                def body(u, last):
                    for w in range(2):
                        if not last:
                            sp.wait_ge(w_lo_done[w], u + 1)
                            load(u + 1, w)
                    for c, (w, t0, n) in enumerate(chunks):
                        if gate:
                            sp.wait_ge(hi_done, u * C + (c + 1))
                            for dst, p0, m in store(u, w, 0, t0, n):
                                sp.dma_start(dst, words(o_hi[p0:p0 + m, c, 0:n])).then_inc(hi_stored[c], 16)
                        else:
                            sp.wait_ge(lo_done, u * C + (c + 1))
                            for dst, p0, m in store(u, w, 0, t0, n):
                                sp.dma_start(dst, words(o_hi[p0:p0 + m, c, 0:n])).then_inc(hi_stored[c], 16)
                            for dst, p0, m in store(u, w, 1, t0, n):
                                sp.dma_start(dst, words(o_lo[p0:p0 + m, c, 0:n])).then_inc(lo_stored[c], 16)

                with sp.Fori(0, UNITS - 1) as u:
                    body(u, False)
                body(UNITS - 1, True)
                for c in range(C):
                    sp.wait_ge(hi_stored[c], 16 * n_st * (UNITS + 1))
                    if not gate:
                        sp.wait_ge(lo_stored[c], 16 * n_st * (UNITS + 1))

            @block.scalar
            def _(act):
                def split(u, w):
                    act.wait_ge(w_loaded[w], u * 16 + 16)
                    act.wait_ge(mm_done, u * C + (first_of[w] + len(chunk_lists[w])))
                    act.activation(w_hi[w][:, :, :], w_raw[w][:, :, :], ACT.Copy).then_inc(w_hi_done[w], 1)

                def swap(u, c):
                    w, t0, n = chunks[c]
                    act.wait_ge(mm_done, (u + 1) * C + (c + 1))
                    act.wait_ge(added, u * C + (c + 1))
                    for q in range(4):
                        o, i = 32 * q, 32 * (q ^ 1)
                        last = act.activation(swp[o:o + 32, c, 0:n], ps[c][i:i + 32, 0:n], ACT.Copy)
                    last.then_inc(swapped, 1)

                def high(u, c):
                    w, t0, n = chunks[c]
                    act.wait_ge(hi_stored[c], (u + 1) * 16 * n_st)
                    if rope:
                        act.wait_ge(added, (u + 1) * C + (c + 1))
                        act.activation(o_hi[:, c, 0:n], rot[:, c, 0:n], ACT.Copy).then_inc(hi_done, 1)
                    else:
                        act.wait_ge(mm_done, (u + 1) * C + (c + 1))
                        act.activation(o_hi[:, c, 0:n], ps[c][:, 0:n],
                                       ACT.Sigmoid if gate else ACT.Copy).then_inc(hi_done, 1)

                def body(u, last):
                    split(u, 1)
                    for c in range(C + 1):
                        if rope and c < C:
                            swap(u, c)
                        if c == first_of[1] and not last:
                            split(u + 1, 0)
                        if rope and c >= 1:
                            high(u, c - 1)
                        if not rope and c < C:
                            high(u, c)

                act.sem_inc(mm_done, C)
                for c in range(C):
                    act.sem_inc(hi_stored[c], 16 * n_st)
                if rope:
                    act.sem_inc(added, C)
                split(0, 0)
                with act.Fori(0, UNITS - 1) as u:
                    body(u, False)
                body(UNITS - 1, True)

            @block.gpsimd
            def _(pool):
                def body(u):
                    for c, (w, t0, n) in enumerate(chunks):
                        pool.wait_ge(swapped, u * C + (c + 1))
                        pool.tensor_tensor(rot2[:, c, 0:n], swp[:, c, 0:n], sin[:, t0:t0 + n],
                                           ALU.mult).then_inc(sin_done, 1)
                if rope:
                    pool.wait_ge(tables, 32)
                    with pool.Fori(0, UNITS) as u:
                        body(u)

            @block.vector
            def _(dve):
                def split(u, w):
                    dve.wait_ge(w_hi_done[w], u + 1)
                    dve.tensor_tensor(w_lo[w][:, :, :], w_raw[w][:, :, :], w_hi[w][:, :, :],
                                      ALU.subtract).then_inc(w_lo_done[w], 1)

                def times_cos(u, c):
                    w, t0, n = chunks[c]
                    dve.wait_ge(swapped, u * C + (c + 1))
                    dve.wait_ge(hi_done, (u + 1) * C - C + c + 1)
                    dve.tensor_tensor(rot[:, c, 0:n], ps[c][:, 0:n], cos[:, t0:t0 + n],
                                      ALU.mult).then_inc(cos_done, 1)

                def add(u, c):
                    w, t0, n = chunks[c]
                    dve.wait_ge(sin_done, u * C + (c + 1))
                    dve.wait_ge(cos_done, u * C + (c + 1))
                    dve.tensor_tensor(rot[:, c, 0:n], rot[:, c, 0:n], rot2[:, c, 0:n], ALU.add).then_inc(added, 1)

                def low(u, c):
                    w, t0, n = chunks[c]
                    dve.wait_ge(lo_stored[c], (u + 1) * 16 * n_st)
                    dve.wait_ge(hi_done, (u + 1) * C + (c + 1) if rope else u * C + (c + 1))
                    src = rot[:, c, 0:n] if rope else ps[c][:, 0:n]
                    dve.tensor_tensor(o_lo[:, c, 0:n], src, o_hi[:, c, 0:n], ALU.subtract).then_inc(lo_done, 1)

                def body(u, last):
                    split(u, 1)
                    for c in range(C + 2):
                        if rope and c < C:
                            times_cos(u, c)
                        if c == first_of[1] and not last:
                            split(u + 1, 0)
                        if rope and 1 <= c <= C:
                            add(u, c - 1)
                        if rope and c >= 2:
                            low(u, c - 2)
                        if not rope and not gate and c < C:
                            low(u, c)

                if not gate:
                    for c in range(C):
                        dve.sem_inc(lo_stored[c], 16 * n_st)
                if rope:
                    dve.wait_ge(tables, 32)
                    dve.sem_inc(hi_done, C)
                split(0, 0)
                with dve.Fori(0, UNITS - 1) as u:
                    body(u, False)
                body(UNITS - 1, True)

            @block.tensor
            def _(pe):
                bank_free = cos_done if rope else (hi_done if gate else lo_done)

                def body(u, first):
                    for c, (w, t0, n) in enumerate(chunks):
                        if c in first_of:
                            pe.wait_ge(w_lo_done[w], u + 1)
                        if not first:
                            pe.wait_ge(bank_free, u * C - C + c + 1)
                        mm = product3(pe, ps[c][:, 0:n],
                                      lambda k: w_hi[w][:, k, :], lambda k: w_lo[w][:, k, :],
                                      lambda k: hn_hi[:, k, t0:t0 + n], lambda k: hn_lo[:, k, t0:t0 + n], range(KT))
                        mm.then_inc(mm_done, 1)

                body(0, True)
                with pe.Fori(1, UNITS) as u:
                    body(u, False)


def stage_values(nc, ps, w_in, hn_hi, hn_lo, v_dram):
    T = QT + 1
    GROUPS = 2
    UPG = BANK // P
    with Scratch(nc) as s:
        w_raw = s.sb("v_w_raw", [P, KT, BANK])
        w_hi, w_lo = s.sb("v_w_hi", [P, KT, BANK], F32R), s.sb("v_w_lo", [P, KT, BANK], F32R)
        out = s.sb("v_out", [P, T, UPG, 2 * P], F32R)
        w_loaded = s.sem("v_w_loaded")
        w_hi_done, w_lo_done = s.sem("v_w_hi_done"), s.sem("v_w_lo_done")
        mm_done, hi_done, lo_done = s.sem("v_mm_done"), s.sem("v_hi_done"), s.sem("v_lo_done")
        stored = s.sems("v_stored", T)
        wv = w_in.rearrange("(k p) n -> p k n", p=P)
        vd = v_dram.rearrange("(g u) t c -> g t u c", u=UPG)

        def rows(t):
            return (0, META) if t == QT else (META + t * P, P)

        with nc.Block() as block:
            @block.sync
            def _(sp):
                cols = [VA_COL, VA_COL + BANK, VB_COL, VB_COL + BANK]

                def load(n):
                    sp.wait_ge(w_lo_done, n * KT + KT)
                    sp.dma_start(w_raw[:, :, :], wv[:, :, cols[n]:cols[n] + BANK]).then_inc(w_loaded, 16)

                load(0)
                for n in range(len(cols)):
                    if n + 1 < len(cols):
                        load(n + 1)
                    for t in range(T):
                        t0, m = rows(t)
                        sp.wait_ge(lo_done, n * T + (t + 1))
                        sp.dma_start(vd[n, t0:t0 + m, :, :], words(out[0:m, t, :, :])).then_inc(stored[t], 16)
                for t in range(T):
                    sp.wait_ge(stored[t], 16 * (2 * GROUPS + 1))

            @block.scalar
            def _(act):
                act.sem_inc(mm_done, T)
                for t in range(T):
                    act.sem_inc(stored[t], 16)
                for b in range(2):
                    with act.Fori(0, GROUPS) as g:
                        n = b * GROUPS + g
                        act.wait_ge(w_loaded, n * 16 + 16)
                        act.wait_ge(mm_done, n * T + T)
                        for k in range(KT):
                            act.activation(w_hi[:, k, :], w_raw[:, k, :], ACT.Copy).then_inc(w_hi_done, 1)
                        for t in range(T):
                            t0, m = rows(t)
                            act.wait_ge(mm_done, n * T + (T + t + 1))
                            act.wait_ge(stored[t], n * 16 + 16)
                            src = ps[t % 8][0:m, :].rearrange("p (u c) -> p u c", c=P)
                            act.activation(out[0:m, t, :, 0:HD], src[:, :, 0:HD], ACT.Copy)
                            act.activation(out[0:m, t, :, 3 * HD:4 * HD], src[:, :, HD:P], ACT.Copy).then_inc(hi_done, 1)

            @block.vector
            def _(dve):
                dve.sem_inc(w_lo_done, KT)
                for b in range(2):
                    with dve.Fori(0, GROUPS) as g:
                        n = b * GROUPS + g
                        for k in range(KT):
                            dve.wait_ge(w_hi_done, n * KT + (k + 1))
                            dve.tensor_tensor(w_lo[:, k, :], w_raw[:, k, :], w_hi[:, k, :],
                                              ALU.subtract).then_inc(w_lo_done, 1)
                        for t in range(T):
                            t0, m = rows(t)
                            dve.wait_ge(hi_done, n * T + (t + 1))
                            src = ps[t % 8][0:m, :].rearrange("p (u c) -> p u c", c=P)
                            dve.tensor_tensor(out[0:m, t, :, HD:2 * HD], src[:, :, 0:HD],
                                              out[0:m, t, :, 0:HD], ALU.subtract)
                            dve.tensor_tensor(out[0:m, t, :, 2 * HD:3 * HD], src[:, :, HD:P],
                                              out[0:m, t, :, 3 * HD:4 * HD], ALU.subtract).then_inc(lo_done, 1)

            @block.tensor
            def _(pe):
                def body(n, first):
                    for t in range(T):
                        t0, m = rows(t)
                        if t == 8:
                            pe.wait_ge(lo_done, n * T + 1)
                        elif t == 0 and not first:
                            pe.wait_ge(lo_done, n * T)
                        elif not first:
                            pe.wait_ge(lo_done, n * T - T + t + 1)
                        for k in range(KT):
                            if t == 0:
                                pe.wait_ge(w_lo_done, n * KT + (KT + k + 1))
                            pe.matmul(ps[t % 8][0:m, :], hn_hi[:, k, t0:t0 + m], w_lo[:, k, :],
                                      start=(k == 0), stop=False)
                            pe.matmul(ps[t % 8][0:m, :], hn_lo[:, k, t0:t0 + m], w_hi[:, k, :],
                                      start=False, stop=False)
                            mm = pe.matmul(ps[t % 8][0:m, :], hn_hi[:, k, t0:t0 + m], w_hi[:, k, :],
                                           start=False, stop=(k == KT - 1))
                        mm.then_inc(mm_done, 1)

                body(0, True)
                with pe.Fori(1, 2 * GROUPS) as n:
                    body(n, False)


def score_chunks(i):
    w = META + P * (i + 1)
    return {1: [(0, w)], 2: [(0, w // 2), (w // 2, w - w // 2)], 3: K_CHUNKS}[-(-w // BANK)]


def turn_groups(i):
    tiles = list(range(i + 2))
    return [tiles[n:n + 4] for n in range(0, len(tiles), 4)]


CHUNKS_BEFORE = [sum(len(score_chunks(j)) for j in range(i)) for i in range(QT + 1)]
GROUPS_BEFORE = [sum(len(turn_groups(j)) for j in range(i)) for i in range(QT + 1)]
CPU = 2 * CHUNKS_BEFORE[QT]
GPH = GROUPS_BEFORE[QT]


def key_col(tile):
    return 0 if tile == 0 else META + P * (tile - 1)


def chunk_no(i, h, c):
    return 2 * CHUNKS_BEFORE[i] + h * len(score_chunks(i)) + c


def interleave(a, b):
    out, used = [], 0
    for n, x in enumerate(a):
        out.append(x)
        upto = (n + 1) * len(b) // len(a)
        out += b[used:upto]
        used = upto
    return out


def slot_order(chunks, groups):
    half = len(chunks) // 2
    g = len(groups) // 2
    return (interleave([("chunk", c) for c in chunks[:half]], [("group", x) for x in groups[:g]]),
            interleave([("chunk", c) for c in chunks[half:]], [("group", x) for x in groups[g:]]))


def groups_later(items):
    out = list(items)
    for n in range(len(out) - 1, 0, -1):
        if out[n][0] == "chunk" and out[n - 1][0] == "group":
            out[n - 1], out[n] = out[n], out[n - 1]
    return out


class UnitBuffers:

    def __init__(self, s, tag, v_parts):
        self.v_parts = v_parts
        self.LOADS = 2 + 8 + 2 * len(v_parts)
        self.q = [[s.sb(f"{tag}_q{p}{h}", [P, SEQ], F32R) for h in range(2)] for p in range(2)]
        self.k = [[[s.sb(f"{tag}_k{p}{h}{x}", [P, L], F32R) for x in range(2)] for h in range(2)] for p in range(2)]
        self.v = [s.sb(f"{tag}_v{p}", [P, KEY_TILES, 2 * P], F32R) for p in range(2)]
        self.loaded = s.sems(f"{tag}_loaded", 2)

    def zero_meta(self, dve, done):
        for p in range(2):
            dve.memset(self.v[p][:, 0, :].bitcast(F32), 0.0).then_inc(done, 1)

    def load(self, sp, u, p, q_dram, k_dram, v_dram, v_unit0):
        for h in range(2):
            sp.dma_start(words(self.q[p][h][:, :]), q_dram[u, h]).then_inc(self.loaded[p], 16)
            for x in range(2):
                for half in range(2):
                    sp.dma_start(words(self.k[p][h][x][half * HD:(half + 1) * HD, :]), k_dram[u, h, x]).then_inc(self.loaded[p], 16)
        for a, b, n in self.v_parts:
            sp.dma_start(words(self.v[p][0:META, 0, b:b + n]),
                         v_dram[u + v_unit0, 0:META, a:a + n]).then_inc(self.loaded[p], 16)
            sp.dma_start(words(self.v[p][:, 1:KEY_TILES, b:b + n]),
                         v_dram[u + v_unit0, META:L, a:a + n].rearrange("(j p) c -> p j c", p=P)).then_inc(self.loaded[p], 16)


def stage_diff(nc, ps, q_dram, k_dram, v_dram, o_dram, lams, subln_g, ident, ident_r, mask_r):
    EXP_LAG, MIX_LAG, LAG = 1, 2, 4
    S_BANKS, T_BANKS, PV_BANK, SUM_BANK = ps[0:4], ps[4:6], ps[6], ps[7]
    with Scratch(nc) as s:
        ub = UnitBuffers(s, "d", [(0, 0, HD), (3 * HD, HD, HD), (HD, P, P)])
        probs = [s.sb(f"d_probs{i}", [P, 2, META + P * (i + 1)]) for i in range(QT)]
        at_hi, at_lo = s.sb("d_at_hi", [P, 2, KEY_TILES, 2 * P], F32R), s.sb("d_at_lo", [P, 2, KEY_TILES, 2 * P], F32R)
        mx = s.sb("d_mx", [P, QT, 2, 4])
        neg_max = s.sb("d_neg_max", [P, QT, 2])
        row_sum = s.sb("d_row_sum", [P, QT, 2])
        weight = s.sb("d_weight", [P, QT, 2])
        coef = s.sb("d_coef", [P, QT])
        o_raw = s.sb("d_o_raw", [P, SEQ])
        o_sq = s.sb("d_o_sq", [P, BANK])
        o_rstd = s.sb("d_o_rstd", [P, BANK])
        o_norm = s.sb("d_o_norm", [P, BANK])
        o_hi, o_lo = s.sb("d_o_hi", [P, 2, BANK], F32R), s.sb("d_o_lo", [P, 2, BANK], F32R)
        ones = s.sb("d_ones", [P, P])
        lam_in = s.sb("d_lam_in", [1, 4, HD])
        lam_t = s.sb("d_lam_t", [1, HD])
        lam_s = s.sb("d_lam_s", [1, 8])
        neg_lam = s.sb("d_neg_lam", [P, 1])
        g8 = s.sb("d_g8", [P, 1])
        eps = s.sb("d_eps", [P, 1])
        small_loaded, prep = s.sem("d_small_loaded"), s.sem("d_prep")
        prep_exp, lam_ready, lam_spread = s.sem("d_prep_exp"), s.sem("d_lam_ready"), s.sem("d_lam_spread")
        scored, copied, shifted, exped = s.sem("d_scored"), s.sem("d_copied"), s.sem("d_shifted"), s.sem("d_exped")
        inverted, coef_done, scaled, mixed = s.sem("d_inverted"), s.sem("d_coef_done"), s.sem("d_scaled"), s.sem("d_mixed")
        turned, at_hi_done, at_lo_done = s.sem("d_turned"), s.sem("d_at_hi_done"), s.sem("d_at_lo_done")
        pv_done, o_copied, squared, summed = s.sem("d_pv_done"), s.sem("d_o_copied"), s.sem("d_squared"), s.sem("d_summed")
        normed = s.sem("d_normed")
        o_chain, o_hi_done, o_lo_done = s.sem("d_o_chain"), s.sem("d_o_hi_done"), s.sem("d_o_lo_done")
        o_stored = s.sems("d_o_stored", 2)

        def slot(i, j):
            chunks = [] if i is None else [(h, c) + kc for h in range(2) for c, kc in enumerate(score_chunks(i))]
            groups = [] if j is None else list(enumerate(turn_groups(j)))
            if not chunks:
                return [], [("group", g) for g in groups]
            return slot_order(chunks, groups)

        def back(u, i, lag, first):
            return (u, i - lag) if i >= lag else (u, None) if first else (u - 1, QT + i - lag)

        def has_before(u):
            return not (isinstance(u, int) and u == 0)

        def late(j, lag):
            return j + LAG - lag if j + LAG - lag < QT else None

        def run(eng, unit, flush):
            unit(0, 0, 0, True)
            unit(0, 1, 1, False)
            with eng.Fori(1, UNITS // 2) as v:
                unit(v, 0, v * 2, False)
                unit(v, 1, v * 2 + 1, False)
            flush(UNITS - 1)

        with nc.Block() as block:
            @block.sync
            def _(sp):
                for n, l in enumerate(lams):
                    sp.dma_start(lam_in[:, n, :], l).then_inc(small_loaded, 16)
                sp.dma_start(g8[:, :], subln_g.rearrange("o p -> p o"), allow_slow_non_contiguous=True).then_inc(small_loaded, 16)
                sp.wait_ge(prep, 2)
                ub.load(sp, 0, 0, q_dram, k_dram, v_dram, 0)
                ub.load(sp, 1, 1, q_dram, k_dram, v_dram, 0)

                def stores(u):
                    for half in range(2):
                        sp.wait_ge(o_lo_done, u * 2 + (half + 3))
                        for x, src in enumerate((o_hi, o_lo)):
                            sp.dma_start(o_dram[x, bass.ds(u * P, P), half * BANK:(half + 1) * BANK],
                                         words(src[:, half, :])).then_inc(o_stored[half], 16)

                with sp.Fori(0, UNITS // 2 - 1) as v:
                    for p in range(2):
                        sp.wait_ge(pv_done, (v * 2 + (p + 1)) * 4 + 2)
                        ub.load(sp, v * 2 + (p + 2), p, q_dram, k_dram, v_dram, 0)
                        stores(v * 2 + p)
                for p in range(2):
                    stores(UNITS - 2 + p)
                for half in range(2):
                    sp.wait_ge(o_stored[half], 32 * (UNITS + 1))

            @block.tensor
            def _(pe):
                def score(p, u, i, h, c, k0, n):
                    no = chunk_no(i, h, c)
                    bank = S_BANKS[no % 4]
                    pe.wait_ge(copied, u * CPU + (no + 1))
                    q = ub.q[p][h][:, i * P:(i + 1) * P]
                    last = c == len(score_chunks(i)) - 1
                    pe.matmul(bank[:, 0:n], q, ub.k[p][h][1][:, k0:k0 + n], start=True, stop=False)
                    mm = pe.matmul(bank[:, 0:n], q, ub.k[p][h][0][:, k0:k0 + n], start=False, stop=not last)
                    if last:
                        mm = pe.matmul(bank[:, n - P:n], ident_r[:, :], mask_r[:, :], start=False, stop=True)
                    mm.then_inc(scored, 1)

                def turn(u, i, n, tiles):
                    no = GROUPS_BEFORE[i] + n
                    if n == 0:
                        pe.wait_ge(mixed, u * QT + (i + 1))
                    pe.wait_ge(at_lo_done, u * GPH + (no + 1))
                    for x, t in enumerate(tiles):
                        mm = pe.transpose(T_BANKS[no % 2][:, x * P:(x + 1) * P],
                                          probs[i][:, 0, key_col(t):key_col(t) + P], ident[:, :])
                    mm.then_inc(turned, 1)

                def value_tile(p, u, pair, t):
                    last = 2 * pair + 2
                    at, q0 = pair % 2, P if t == last else 0
                    if t == 0:
                        pe.wait_ge(at_lo_done, u * GPH + (2 + GROUPS_BEFORE[2 * pair + 2]))
                        pe.wait_ge(o_copied, u * 4 + (pair + 1))
                    v_hi, v_lo = ub.v[p][:, t, 0:P], ub.v[p][:, t, P:2 * P]
                    o = PV_BANK[:, q0:2 * P]
                    pe.matmul(o, v_lo, at_hi[:, at, t, q0:2 * P], start=(t == 0), stop=False)
                    pe.matmul(o, v_hi, at_lo[:, at, t, q0:2 * P], start=False, stop=False)
                    mm = pe.matmul(o, v_hi, at_hi[:, at, t, q0:2 * P], start=False, stop=(t == last))
                    if t == last:
                        mm.then_inc(pv_done, 1)

                def sums(u, half):
                    pe.wait_ge(squared, u * 2 + (half + 1))
                    pe.wait_ge(o_lo_done, u * 2 + (half + 2))
                    pe.matmul(SUM_BANK[:, :], ones[:, :], o_sq[:, :], start=True, stop=True).then_inc(summed, 1)

                def step(p, u, i, lp, lu, j):
                    items = sum(slot(i, j), [])
                    tiles = []
                    if j is not None and (j > 1 or has_before(lu)):
                        vp, vu, pair = (lp, lu, j // 2 - 1) if j > 1 else (1 - lp, lu - 1, 3)
                        n_t = 2 * pair + 3
                        tiles = range(n_t // 2) if j % 2 == 0 else range(n_t // 2, n_t)
                    done = 0
                    for n, (kind, x) in enumerate(items):
                        if kind == "chunk":
                            score(p, u, i, *x)
                        else:
                            turn(lu, j, *x)
                        upto = (n + 1) * len(tiles) // len(items)
                        for t in tiles[done:upto]:
                            value_tile(vp, vu, pair, t)
                        done = upto
                    if j == 7:
                        sums(lu, 0)
                    if j == 4 and has_before(lu):
                        sums(lu - 1, 1)

                def unit(v, p, u, first):
                    pe.wait_ge(ub.loaded[p], (v + 1) * (16 * ub.LOADS))
                    for i in range(QT):
                        lu, j = back(u, i, LAG, first)
                        step(p, u, i, p if i >= LAG else 1 - p, lu, j)

                def flush(u):
                    for j in range(QT - LAG, QT):
                        step(0, 0, None, u % 2, u, j)
                    for t in range(KEY_TILES):
                        value_tile(u % 2, u, 3, t)
                    sums(u, 1)

                pe.wait_ge(prep, 5)
                run(pe, unit, flush)

            @block.vector
            def _(dve):
                def copy_scores(u, i, h, c, k0, n):
                    no = chunk_no(i, h, c)
                    dve.wait_ge(scored, u * CPU + (no + 1))
                    if c:
                        dve.wait_ge(copied, u * CPU + (no + 4))
                    dve.tensor_scalar(probs[i][:, h, k0:k0 + n], S_BANKS[no % 4][:, 0:n], 1.0,
                                      mx[:, i, h, c - 1:c] if c else None, ALU.mult, ALU.max,
                                      accum_out=mx[:, i, h, c:c + 1]).then_inc(copied, 1)

                def shift(u, i, h):
                    c = len(score_chunks(i)) - 1
                    dve.wait_ge(copied, u * CPU + (chunk_no(i, h, c) + 5))
                    dve.tensor_scalar(neg_max[:, i, h:h + 1], mx[:, i, h, c:c + 1], -SCALE, None,
                                      ALU.mult).then_inc(shifted, 1)

                def invert(u, i, h):
                    dve.wait_ge(exped, (u * QT + i) * 2 + (h + 1))
                    dve.reciprocal(weight[:, i, h:h + 1], row_sum[:, i, h:h + 1]).then_inc(inverted, 1)
                    if h:
                        dve.wait_ge(inverted, (u * QT + i) * 2 + 2)
                        dve.tensor_scalar(coef[:, i:i + 1], weight[:, i, 1:2], neg_lam[:, 0:1], None,
                                          ALU.mult).then_inc(coef_done, 1)

                def mix(u, i):
                    w = META + P * (i + 1)
                    dve.wait_ge(coef_done, u * QT + (i + 1))
                    dve.wait_ge(scaled, u * QT + (i + 1))
                    dve.scalar_tensor_tensor(out=probs[i][:, 0, 0:w], in0=probs[i][:, 1, 0:w],
                                             scalar=coef[:, i:i + 1], in1=probs[i][:, 0, 0:w],
                                             op0=ALU.mult, op1=ALU.add).then_inc(mixed, 1)

                def low(u, i, n, tiles):
                    no = GROUPS_BEFORE[i] + n
                    m, q0, at = len(tiles), (i % 2) * P, i // 2 % 2
                    dve.wait_ge(at_hi_done, u * GPH + (no + 1))
                    dve.tensor_tensor(at_lo[:, at, tiles[0]:tiles[0] + m, q0:q0 + P],
                                      T_BANKS[no % 2][:, 0:m * P].rearrange("p (t c) -> p t c", c=P),
                                      at_hi[:, at, tiles[0]:tiles[0] + m, q0:q0 + P],
                                      ALU.subtract).then_inc(at_lo_done, 1)

                def square(u, half):
                    dve.wait_ge(o_copied, u * 4 + (2 * half + 3))
                    dve.tensor_tensor(o_sq[:, :], o_raw[:, half * BANK:(half + 1) * BANK],
                                      o_raw[:, half * BANK:(half + 1) * BANK], ALU.mult).then_inc(squared, 1)

                def normalise(u, half):
                    dve.wait_ge(o_chain, (u * 2 + half) * 2 + 2)
                    dve.scalar_tensor_tensor(out=o_norm[:, :], in0=o_raw[:, half * BANK:(half + 1) * BANK],
                                             scalar=g8[:, 0:1], in1=o_rstd[:, :], op0=ALU.mult,
                                             op1=ALU.mult).then_inc(normed, 1)
                    dve.wait_ge(o_hi_done, u * 2 + (half + 1))
                    dve.wait_ge(o_stored[half], u * 32 + 32)
                    dve.tensor_tensor(o_lo[:, half, :], o_norm[:, :], o_hi[:, half, :], ALU.subtract).then_inc(o_lo_done, 1)

                def step(u, i, mu, m, lu, j):
                    for half, items in enumerate(slot(i, j)):
                        if m is not None:
                            invert(mu, m, half)
                        for kind, x in groups_later(items):
                            if kind == "chunk":
                                copy_scores(u, i, *x)
                            else:
                                low(lu, j, *x)
                        if i is not None:
                            shift(u, i, half)
                    if m is not None:
                        mix(mu, m)
                    if j == 6:
                        square(lu, 0)
                    if j is not None and has_before(lu):
                        if j == 0:
                            normalise(lu - 1, 0)
                        if j == 3:
                            square(lu - 1, 1)
                        if j == 5:
                            normalise(lu - 1, 1)

                def unit(v, p, u, first):
                    for i in range(QT):
                        lu, j = back(u, i, LAG, first)
                        step(u, i, *back(u, i, MIX_LAG, first), lu, j)

                def flush(u):
                    for j in range(QT - LAG, QT):
                        step(u, None, u, late(j, MIX_LAG), u, j)
                    normalise(u, 0)
                    square(u, 1)
                    normalise(u, 1)

                ub.zero_meta(dve, prep)
                dve.memset(ones[:, :], 1.0).then_inc(prep, 1)
                dve.memset(eps[:, :], EPS).then_inc(prep, 1)
                dve.wait_ge(small_loaded, 16 * 5)
                dve.tensor_scalar(g8[:, :], g8[:, :], 1.0 - LAM_INIT, None, ALU.mult).then_inc(prep, 1)
                for n in range(2):
                    dve.tensor_tensor(lam_in[:, 2 * n, :], lam_in[:, 2 * n, :], lam_in[:, 2 * n + 1, :],
                                      ALU.mult).then_inc(lam_ready, 1)
                    dve.wait_ge(lam_ready, 2 * n + 1)
                    dve.reduce_sum(lam_s[:, n:n + 1], lam_in[:, 2 * n, :], AXX).then_inc(lam_ready, 1)
                dve.wait_ge(prep_exp, 1)
                dve.tensor_scalar(lam_s[:, 4:5], lam_s[:, 2:3], LAM_INIT, None, ALU.add).then_inc(lam_ready, 1)
                dve.wait_ge(lam_ready, 5)
                dve.tensor_tensor(lam_s[:, 5:6], lam_s[:, 3:4], lam_s[:, 4:5], ALU.subtract).then_inc(lam_ready, 1)
                dve.wait_ge(lam_spread, 1)
                dve.sem_inc(copied, 4)
                dve.sem_inc(at_lo_done, 2)
                dve.sem_inc(o_lo_done, 2)
                run(dve, unit, flush)

            @block.scalar
            def _(act):
                def exp(u, i, h):
                    w = META + P * (i + 1)
                    act.wait_ge(shifted, (u * QT + i) * 2 + (h + 1))
                    act.activation(probs[i][:, h, 0:w], probs[i][:, h, 0:w], ACT.Exp, bias=neg_max[:, i, h:h + 1],
                                   scale=SCALE, accum_out=row_sum[:, i, h:h + 1]).then_inc(exped, 1)

                def high(u, i, n, tiles):
                    no = GROUPS_BEFORE[i] + n
                    m, q0, at = len(tiles), (i % 2) * P, i // 2 % 2
                    if n == 0 and i % 2 == 0:
                        act.wait_ge(pv_done, u * 4 + (i // 2 + 1))
                    act.wait_ge(turned, u * GPH + (no + 1))
                    act.activation(at_hi[:, at, tiles[0]:tiles[0] + m, q0:q0 + P],
                                   T_BANKS[no % 2][:, 0:m * P].rearrange("p (t c) -> p t c", c=P),
                                   ACT.Copy).then_inc(at_hi_done, 1)

                def copy_out(u, q):
                    act.wait_ge(pv_done, u * 4 + (q + 3))
                    act.wait_ge(o_lo_done, u * 2 + (q // 2 + 1))
                    act.activation(o_raw[:, q * 2 * P:(q + 1) * 2 * P], PV_BANK[:, 0:2 * P], ACT.Copy).then_inc(o_copied, 1)

                def out_rstd(u, half):
                    act.wait_ge(summed, u * 2 + (half + 1))
                    act.wait_ge(normed, u * 2 + (half + 1))
                    act.activation(o_rstd[:, :], SUM_BANK[:, :], ACT.Ln, bias=eps[:, 0:1], scale=1.0 / P).then_inc(o_chain, 1)
                    act.wait_ge(o_chain, (u * 2 + half) * 2 + 1)
                    act.activation(o_rstd[:, :], o_rstd[:, :], ACT.Exp, scale=-0.5).then_inc(o_chain, 1)

                def out_high(u, half):
                    act.wait_ge(normed, u * 2 + (half + 2))
                    act.wait_ge(o_stored[half], u * 32 + 32)
                    act.activation(o_hi[:, half, :], o_norm[:, :], ACT.Copy).then_inc(o_hi_done, 1)

                def step(eu, e, lu, j):
                    if j in (4, 6):
                        copy_out(lu, j // 2 - 2)
                    if j in (0, 2) and has_before(lu):
                        copy_out(lu - 1, j // 2 + 2)
                    for half, items in enumerate(slot(e, j)):
                        if e is not None:
                            exp(eu, e, half)
                        for kind, x in items:
                            if kind == "group":
                                high(lu, j, *x)
                    if j is not None and has_before(lu):
                        if j == 0:
                            out_rstd(lu - 1, 0)
                            out_high(lu - 1, 0)
                        if j == 5:
                            out_rstd(lu - 1, 1)
                            out_high(lu - 1, 1)

                def unit(v, p, u, first):
                    for i in range(QT):
                        lu, j = back(u, i, LAG, first)
                        step(*back(u, i, EXP_LAG, first), lu, j)

                def flush(u):
                    for j in range(QT - LAG, QT):
                        step(u, late(j, EXP_LAG), u, j)
                    copy_out(u, 2)
                    out_rstd(u, 0)
                    out_high(u, 0)
                    copy_out(u, 3)
                    out_rstd(u, 1)
                    out_high(u, 1)

                act.preload_act_table_set("natural_log_exp_and_others")
                act.sem_inc(pv_done, 2)
                act.sem_inc(o_copied, 1)
                act.sem_inc(normed, 1)
                act.wait_ge(lam_ready, 4)
                act.wait_ge(prep, 5)
                act.activation(lam_s[:, 2:4], lam_s[:, 0:2], ACT.Exp).then_inc(prep_exp, 1)
                for half in range(2):
                    act.sem_inc(o_stored[half], 32)
                run(act, unit, flush)

            @block.gpsimd
            def _(pool):
                pool.wait_ge(lam_ready, 6)
                pool.partition_broadcast(neg_lam[:, :], lam_s[0:1, 5:6]).then_inc(lam_spread, 1)
                with pool.Fori(0, UNITS) as u:
                    for i in range(QT):
                        w = META + P * (i + 1)
                        pool.wait_ge(inverted, (u * QT + i) * 2 + 1)
                        pool.tensor_tensor(probs[i][:, 0, 0:w], probs[i][:, 0, 0:w], weight[:, i, 0:1].broadcast_to([P, w]),
                                           ALU.mult).then_inc(scaled, 1)


def stage_stick(nc, ps, q_dram, k_dram, v_dram, o_dram, ident, ident_r, mask_r):
    ITEMS = 2 * QT
    LAG, RING = 3, 4
    S_BANKS, T_BANKS, PV_BANKS = ps[0:4], ps[4:6], ps[6:8]
    GPU = 2 * GPH
    with Scratch(nc) as s:
        ub = UnitBuffers(s, "s", [(0, 0, 2 * P)])
        take = s.sb("s_take", [P, RING, L])
        leave = s.sb("s_leave", [P, RING, L])
        one = s.sb("s_one", [P, L])
        at_hi = s.sb("s_at_hi", [P, 2, KEY_TILES, 2 * P], F32R)
        at_lo = s.sb("s_at_lo", [P, 2, KEY_TILES, 2 * P], F32R)
        o_low = s.sb("s_o_low", [P, 2 * P])
        o_sum = s.sb("s_o_sum", [P, 2 * P])
        o_hi, o_lo = s.sb("s_o_hi", [P, 4, 2 * P], F32R), s.sb("s_o_lo", [P, 4, 2 * P], F32R)
        prep = s.sem("s_prep")
        scored, split = s.sem("s_scored"), s.sem("s_split")
        scanned, taken = s.sem("s_scanned"), s.sem("s_taken")
        turned, at_hi_done, at_lo_done = s.sem("s_turned"), s.sem("s_at_hi_done"), s.sem("s_at_lo_done")
        pv_done, o_low_done, o_summed = s.sem("s_pv_done"), s.sem("s_o_low_done"), s.sem("s_o_summed")
        o_hi_done, o_lo_done = s.sem("s_o_hi_done"), s.sem("s_o_lo_done")
        o_stored = s.sems("s_o_stored", 4)

        def group_no(n, g):
            i, h = n // 2, n % 2
            return 2 * GROUPS_BEFORE[i] + h * len(turn_groups(i)) + g

        def slot(n, j):
            chunks = [] if n is None else [("chunk", (c,) + kc) for c, kc in enumerate(score_chunks(n // 2))]
            groups = [] if j is None else [("group", x) for x in enumerate(turn_groups(j // 2))]
            return interleave(chunks, groups) if chunks else groups

        def run(eng, unit, flush):
            unit(0, 0, 0, True)
            unit(0, 1, 1, False)
            with eng.Fori(1, UNITS // 2) as v:
                unit(v, 0, v * 2, False)
                unit(v, 1, v * 2 + 1, False)
            flush(UNITS - 1)

        with nc.Block() as block:
            @block.sync
            def _(sp):
                sp.wait_ge(prep, 2)
                ub.load(sp, 0, 0, q_dram, k_dram, v_dram, UNITS)
                ub.load(sp, 1, 1, q_dram, k_dram, v_dram, UNITS)

                def stores(u):
                    for q in range(4):
                        sp.wait_ge(o_lo_done, u * 4 + (q + 2))
                        for x, src in enumerate((o_hi, o_lo)):
                            sp.dma_start(o_dram[x, bass.ds(u * P, P), q * 2 * P:(q + 1) * 2 * P],
                                         words(src[:, q, :])).then_inc(o_stored[q], 16)

                with sp.Fori(0, UNITS // 2 - 1) as v:
                    for p in range(2):
                        sp.wait_ge(pv_done, (v * 2 + (p + 1)) * 8 + 2)
                        ub.load(sp, v * 2 + (p + 2), p, q_dram, k_dram, v_dram, UNITS)
                        stores(v * 2 + p)
                for p in range(2):
                    stores(UNITS - 2 + p)
                for q in range(4):
                    sp.wait_ge(o_stored[q], 32 * (UNITS + 1))

            @block.tensor
            def _(pe):
                def score(p, u, n_item, c, k0, n):
                    i, h = n_item // 2, n_item % 2
                    no = chunk_no(i, h, c)
                    bank = S_BANKS[no % 4]
                    pe.wait_ge(split, u * CPU + (no + 1))
                    q = ub.q[p][h][:, i * P:(i + 1) * P]
                    last = c == len(score_chunks(i)) - 1
                    pe.matmul(bank[:, 0:n], q, ub.k[p][h][1][:, k0:k0 + n], start=True, stop=False)
                    mm = pe.matmul(bank[:, 0:n], q, ub.k[p][h][0][:, k0:k0 + n], start=False, stop=not last)
                    if last:
                        mm = pe.matmul(bank[:, n - P:n], ident_r[:, :], mask_r[:, :], start=False, stop=True)
                    mm.then_inc(scored, 1)

                def turn(u, n_item, g, tiles):
                    if g == 0:
                        pe.wait_ge(taken, u * ITEMS + (n_item + 1))
                    no = group_no(n_item, g)
                    pe.wait_ge(at_lo_done, u * GPU + (no + 1))
                    for x, t in enumerate(tiles):
                        mm = pe.transpose(T_BANKS[no % 2][:, x * P:(x + 1) * P],
                                          take[:, n_item % RING, key_col(t):key_col(t) + P], ident[:, :])
                    mm.then_inc(turned, 1)

                def values(p, u, s_, h):
                    last_item = 4 * s_ + 2 + h
                    pe.wait_ge(at_lo_done, u * GPU + (2 + group_no(last_item, len(turn_groups(2 * s_ + 1)) - 1) + 1))
                    pe.wait_ge(o_summed, u * 4 + (s_ + 1))
                    n_t = 2 * s_ + 3
                    for t in range(n_t):
                        q0 = P if t == n_t - 1 else 0
                        w = ub.v[p][:, t, h * P:(h + 1) * P]
                        o = PV_BANKS[h][:, q0:2 * P]
                        pe.matmul(o, w, at_lo[:, h, t, q0:2 * P], start=(t == 0), stop=False)
                        mm = pe.matmul(o, w, at_hi[:, h, t, q0:2 * P], start=False, stop=(t == n_t - 1))
                    mm.then_inc(pv_done, 1)

                def step(p, u, n, lp, lu, j):
                    for kind, x in slot(n, j):
                        if kind == "chunk":
                            score(p, u, n, *x)
                        else:
                            turn(lu, j, *x)
                    if j is not None and j % 4 == 3:
                        values(lp, lu, j // 4, 0)
                    if j is not None and j % 4 == 0 and j > 0:
                        values(lp, lu, j // 4 - 1, 1)

                def unit(v, p, u, first):
                    pe.wait_ge(ub.loaded[p], (v + 1) * (16 * ub.LOADS))
                    for n in range(ITEMS):
                        if n >= LAG:
                            step(p, u, n, p, u, n - LAG)
                            if n == LAG and not first:
                                values(1 - p, u - 1, 3, 1)
                        elif first:
                            step(p, u, n, p, u, None)
                        else:
                            step(p, u, n, 1 - p, u - 1, ITEMS - LAG + n)

                def flush(u):
                    for j in range(ITEMS - LAG, ITEMS):
                        step(0, 0, None, u % 2, u, j)
                    values(u % 2, u, 3, 1)

                run(pe, unit, flush)

            @block.scalar
            def _(act):
                def sigmoids(u, n_item, c, k0, n):
                    i, h = n_item // 2, n_item % 2
                    no = chunk_no(i, h, c)
                    act.wait_ge(scored, u * CPU + (no + 1))
                    act.activation(leave[:, n_item % RING, k0:k0 + n], S_BANKS[no % 4][:, 0:n], ACT.Sigmoid,
                                   scale=-SCALE)
                    act.activation(take[:, n_item % RING, k0:k0 + n], S_BANKS[no % 4][:, 0:n], ACT.Sigmoid,
                                   scale=SCALE).then_inc(split, 1)

                def high(u, n_item, g, tiles):
                    i, h = n_item // 2, n_item % 2
                    q0, no, m = (i % 2) * P, group_no(n_item, g), len(tiles)
                    if g == 0 and i % 2 == 0:
                        act.wait_ge(pv_done, (u * 4 + i // 2) * 2 + (h + 1))
                    act.wait_ge(turned, u * GPU + (no + 1))
                    act.activation(at_hi[:, h, tiles[0]:tiles[0] + m, q0:q0 + P],
                                   T_BANKS[no % 2][:, 0:m * P].rearrange("p (t c) -> p t c", c=P),
                                   ACT.Copy).then_inc(at_hi_done, 1)

                def out_low(u, s_):
                    act.wait_ge(pv_done, (u * 4 + s_) * 2 + 4)
                    act.wait_ge(o_summed, u * 4 + (s_ + 1))
                    act.activation(o_low[0:HD, :], PV_BANKS[0][HD:P, 0:2 * P], ACT.Copy)
                    act.activation(o_low[HD:P, :], PV_BANKS[1][0:HD, 0:2 * P], ACT.Copy).then_inc(o_low_done, 1)

                def out_high(u, s_):
                    act.wait_ge(o_summed, u * 4 + (s_ + 2))
                    act.wait_ge(o_stored[s_], u * 32 + 32)
                    act.activation(o_hi[:, s_, :], o_sum[:, :], ACT.Copy).then_inc(o_hi_done, 1)

                def step(u, n, lu, j):
                    for kind, x in slot(n, j):
                        if kind == "chunk":
                            sigmoids(u, n, *x)
                        else:
                            high(lu, j, *x)
                    if j is not None and j % 4 == 1 and j > 1:
                        out_low(lu, j // 4 - 1)
                    if j is not None and j % 4 == 3 and j > 3:
                        out_high(lu, j // 4 - 1)

                def unit(v, p, u, first):
                    for n in range(ITEMS):
                        step(u, n, *((u, n - LAG) if n >= LAG else (u, None) if first else (u - 1, ITEMS - LAG + n)))
                        if n == LAG + 1 and not first:
                            out_low(u - 1, 3)
                        if n == LAG + 3 and not first:
                            out_high(u - 1, 3)

                def flush(u):
                    for j in range(ITEMS - LAG, ITEMS):
                        step(u, None, u, j)
                    out_low(u, 3)
                    out_high(u, 3)

                for q in range(4):
                    act.sem_inc(o_stored[q], 32)
                act.sem_inc(split, 4)
                act.sem_inc(pv_done, 2)
                run(act, unit, flush)

            @block.vector
            def _(dve):
                def scan(u, n_item):
                    i, h = n_item // 2, n_item % 2
                    w = META + P * (i + 1)
                    no = chunk_no(i, h, len(score_chunks(i)) - 1)
                    dve.wait_ge(split, u * CPU + (no + 5))
                    r = leave[:, n_item % RING, w - 1::-1] if w == L else leave[:, n_item % RING, 0:w][:, ::-1]
                    dve.tensor_tensor_scan(r, r, one[:, 0:w], 1.0, ALU.mult, ALU.mult).then_inc(scanned, 1)

                def low(u, n_item):
                    i, h = n_item // 2, n_item % 2
                    q0 = (i % 2) * P
                    for g, tiles in enumerate(turn_groups(i)):
                        no, m = group_no(n_item, g), len(tiles)
                        dve.wait_ge(at_hi_done, u * GPU + (no + 1))
                        dve.tensor_tensor(at_lo[:, h, tiles[0]:tiles[0] + m, q0:q0 + P],
                                          T_BANKS[no % 2][:, 0:m * P].rearrange("p (t c) -> p t c", c=P),
                                          at_hi[:, h, tiles[0]:tiles[0] + m, q0:q0 + P],
                                          ALU.subtract).then_inc(at_lo_done, 1)

                def out_sum(u, s_):
                    dve.wait_ge(o_low_done, u * 4 + (s_ + 1))
                    dve.wait_ge(o_lo_done, u * 4 + (s_ + 1))
                    for h in range(2):
                        a, b = h * HD, (h + 1) * HD
                        last = dve.tensor_tensor(o_sum[a:b, :], PV_BANKS[h][a:b, 0:2 * P], o_low[a:b, :], ALU.add)
                    last.then_inc(o_summed, 1)

                def out_lo(u, s_):
                    dve.wait_ge(o_hi_done, u * 4 + (s_ + 1))
                    dve.wait_ge(o_stored[s_], u * 32 + 32)
                    dve.tensor_tensor(o_lo[:, s_, :], o_sum[:, :], o_hi[:, s_, :], ALU.subtract).then_inc(o_lo_done, 1)

                def lagged(u, n):
                    low(u, n)
                    if n % 4 == 1 and n > 1:
                        out_sum(u, n // 4 - 1)
                    if n % 4 == 3 and n > 3:
                        out_lo(u, n // 4 - 1)

                def unit(v, p, u, first):
                    for n in range(ITEMS):
                        if n >= LAG:
                            lagged(u, n - LAG)
                        elif not first:
                            lagged(u - 1, ITEMS - LAG + n)
                        scan(u, n)
                        if n == LAG + 1 and not first:
                            out_sum(u - 1, 3)
                        if n == LAG + 3 and not first:
                            out_lo(u - 1, 3)

                def flush(u):
                    for n in range(ITEMS - LAG, ITEMS):
                        lagged(u, n)
                    out_sum(u, 3)
                    out_lo(u, 3)

                ub.zero_meta(dve, prep)
                dve.memset(one[:, :], 1.0).then_inc(prep, 1)
                dve.wait_ge(prep, 3)
                dve.sem_inc(at_lo_done, 2)
                dve.sem_inc(o_summed, 1)
                dve.sem_inc(o_lo_done, 1)
                run(dve, unit, flush)

            @block.gpsimd
            def _(pool):
                with pool.Fori(0, UNITS) as u:
                    for n in range(ITEMS):
                        w, r = META + P * (n // 2 + 1), n % RING
                        pool.wait_ge(scanned, u * ITEMS + (n + 1))
                        pool.tensor_tensor(take[:, r, 0:w - 1], take[:, r, 0:w - 1], leave[:, r, 1:w],
                                           ALU.mult).then_inc(taken, 1)


def stage_constants(nc, ident, ident_r, causal_r, strict_r):
    with Scratch(nc) as s:
        masks = s.sb("c_masks", [P, 2, P])
        zeroed, selected, done = s.sem("c_zeroed"), s.sem("c_selected"), s.sem("c_done")
        with nc.Block() as block:
            @block.gpsimd
            def _(pool):
                pool.memset(ident[:, :], 0.0).then_inc(zeroed, 1)
                pool.memset(masks[:, :, :], 0.0).then_inc(zeroed, 1)
                pool.wait_ge(zeroed, 2)
                pool.affine_select(out=ident[:, :], in_=ident[:, :], pattern=[[-1, P]], compare_op=ALU.not_equal,
                                   fill=1.0, base=0, channel_multiplier=1).then_inc(selected, 1)
                for m in range(2):
                    pool.affine_select(out=masks[:, m, :], in_=masks[:, m, :], pattern=[[-1, P]],
                                       compare_op=ALU.is_ge, fill=NEG, base=-m,
                                       channel_multiplier=1).then_inc(selected, 1)

            @block.vector
            def _(dve):
                dve.wait_ge(selected, 3)
                dve.tensor_copy(ident_r[:, :], ident[:, :]).then_inc(done, 1)
                dve.tensor_copy(causal_r[:, :], masks[:, 0, :]).then_inc(done, 1)
                dve.tensor_copy(strict_r[:, :], masks[:, 1, :]).then_inc(done, 1)
                dve.wait_ge(done, 3)


def stage_merge(nc, ps, w_out_a, w_out_b, oa_dram, ob_dram, gate_dram, m_dram):
    CH = 2
    with Scratch(nc) as s:
        o = [[s.sb(f"m_o{b}{x}", [P, KT, SEQ], F32R) for x in range(2)] for b in range(2)]
        w_raw = [s.sb(f"m_w_raw{b}", [P, KT, P]) for b in range(2)]
        w_hi = [s.sb(f"m_w_hi{b}", [P, KT, P], F32R) for b in range(2)]
        w_lo = [s.sb(f"m_w_lo{b}", [P, KT, P], F32R) for b in range(2)]
        gates = [s.sb(f"m_gate{b}", [P, SEQ]) for b in range(2)]
        part = s.sb("m_part", [P, CH, BANK])
        m_hi, m_lo = s.sb("m_hi", [P, CH, BANK], F32R), s.sb("m_lo", [P, CH, BANK], F32R)
        o_loaded = [[s.sem(f"m_o_loaded{b}{c}") for c in range(CH)] for b in range(2)]
        w_loaded, g_loaded = s.sems("m_w_loaded", 2), s.sems("m_g_loaded", 2)
        w_hi_done, w_lo_done = s.sems("m_w_hi_done", 2), s.sems("m_w_lo_done", 2)
        mm_done, gated, added = s.sem("m_mm_done"), s.sem("m_gated"), s.sem("m_added")
        hi_done, lo_done, stored = s.sem("m_hi_done"), s.sem("m_lo_done"), s.sems("m_stored", CH)
        wv = [w.rearrange("o (k p) n -> p (o k) n", p=P) for w in (w_out_a, w_out_b)]
        ov = [x.rearrange("x (k p) t -> x p k t", p=P) for x in (oa_dram, ob_dram)]
        with nc.Block() as block:
            @block.sync
            def _(sp):
                def load_w(u, b):
                    sp.dma_start(w_raw[b][:, :, :], wv[b][:, :, bass.ds(u * P, P)]).then_inc(w_loaded[b], 16)

                def load_g(u, b):
                    sp.dma_start(gates[b][:, :], gate_dram[b, bass.ds(u * P, P), :]).then_inc(g_loaded[b], 16)

                load_w(0, 0)
                for b in range(2):
                    for c in range(CH):
                        for x in range(2):
                            sp.dma_start(words(o[b][x][:, :, c * BANK:(c + 1) * BANK]),
                                         ov[b][x, :, :, c * BANK:(c + 1) * BANK]).then_inc(o_loaded[b][c], 16)
                    if b == 0:
                        load_w(0, 1)
                        load_g(0, 0)
                        load_g(0, 1)

                def body(u, last):
                    if not last:
                        for b in range(2):
                            sp.wait_ge(w_lo_done[b], u + 1)
                            load_w(u + 1, b)
                    for c in range(CH):
                        sp.wait_ge(lo_done, u * CH + (c + 1))
                        for x, src in enumerate((m_hi, m_lo)):
                            sp.dma_start(m_dram[x, bass.ds(u * P, P), c * BANK:(c + 1) * BANK],
                                         words(src[:, c, :])).then_inc(stored[c], 16)
                    if not last:
                        for b in range(2):
                            sp.wait_ge(gated, (u + 1) * 4)
                            load_g(u + 1, b)

                with sp.Fori(0, KT - 1) as u:
                    body(u, False)
                body(KT - 1, True)
                for c in range(CH):
                    sp.wait_ge(stored[c], 32 * (KT + 1))

            @block.scalar
            def _(act):
                def body(u):
                    for b in range(2):
                        act.wait_ge(w_loaded[b], u * 16 + 16)
                        act.wait_ge(mm_done, u * 4 + (2 * b + 2))
                        act.activation(w_hi[b][:, :, :], w_raw[b][:, :, :], ACT.Copy).then_inc(w_hi_done[b], 1)
                        if b == 0:
                            pass
                    for c in range(CH):
                        act.wait_ge(added, u * CH + (c + 1))
                        act.wait_ge(stored[c], u * 32 + 32)
                        act.activation(m_hi[:, c, :], part[:, c, :], ACT.Copy).then_inc(hi_done, 1)

                act.sem_inc(mm_done, 4)
                for c in range(CH):
                    act.sem_inc(stored[c], 32)
                with act.Fori(0, KT) as u:
                    body(u)

            @block.vector
            def _(dve):
                with dve.Fori(0, KT) as u:
                    for b in range(2):
                        dve.wait_ge(w_hi_done[b], u + 1)
                        dve.tensor_tensor(w_lo[b][:, :, :], w_raw[b][:, :, :], w_hi[b][:, :, :],
                                          ALU.subtract).then_inc(w_lo_done[b], 1)
                        dve.wait_ge(g_loaded[b], u * 16 + 16)
                        if b == 0:
                            for c in range(CH):
                                dve.wait_ge(mm_done, u * 4 + (c + 5))
                                dve.tensor_tensor(part[:, c, :], ps[c][:, :], gates[0][:, c * BANK:(c + 1) * BANK],
                                                  ALU.mult).then_inc(gated, 1)
                    for c in range(CH):
                        dve.wait_ge(mm_done, u * 4 + (c + 7))
                        dve.tensor_tensor(gates[1][:, c * BANK:(c + 1) * BANK], ps[2 + c][:, :],
                                          gates[1][:, c * BANK:(c + 1) * BANK], ALU.mult).then_inc(gated, 1)
                        dve.wait_ge(gated, u * 4 + (c + 3))
                        dve.tensor_tensor(part[:, c, :], part[:, c, :], gates[1][:, c * BANK:(c + 1) * BANK],
                                          ALU.add).then_inc(added, 1)
                    for c in range(CH):
                        dve.wait_ge(hi_done, u * CH + (c + 1))
                        dve.wait_ge(stored[c], u * 32 + 32)
                        dve.tensor_tensor(m_lo[:, c, :], part[:, c, :], m_hi[:, c, :],
                                          ALU.subtract).then_inc(lo_done, 1)

            @block.tensor
            def _(pe):
                def body(u, first):
                    for b in range(2):
                        pe.wait_ge(w_lo_done[b], u + 1)
                        for c in range(CH):
                            if first:
                                pe.wait_ge(o_loaded[b][c], 32)
                            else:
                                pe.wait_ge(gated, u * 4 - 4 + (2 * b + c + 1))
                            product3(pe, ps[2 * b + c][:, :], lambda k: w_hi[b][:, k, :], lambda k: w_lo[b][:, k, :],
                                     lambda k: o[b][0][:, k, c * BANK:(c + 1) * BANK],
                                     lambda k: o[b][1][:, k, c * BANK:(c + 1) * BANK], range(KT)).then_inc(mm_done, 1)

                body(0, True)
                with pe.Fori(1, KT) as u:
                    body(u, False)


def stage_residual(nc, ps, x, w_out, mlp_g, m_dram, ident, h2, hm_hi, hm_lo):
    with Scratch(nc) as s:
        w_raw = s.sb("r_w_raw", [P, KT, BANK])
        w_hi, w_lo = s.sb("r_w_hi", [P, KT, D], F32R), s.sb("r_w_lo", [P, KT, D], F32R)
        m = [[s.sb(f"r_m{p}{q}", [P, KT, P], F32R) for q in range(2)] for p in range(2)]
        sq = s.sb("r_sq", [P, D])
        ssum, rstd = s.sb("r_ssum", [P, 2]), s.sb("r_rstd", [P, 2])
        y = s.sb("r_y", [P, 2, D])
        g = s.sb("r_g", [P, KT])
        w_loaded, x_loaded, m_loaded, g_loaded = (s.sem("r_w_loaded"), s.sem("r_x_loaded"),
                                                  s.sems("r_m_loaded", 2), s.sem("r_g_loaded"))
        w_hi_done, w_lo_done = s.sem("r_w_hi_done"), s.sem("r_w_lo_done")
        mm_done, added, squared, scaled = s.sem("r_mm_done"), s.sem("r_added"), s.sem("r_squared"), s.sem("r_scaled")
        mean_eps, rooted, inverted = s.sem("r_mean_eps"), s.sem("r_rooted"), s.sem("r_inverted")
        turned, hi_done, lo_done = s.sem("r_turned"), s.sem("r_hi_done"), s.sem("r_lo_done")
        wv = w_out.rearrange("o (k p) n -> p (o k) n", p=P)
        mv = m_dram.rearrange("x (k p) t -> x p k t", p=P)
        TP = QT // 2
        with nc.Block() as block:
            @block.sync
            def _(sp):
                def load_m(t, p):
                    for q in range(2):
                        sp.dma_start(words(m[p][q][:, :, :]), mv[q, :, :, bass.ds(t * P, P)]).then_inc(m_loaded[p], 16)

                sp.dma_start(w_raw[:, :, :], wv[:, :, 0:BANK]).then_inc(w_loaded, 16)
                load_m(0, 0)
                sp.wait_ge(w_lo_done, KT)
                sp.dma_start(w_raw[:, :, :], wv[:, :, BANK:D]).then_inc(w_loaded, 16)
                sp.dma_start(h2[:, :, :], x[0].rearrange("(t p) c -> p t c", p=P)).then_inc(x_loaded, 16)
                sp.dma_start(g[:, :], mlp_g.rearrange("o (k p) -> p (o k)", p=P),
                             allow_slow_non_contiguous=True).then_inc(g_loaded, 16)
                load_m(1, 1)
                with sp.Fori(0, TP - 1) as v:
                    for p in range(2):
                        sp.wait_ge(mm_done, (v * 2 + p) * 2 + 2)
                        load_m(v * 2 + (p + 2), p)

            @block.scalar
            def _(act):
                def square(t, p):
                    act.wait_ge(added, t * 2 + 2)
                    act.activation(sq[:, :], h2[:, bass.ds(t, 1), :].rearrange("p o c -> p (o c)"), ACT.Square,
                                   accum_out=ssum[:, p:p + 1]).then_inc(squared, 1)
                    act.wait_ge(mean_eps, t + 1)
                    act.activation(rstd[:, p:p + 1], ssum[:, p:p + 1], ACT.Sqrt).then_inc(rooted, 1)

                def high(t):
                    for k in range(KT):
                        if k % 4 == 0:
                            act.wait_ge(turned, t * 2 + (k // 4 + 1))
                        act.activation(hm_hi[:, k, bass.ds(t * P, P)], ps[4 + k // 4][:, (k % 4) * P:(k % 4 + 1) * P],
                                       ACT.Copy, scale=g[:, k:k + 1]).then_inc(hi_done, 1)

                for half in range(2):
                    act.wait_ge(w_loaded, 16 * (half + 1))
                    for k in range(KT):
                        act.activation(w_hi[:, k, half * BANK:(half + 1) * BANK], w_raw[:, k, :],
                                       ACT.Copy).then_inc(w_hi_done, 1)
                act.wait_ge(g_loaded, 16)
                square(0, 0)
                with act.Fori(0, TP - 1) as v:
                    square(v * 2 + 1, 1)
                    high(v * 2)
                    square(v * 2 + 2, 0)
                    high(v * 2 + 1)
                square(QT - 1, 1)
                high(QT - 2)
                high(QT - 1)

            @block.vector
            def _(dve):
                def add(t):
                    for half in range(2):
                        dve.wait_ge(mm_done, t * 2 + (half + 1))
                        dst = h2[:, bass.ds(t, 1), half * BANK:(half + 1) * BANK].rearrange("p o c -> p (o c)")
                        dve.tensor_tensor(dst, ps[half][:, :], dst, ALU.add).then_inc(added, 1)

                def scale(t, p):
                    dve.wait_ge(squared, t + 1)
                    dve.tensor_scalar(ssum[:, p:p + 1], ssum[:, p:p + 1], 1.0 / D, EPS, ALU.mult, ALU.add).then_inc(mean_eps, 1)
                    dve.wait_ge(rooted, t + 1)
                    dve.reciprocal(rstd[:, p:p + 1], rstd[:, p:p + 1]).then_inc(inverted, 1)
                    dve.wait_ge(inverted, t + 1)
                    dve.tensor_scalar(y[:, p, :], h2[:, bass.ds(t, 1), :].rearrange("p o c -> p (o c)"),
                                      rstd[:, p:p + 1], None, ALU.mult).then_inc(scaled, 1)

                def low(t):
                    for k in range(KT):
                        if k % 4 == 0:
                            dve.wait_ge(hi_done, t * KT + (k + 4))
                        dve.scalar_tensor_tensor(out=hm_lo[:, k, bass.ds(t * P, P)],
                                                 in0=ps[4 + k // 4][:, (k % 4) * P:(k % 4 + 1) * P],
                                                 scalar=g[:, k:k + 1], in1=hm_hi[:, k, bass.ds(t * P, P)],
                                                 op0=ALU.mult, op1=ALU.subtract).then_inc(lo_done, 1)

                for half in range(2):
                    for k in range(KT):
                        dve.wait_ge(w_hi_done, half * KT + k + 1)
                        dve.tensor_tensor(w_lo[:, k, half * BANK:(half + 1) * BANK], w_raw[:, k, :],
                                          w_hi[:, k, half * BANK:(half + 1) * BANK], ALU.subtract).then_inc(w_lo_done, 1)
                dve.wait_ge(x_loaded, 16)
                dve.wait_ge(g_loaded, 16)
                add(0)
                scale(0, 0)
                with dve.Fori(0, TP - 1) as v:
                    add(v * 2 + 1)
                    scale(v * 2 + 1, 1)
                    low(v * 2)
                    add(v * 2 + 2)
                    scale(v * 2 + 2, 0)
                    low(v * 2 + 1)
                add(QT - 1)
                scale(QT - 1, 1)
                low(QT - 2)
                low(QT - 1)

            @block.tensor
            def _(pe):
                def product(v, t, p, first):
                    pe.wait_ge(m_loaded[p], (v + 1) * 32)
                    for half in range(2):
                        if first:
                            pe.wait_ge(w_lo_done, KT * (half + 1))
                        else:
                            pe.wait_ge(added, t * 2 - 2 + (half + 1))
                        product3(pe, ps[half][:, :], lambda k: m[p][0][:, k, :], lambda k: m[p][1][:, k, :],
                                 lambda k: w_hi[:, k, half * BANK:(half + 1) * BANK],
                                 lambda k: w_lo[:, k, half * BANK:(half + 1) * BANK], range(KT)).then_inc(mm_done, 1)

                def turn(t, p, first=False):
                    pe.wait_ge(scaled, t + 1)
                    if not first:
                        pe.wait_ge(lo_done, t * KT)
                    for k in range(KT):
                        mm = pe.transpose(ps[4 + k // 4][:, (k % 4) * P:(k % 4 + 1) * P], y[:, p, k * P:(k + 1) * P],
                                          ident[:, :])
                        if k % 4 == 3:
                            mm.then_inc(turned, 1)

                product(0, 0, 0, True)
                product(0, 1, 1, False)
                turn(0, 0, True)
                with pe.Fori(1, TP) as v:
                    product(v, v * 2, 0, False)
                    turn(v * 2 - 1, 1)
                    product(v, v * 2 + 1, 1, False)
                    turn(v * 2, 0)
                turn(QT - 1, 1)


def stage_mlp(nc, ps, w_up, w_down, h2, hm_hi, hm_lo):
    FT = 4
    GROUPS = D_FF // (FT * P)
    CH = 2
    with Scratch(nc) as s:
        u_raw = [s.sb(f"f_u_raw{i}", [P, KT, P]) for i in range(2)]
        u_hi = [s.sb(f"f_u_hi{i}", [P, KT, P], F32R) for i in range(2)]
        u_lo = [s.sb(f"f_u_lo{i}", [P, KT, P], F32R) for i in range(2)]
        d_raw = s.sb("f_d_raw", [P, FT, BANK])
        d_hi = [s.sb(f"f_d_hi{i}", [P, FT, BANK], F32R) for i in range(2)]
        d_lo = [s.sb(f"f_d_lo{i}", [P, FT, BANK], F32R) for i in range(2)]
        relu = s.sb("f_relu", [P, 2, BANK])
        sq = s.sb("f_sq", [P, 2, BANK])
        r_hi, r_lo = s.sb("f_r_hi", [P, FT, SEQ], F32R), s.sb("f_r_lo", [P, FT, SEQ], F32R)
        u_loaded, d_loaded = s.sems("f_u_loaded", 2), s.sem("f_d_loaded")
        u_hi_done, u_lo_done, d_hi_done, d_lo_done = (s.sem("f_u_hi_done"), s.sem("f_u_lo_done"),
                                                      s.sem("f_d_hi_done"), s.sem("f_d_lo_done"))
        up_done, relued, sqd, r_hi_done, r_lo_done = (s.sem("f_up_done"), s.sem("f_relued"), s.sem("f_sqd"),
                                                      s.sem("f_r_hi_done"), s.sem("f_r_lo_done"))
        down_done, added = s.sem("f_down_done"), s.sem("f_added")
        uv = w_up.rearrange("o (k p) n -> p (o k) n", p=P)
        dv = w_down.rearrange("o (g k p) n -> (o g) p k n", p=P, k=FT)
        UC = FT * CH
        DC = QT * 2
        with nc.Block() as block:
            @block.sync
            def _(sp):
                def load_u(g, f):
                    sp.dma_start(u_raw[f % 2][:, :, :], uv[:, :, bass.ds((g * FT + f) * P, P)]).then_inc(u_loaded[f % 2], 16)

                def body(g, last):
                    for f in range(FT):
                        if f < FT - 2 or not last:
                            sp.wait_ge(u_lo_done, g * FT + (f + 1))
                            load_u(g + 1 if f >= FT - 2 else g, (f + 2) % FT)
                        if f == 0:
                            sp.wait_ge(d_lo_done, g * 2 + 2)
                            sp.dma_start(d_raw[:, :, :], dv[g, :, :, 0:BANK]).then_inc(d_loaded, 16)
                        if f == 2:
                            sp.wait_ge(d_lo_done, g * 2 + 3)
                            sp.dma_start(d_raw[:, :, :], dv[g, :, :, BANK:D]).then_inc(d_loaded, 16)

                load_u(0, 0)
                load_u(0, 1)
                with sp.Fori(0, GROUPS - 1) as g:
                    body(g, False)
                body(GROUPS - 1, True)

            @block.scalar
            def _(act):
                def split_u(g, f):
                    act.wait_ge(u_loaded[f % 2], (g * 2 + (f // 2 + 1)) * 16)
                    act.wait_ge(up_done, (g * FT + f) * CH + 2)
                    act.activation(u_hi[f % 2][:, :, :], u_raw[f % 2][:, :, :], ACT.Copy).then_inc(u_hi_done, 1)

                def split_d(g, half):
                    act.wait_ge(d_loaded, (g * 2 + (half + 1)) * 16)
                    act.wait_ge(down_done, (g + 1) * DC)
                    act.activation(d_hi[half][:, :, :], d_raw[:, :, :], ACT.Copy).then_inc(d_hi_done, 1)

                def rectify(g, n):
                    act.wait_ge(up_done, g * UC + (n + 5))
                    act.wait_ge(sqd, g * UC + (n + 1))
                    act.activation(relu[:, n % 2, :], ps[n % 4][:, :], ACT.Relu).then_inc(relued, 1)

                def high(g, n):
                    f, c = n // CH, n % CH
                    act.wait_ge(sqd, g * UC + (n + 3))
                    act.activation(r_hi[:, f, c * BANK:(c + 1) * BANK], sq[:, n % 2, :], ACT.Copy).then_inc(r_hi_done, 1)

                act.sem_inc(up_done, 4)
                act.sem_inc(down_done, DC)
                act.sem_inc(sqd, 2)

                def body(g):
                    split_u(g, 0)
                    split_u(g, 1)
                    for n in range(UC):
                        rectify(g, n)
                        high(g, n)
                        if n in (1, 3):
                            split_u(g, n // 2 + 2)
                        if n in (2, 5):
                            split_d(g, n // 3)

                with act.Fori(0, GROUPS) as g:
                    body(g)

            @block.vector
            def _(dve):
                def split_u(g, f):
                    dve.wait_ge(u_hi_done, g * FT + (f + 1))
                    dve.tensor_tensor(u_lo[f % 2][:, :, :], u_raw[f % 2][:, :, :], u_hi[f % 2][:, :, :],
                                      ALU.subtract).then_inc(u_lo_done, 1)

                def split_d(g, half):
                    dve.wait_ge(d_hi_done, g * 2 + (half + 1))
                    dve.tensor_tensor(d_lo[half][:, :, :], d_raw[:, :, :], d_hi[half][:, :, :],
                                      ALU.subtract).then_inc(d_lo_done, 1)

                def square(g, n):
                    dve.wait_ge(relued, g * UC + (n + 1))
                    dve.scalar_tensor_tensor(out=sq[:, n % 2, :], in0=ps[n % 4][:, :], scalar=0.0,
                                             in1=relu[:, n % 2, :], op0=ALU.max, op1=ALU.mult).then_inc(sqd, 1)

                def low(g, n):
                    f, c = n // CH, n % CH
                    dve.wait_ge(r_hi_done, g * UC + (n + 1))
                    dve.tensor_tensor(r_lo[:, f, c * BANK:(c + 1) * BANK], sq[:, n % 2, :],
                                      r_hi[:, f, c * BANK:(c + 1) * BANK], ALU.subtract).then_inc(r_lo_done, 1)

                def add(g, n):
                    t, half = n // 2, n % 2
                    dve.wait_ge(down_done, g * DC + (DC + n + 1))
                    dst = h2[:, t, half * BANK:(half + 1) * BANK]
                    dve.tensor_tensor(dst, ps[4 + n % 4][:, :], dst, ALU.add).then_inc(added, 1)

                dve.sem_inc(added, 4)
                dve.sem_inc(d_lo_done, 2)
                with dve.Fori(0, GROUPS) as g:
                    split_u(g, 0)
                    split_u(g, 1)
                    for n in range(UC):
                        square(g, n)
                        low(g, n)
                        if n in (1, 3):
                            split_u(g, n // 2 + 2)
                        if n in (2, 5):
                            split_d(g, n // 3)
                    for n in range(DC):
                        add(g, n)

            @block.tensor
            def _(pe):
                def body(g, first):
                    for n in range(UC):
                        f, c = n // CH, n % CH
                        if c == 0:
                            pe.wait_ge(u_lo_done, g * FT + (f + 1))
                        if not (first and n < 4):
                            pe.wait_ge(sqd, g * UC + (n - 1))
                        product3(pe, ps[n % 4][:, :], lambda k: u_hi[f % 2][:, k, :], lambda k: u_lo[f % 2][:, k, :],
                                 lambda k: hm_hi[:, k, c * BANK:(c + 1) * BANK],
                                 lambda k: hm_lo[:, k, c * BANK:(c + 1) * BANK], range(KT)).then_inc(up_done, 1)
                    for n in range(DC):
                        t, half = n // 2, n % 2
                        if n < 2:
                            pe.wait_ge(d_lo_done, g * 2 + (half + 3))
                        pe.wait_ge(added, g * DC + (n + 1))
                        for k in range(FT):
                            if n == 0:
                                pe.wait_ge(r_lo_done, g * UC + (k + 1) * CH)
                            x = lambda a: a[:, k, t * P:(t + 1) * P]
                            o = ps[4 + n % 4][:, :]
                            pe.matmul(o, x(r_lo), d_hi[half][:, k, :], start=(k == 0), stop=False)
                            pe.matmul(o, x(r_hi), d_lo[half][:, k, :], start=False, stop=False)
                            mm = pe.matmul(o, x(r_hi), d_hi[half][:, k, :], start=False, stop=(k == FT - 1))
                        mm.then_inc(down_done, 1)

                body(0, True)
                with pe.Fori(1, GROUPS) as g:
                    body(g, False)


def stage_final(nc, final_g, h2, out):
    with Scratch(nc) as s:
        g = s.sb("z_g", [P, D])
        sq = s.sb("z_sq", [P, 2, D])
        ssum, rstd = s.sb("z_ssum", [P, QT]), s.sb("z_rstd", [P, QT])
        g_loaded, squared, normed, stored = s.sem("z_g_loaded"), s.sem("z_squared"), s.sem("z_normed"), s.sem("z_stored")
        mean_eps, rooted, inverted = s.sem("z_mean_eps"), s.sem("z_rooted"), s.sem("z_inverted")
        with nc.Block() as block:
            @block.sync
            def _(sp):
                sp.dma_start(g[:, :], final_g.rearrange("(o c) -> o c", o=1).broadcast_to([P, D])).then_inc(g_loaded, 16)
                for t in range(QT):
                    sp.wait_ge(normed, t + 1)
                    sp.dma_start(out[0, t * P:(t + 1) * P, :], h2[:, t, :]).then_inc(stored, 16)
                sp.wait_ge(stored, 16 * QT)

            @block.scalar
            def _(act):
                for t in range(QT):
                    if t >= 2:
                        act.wait_ge(squared, t - 1)
                    act.activation(sq[:, t % 2, :], h2[:, t, :], ACT.Square,
                                   accum_out=ssum[:, t:t + 1]).then_inc(squared, 1)
                    act.wait_ge(mean_eps, t + 1)
                    act.activation(rstd[:, t:t + 1], ssum[:, t:t + 1], ACT.Sqrt).then_inc(rooted, 1)

            @block.vector
            def _(dve):
                dve.wait_ge(g_loaded, 16)
                for t in range(QT):
                    dve.wait_ge(squared, t + 1)
                    dve.tensor_scalar(ssum[:, t:t + 1], ssum[:, t:t + 1], 1.0 / D, EPS, ALU.mult, ALU.add).then_inc(mean_eps, 1)
                    dve.wait_ge(rooted, t + 1)
                    dve.reciprocal(rstd[:, t:t + 1], rstd[:, t:t + 1]).then_inc(inverted, 1)
                    dve.wait_ge(inverted, t + 1)
                    dve.scalar_tensor_tensor(out=h2[:, t, :], in0=h2[:, t, :], scalar=rstd[:, t:t + 1], in1=g[:, :],
                                             op0=ALU.mult, op1=ALU.mult).then_inc(normed, 1)


def layer(nc, a, cos, sin, out):
    with ExitStack() as keep:
        def sb(name, shape, dt=F32):
            return keep.enter_context(nc.sbuf_tensor(name, shape, dt))

        ps = [keep.enter_context(nc.psum_tensor(f"bank{i}", [P, BANK], F32)) for i in range(8)]
        ident, ident_r = sb("ident", [P, P]), sb("ident_r", [P, P], F32R)
        causal_r, strict_r = sb("causal_r", [P, P], F32R), sb("strict_r", [P, P], F32R)
        q_dram = [nc.dram_tensor(f"q_scratch{b}", (UNITS, 2, 2, HD, SEQ), F32).ap() for b in range(2)]
        k_dram = [nc.dram_tensor(f"k_scratch{b}", (UNITS, 2, 2, HD, L), F32).ap() for b in range(2)]
        v_dram = nc.dram_tensor("v_scratch", (2 * UNITS, L, 2 * P), F32).ap()
        o_dram = [nc.dram_tensor(f"o_scratch{b}", (2, D, SEQ), F32).ap() for b in range(2)]
        m_dram = nc.dram_tensor("m_scratch", (2, D, SEQ), F32).ap()
        gate_dram = nc.dram_tensor("gate_scratch", (2, D, SEQ), F32).ap()
        w_in = a["w_in"].rearrange("o k n -> (o k) n")

        stage_constants(nc, ident, ident_r, causal_r, strict_r)
        with Scratch(nc) as s:
            hn_hi, hn_lo = s.sb("hn_hi", [P, KT, L], F32R), s.sb("hn_lo", [P, KT, L], F32R)
            stage_norm(nc, ps, a["x"], a["meta_tokens"], a["norm_mix_g"], ident, hn_hi, hn_lo)

            def place_qk(b):
                def place(u, w, part, t0, n):
                    if w == 0:
                        return [(q_dram[b][u, h, part, :, t0 - META:t0 - META + n], h * HD, HD) for h in range(2)]
                    return [(k_dram[b][u, h, part, :, t0:t0 + n], h * HD, HD) for h in range(2)]
                return place

            def place_gate(u, w, part, t0, n):
                return [(gate_dram[w, bass.ds(u * P, P), t0 - META:t0 - META + n], 0, P)]

            stage_channels(nc, ps, "pa", w_in, (QA_COL, KA_COL), (Q_CHUNKS, K_CHUNKS), hn_hi, hn_lo,
                           (cos, sin), place_qk(0))
            stage_channels(nc, ps, "pb", w_in, (QB_COL, KB_COL), (Q_CHUNKS, K_CHUNKS), hn_hi, hn_lo,
                           None, place_qk(1))
            stage_channels(nc, ps, "pg", w_in, (GA_COL, GB_COL), (Q_CHUNKS, Q_CHUNKS), hn_hi, hn_lo,
                           None, place_gate, gate=True)
            stage_values(nc, ps, w_in, hn_hi, hn_lo, v_dram)
        stage_diff(nc, ps, q_dram[0], k_dram[0], v_dram, o_dram[0],
                   [a["lambda_q1"], a["lambda_k1"], a["lambda_q2"], a["lambda_k2"]], a["subln_g"],
                   ident, ident_r, causal_r)
        stage_stick(nc, ps, q_dram[1], k_dram[1], v_dram, o_dram[1], ident, ident_r, strict_r)
        stage_merge(nc, ps, a["w_out_a"], a["w_out_b"], o_dram[0], o_dram[1], gate_dram, m_dram)
        h2 = sb("h2", [P, QT, D])
        with Scratch(nc) as s:
            hm_hi, hm_lo = s.sb("hm_hi", [P, KT, SEQ], F32R), s.sb("hm_lo", [P, KT, SEQ], F32R)
            stage_residual(nc, ps, a["x"], a["w_out"], a["norm_mlp_g"], m_dram, ident, h2, hm_hi, hm_lo)
            stage_mlp(nc, ps, a["w_up"], a["w_down"], h2, hm_hi, hm_lo)
        stage_final(nc, a["norm_final_g"], h2, out)


INPUTS = ["x", "meta_tokens", "norm_mix_g", "w_in", "lambda_q1", "lambda_k1", "lambda_q2", "lambda_k2", "subln_g",
          "w_out_a", "w_out_b", "w_out", "norm_mlp_g", "w_up", "w_down", "norm_final_g"]


def rope_tables():
    inv = (np.float32(ROPE_THETA) ** (-np.arange(0, HD, 2, dtype=np.float32) / np.float32(HD))).astype(np.float32)
    ang = inv[:, None] * np.arange(L, dtype=np.float32)[None, :]
    cos, sin = np.cos(ang).astype(np.float32), np.sin(ang).astype(np.float32)
    return np.concatenate([cos] * 4, axis=0), np.concatenate([-sin, sin, -sin, sin], axis=0)


def kernel(**inputs):
    import concourse.bacc as _bacc
    from concourse.bass_utils import run_bass_kernel_spmd as _run

    nc = _bacc.Bacc("TRN2", target_bir_lowering=False, num_devices=1)
    arrays, aps = {}, {}
    for name in INPUTS:
        arrays[f"in_{name}"] = np.ascontiguousarray(inputs[name])
        aps[name] = nc.dram_tensor(f"in_{name}", arrays[f"in_{name}"].shape, F32, kind="ExternalInput").ap()
    tables = []
    for name, table in zip(("rope_cos", "rope_sin"), rope_tables()):
        arrays[name] = table
        tables.append(nc.dram_tensor(name, table.shape, F32, kind="ExternalInput").ap())
    out = nc.dram_tensor("out_0", (1, SEQ, D), F32, kind="ExternalOutput").ap()
    layer(nc, aps, tables[0], tables[1], out)
    r = _run(nc, [arrays], core_ids=[0])
    return r.results[0]["out_0"]
```

```python
from contextlib import ExitStack
import math

import numpy as np
import concourse.bass as bass
from concourse import mybir

F32 = mybir.dt.float32
F32R = mybir.dt.float32r
ALU = mybir.AluOpType
ACT = mybir.ActivationFunctionType
AXX = mybir.AxisListType.X

P = 128
BANK = 512
D = 1024
KT = D // P
META = 16
SEQ = 1024
L = META + SEQ
HD = 64
UNITS = 8
D_FF = 4 * D
EPS = 1e-6
LAM_INIT = 0.8 - 0.6 * math.exp(-0.3 * 0)
SCALE = 1.0 / math.sqrt(HD)
NEG = -1.0e30
ROPE_THETA = 10000.0

QA_COL, KA_COL, VA_COL = 0, D, 2 * D
QB_COL, KB_COL, VB_COL = 3 * D, 4 * D, 5 * D
GA_COL, GB_COL = 6 * D, 7 * D

Q_CHUNKS = [(META, 512), (META + 512, 512)]
K_CHUNKS = [(0, 352), (352, 344), (696, 344)]
QT = SEQ // P
KEY_TILES = QT + 1


def words(ap):
    return ap.bitcast(F32)


class Scratch:

    def __init__(self, nc):
        self.nc, self.ctx, self.used = nc, ExitStack(), []

    def __enter__(self):
        return self

    def __exit__(self, *a):
        if self.used and a[0] is None:
            self.nc.clear_and_free_semaphores(self.used)
            self.nc.all_engine_barrier()
        return self.ctx.__exit__(*a)

    def sb(self, name, shape, dt=F32):
        return self.ctx.enter_context(self.nc.sbuf_tensor(name, shape, dt))

    def sem(self, name):
        self.used.append(self.nc.alloc_semaphore(name))
        return self.used[-1]

    def sems(self, name, n):
        return [self.sem(f"{name}{i}") for i in range(n)]


def stage_norm(nc, ps, x, meta, norm_g, ident, hn_hi, hn_lo):
    with Scratch(nc) as s:
        xt = s.sb("n_xt", [P, QT + 1, D])
        sq = s.sb("n_sq", [P, D])
        ssum = s.sb("n_ssum", [P, QT + 1])
        rstd = s.sb("n_rstd", [P, QT + 1])
        g = s.sb("n_g", [P, KT])
        loaded = s.sems("n_loaded", QT + 1)
        g_loaded = s.sem("n_g_loaded")
        zeroed = s.sem("n_zeroed")
        summed, mean_eps, rooted = s.sem("n_summed"), s.sem("n_mean_eps"), s.sem("n_rooted")
        inverted, scaled = s.sem("n_inverted"), s.sem("n_scaled")
        turned, hi_done, lo_done = s.sem("n_turned"), s.sem("n_hi_done"), s.sem("n_lo_done")
        groups = []
        for kt in range(KT):
            groups.append((kt, 0, META, [QT]))
            groups.append((kt, META, 512, [0, 1, 2, 3]))
            groups.append((kt, META + 512, 512, [4, 5, 6, 7]))
        groups.sort(key=lambda q: q[1])
        with nc.Block() as block:
            @block.sync
            def _(sp):
                sp.dma_start(xt[0:META, QT, :], meta).then_inc(loaded[QT], 16)
                for t in range(QT):
                    sp.dma_start(xt[:, t, :], x[0, t * P:(t + 1) * P, :]).then_inc(loaded[t], 16)
                    if t == 0:
                        sp.dma_start(g[:, :], norm_g.rearrange("o (k p) -> p (o k)", p=P),
                                     allow_slow_non_contiguous=True).then_inc(g_loaded, 16)

            order = [QT] + list(range(QT))

            @block.scalar
            def _(act):
                for n, t in enumerate(order):
                    m = META if t == QT else P
                    act.wait_ge(loaded[t], 16)
                    if n:
                        act.wait_ge(summed, n)
                    act.activation(sq[0:m, :], xt[0:m, t, :], ACT.Square,
                                   accum_out=ssum[0:m, t:t + 1]).then_inc(summed, 1)
                    act.wait_ge(mean_eps, n + 1)
                    act.activation(rstd[0:m, t:t + 1], ssum[0:m, t:t + 1], ACT.Sqrt).then_inc(rooted, 1)
                act.wait_ge(g_loaded, 16)
                for n, (kt, c0, w, tiles) in enumerate(groups):
                    act.wait_ge(turned, n + 1)
                    act.activation(hn_hi[:, kt, c0:c0 + w], ps[n % 8][:, 0:w], ACT.Copy,
                                   scale=g[:, kt:kt + 1]).then_inc(hi_done, 1)

            @block.vector
            def _(dve):
                for n, t in enumerate(order):
                    m = META if t == QT else P
                    dve.wait_ge(summed, n + 1)
                    dve.tensor_scalar(ssum[0:m, t:t + 1], ssum[0:m, t:t + 1], 1.0 / D, EPS,
                                      ALU.mult, ALU.add).then_inc(mean_eps, 1)
                    dve.wait_ge(rooted, n + 1)
                    dve.reciprocal(rstd[0:m, t:t + 1], rstd[0:m, t:t + 1]).then_inc(inverted, 1)
                    dve.wait_ge(inverted, n + 1)
                    dve.tensor_scalar(xt[0:m, t, :], xt[0:m, t, :], rstd[0:m, t:t + 1], None,
                                      ALU.mult).then_inc(scaled, 1)
                dve.wait_ge(g_loaded, 16)
                for n, (kt, c0, w, tiles) in enumerate(groups):
                    dve.wait_ge(hi_done, n + 1)
                    dve.scalar_tensor_tensor(out=hn_lo[:, kt, c0:c0 + w], in0=ps[n % 8][:, 0:w],
                                             scalar=g[:, kt:kt + 1], in1=hn_hi[:, kt, c0:c0 + w],
                                             op0=ALU.mult, op1=ALU.subtract).then_inc(lo_done, 1)

            @block.tensor
            def _(pe):
                for n, (kt, c0, w, tiles) in enumerate(groups):
                    if n >= 8:
                        pe.wait_ge(lo_done, n - 7)
                    pe.wait_ge(scaled, order.index(tiles[-1]) + 1)
                    for i, t in enumerate(tiles):
                        m = META if t == QT else P
                        mm = pe.transpose(ps[n % 8][:, i * P:i * P + m], xt[0:m, t, kt * P:(kt + 1) * P],
                                          ident[0:m, 0:m])
                    mm.then_inc(turned, 1)


def product3(pe, bank, w_hi, w_lo, x_hi, x_lo, kts, first=True, last=True):
    for n, kt in enumerate(kts):
        pe.matmul(bank, w_lo(kt), x_hi(kt), start=(first and n == 0), stop=False)
        pe.matmul(bank, w_hi(kt), x_lo(kt), start=False, stop=False)
        mm = pe.matmul(bank, w_hi(kt), x_hi(kt), start=False, stop=(last and n == len(kts) - 1))
    return mm


def stage_channels(nc, ps, tag, w_in, cols, chunk_lists, hn_hi, hn_lo, rope, store, gate=None):
    chunks = [(w, t0, n) for w in range(2) for (t0, n) in chunk_lists[w]]
    C = len(chunks)
    first_of = [0, len(chunk_lists[0])]
    wv = w_in.rearrange("(k p) n -> p k n", p=P)
    with Scratch(nc) as s:
        w_raw = [s.sb(f"{tag}_w_raw{i}", [P, KT, P]) for i in range(2)]
        w_hi = [s.sb(f"{tag}_w_hi{i}", [P, KT, P], F32R) for i in range(2)]
        w_lo = [s.sb(f"{tag}_w_lo{i}", [P, KT, P], F32R) for i in range(2)]
        o_hi = s.sb(f"{tag}_o_hi", [P, C, BANK], F32 if gate else F32R)
        o_lo = None if gate else s.sb(f"{tag}_o_lo", [P, C, BANK], F32R)
        if rope:
            cos, sin = s.sb(f"{tag}_cos", [P, L]), s.sb(f"{tag}_sin", [P, L])
            swp = s.sb(f"{tag}_swp", [P, C, BANK])
            rot = s.sb(f"{tag}_rot", [P, C, BANK])
            rot2 = s.sb(f"{tag}_rot2", [P, C, BANK])
        w_loaded = s.sems(f"{tag}_w_loaded", 2)
        w_hi_done, w_lo_done = s.sems(f"{tag}_w_hi_done", 2), s.sems(f"{tag}_w_lo_done", 2)
        tables = s.sem(f"{tag}_tables")
        mm_done = s.sem(f"{tag}_mm_done")
        swapped, sin_done, cos_done, added = (s.sem(f"{tag}_swapped"), s.sem(f"{tag}_sin_done"),
                                              s.sem(f"{tag}_cos_done"), s.sem(f"{tag}_added"))
        hi_done, lo_done = s.sem(f"{tag}_hi_done"), s.sem(f"{tag}_lo_done")
        hi_stored, lo_stored = s.sems(f"{tag}_hi_stored", C), s.sems(f"{tag}_lo_stored", C)
        n_st = 1 if gate else 2

        with nc.Block() as block:
            @block.sync
            def _(sp):
                def load(u, w):
                    sp.dma_start(w_raw[w][:, :, :], wv[:, :, bass.ds(u * P + cols[w], P)]).then_inc(w_loaded[w], 16)

                if rope:
                    sp.dma_start(cos[:, :], rope[0]).then_inc(tables, 16)
                    sp.dma_start(sin[:, :], rope[1]).then_inc(tables, 16)
                load(0, 0)
                load(0, 1)

                def body(u, last):
                    for w in range(2):
                        if not last:
                            sp.wait_ge(w_lo_done[w], u + 1)
                            load(u + 1, w)
                    for c, (w, t0, n) in enumerate(chunks):
                        if gate:
                            sp.wait_ge(hi_done, u * C + (c + 1))
                            for dst, p0, m in store(u, w, 0, t0, n):
                                sp.dma_start(dst, words(o_hi[p0:p0 + m, c, 0:n])).then_inc(hi_stored[c], 16)
                        else:
                            sp.wait_ge(lo_done, u * C + (c + 1))
                            for dst, p0, m in store(u, w, 0, t0, n):
                                sp.dma_start(dst, words(o_hi[p0:p0 + m, c, 0:n])).then_inc(hi_stored[c], 16)
                            for dst, p0, m in store(u, w, 1, t0, n):
                                sp.dma_start(dst, words(o_lo[p0:p0 + m, c, 0:n])).then_inc(lo_stored[c], 16)

                with sp.Fori(0, UNITS - 1) as u:
                    body(u, False)
                body(UNITS - 1, True)
                for c in range(C):
                    sp.wait_ge(hi_stored[c], 16 * n_st * (UNITS + 1))
                    if not gate:
                        sp.wait_ge(lo_stored[c], 16 * n_st * (UNITS + 1))

            @block.scalar
            def _(act):
                def split(u, w):
                    act.wait_ge(w_loaded[w], u * 16 + 16)
                    act.wait_ge(mm_done, u * C + (first_of[w] + len(chunk_lists[w])))
                    act.activation(w_hi[w][:, :, :], w_raw[w][:, :, :], ACT.Copy).then_inc(w_hi_done[w], 1)

                def swap(u, c):
                    w, t0, n = chunks[c]
                    act.wait_ge(mm_done, (u + 1) * C + (c + 1))
                    act.wait_ge(added, u * C + (c + 1))
                    for q in range(4):
                        o, i = 32 * q, 32 * (q ^ 1)
                        last = act.activation(swp[o:o + 32, c, 0:n], ps[c][i:i + 32, 0:n], ACT.Copy)
                    last.then_inc(swapped, 1)

                def high(u, c):
                    w, t0, n = chunks[c]
                    act.wait_ge(hi_stored[c], (u + 1) * 16 * n_st)
                    if rope:
                        act.wait_ge(added, (u + 1) * C + (c + 1))
                        act.activation(o_hi[:, c, 0:n], rot[:, c, 0:n], ACT.Copy).then_inc(hi_done, 1)
                    else:
                        act.wait_ge(mm_done, (u + 1) * C + (c + 1))
                        act.activation(o_hi[:, c, 0:n], ps[c][:, 0:n],
                                       ACT.Sigmoid if gate else ACT.Copy).then_inc(hi_done, 1)

                def body(u, last):
                    split(u, 1)
                    for c in range(C + 1):
                        if rope and c < C:
                            swap(u, c)
                        if c == first_of[1] and not last:
                            split(u + 1, 0)
                        if rope and c >= 1:
                            high(u, c - 1)
                        if not rope and c < C:
                            high(u, c)

                act.sem_inc(mm_done, C)
                for c in range(C):
                    act.sem_inc(hi_stored[c], 16 * n_st)
                if rope:
                    act.sem_inc(added, C)
                split(0, 0)
                with act.Fori(0, UNITS - 1) as u:
                    body(u, False)
                body(UNITS - 1, True)

            @block.gpsimd
            def _(pool):
                def body(u):
                    for c, (w, t0, n) in enumerate(chunks):
                        pool.wait_ge(swapped, u * C + (c + 1))
                        pool.tensor_tensor(rot2[:, c, 0:n], swp[:, c, 0:n], sin[:, t0:t0 + n],
                                           ALU.mult).then_inc(sin_done, 1)
                if rope:
                    pool.wait_ge(tables, 32)
                    with pool.Fori(0, UNITS) as u:
                        body(u)

            @block.vector
            def _(dve):
                def split(u, w):
                    dve.wait_ge(w_hi_done[w], u + 1)
                    dve.tensor_tensor(w_lo[w][:, :, :], w_raw[w][:, :, :], w_hi[w][:, :, :],
                                      ALU.subtract).then_inc(w_lo_done[w], 1)

                def times_cos(u, c):
                    w, t0, n = chunks[c]
                    dve.wait_ge(swapped, u * C + (c + 1))
                    dve.wait_ge(hi_done, (u + 1) * C - C + c + 1)
                    dve.tensor_tensor(rot[:, c, 0:n], ps[c][:, 0:n], cos[:, t0:t0 + n],
                                      ALU.mult).then_inc(cos_done, 1)

                def add(u, c):
                    w, t0, n = chunks[c]
                    dve.wait_ge(sin_done, u * C + (c + 1))
                    dve.wait_ge(cos_done, u * C + (c + 1))
                    dve.tensor_tensor(rot[:, c, 0:n], rot[:, c, 0:n], rot2[:, c, 0:n], ALU.add).then_inc(added, 1)

                def low(u, c):
                    w, t0, n = chunks[c]
                    dve.wait_ge(lo_stored[c], (u + 1) * 16 * n_st)
                    dve.wait_ge(hi_done, (u + 1) * C + (c + 1) if rope else u * C + (c + 1))
                    src = rot[:, c, 0:n] if rope else ps[c][:, 0:n]
                    dve.tensor_tensor(o_lo[:, c, 0:n], src, o_hi[:, c, 0:n], ALU.subtract).then_inc(lo_done, 1)

                def body(u, last):
                    split(u, 1)
                    for c in range(C + 2):
                        if rope and c < C:
                            times_cos(u, c)
                        if c == first_of[1] and not last:
                            split(u + 1, 0)
                        if rope and 1 <= c <= C:
                            add(u, c - 1)
                        if rope and c >= 2:
                            low(u, c - 2)
                        if not rope and not gate and c < C:
                            low(u, c)

                if not gate:
                    for c in range(C):
                        dve.sem_inc(lo_stored[c], 16 * n_st)
                if rope:
                    dve.wait_ge(tables, 32)
                    dve.sem_inc(hi_done, C)
                split(0, 0)
                with dve.Fori(0, UNITS - 1) as u:
                    body(u, False)
                body(UNITS - 1, True)

            @block.tensor
            def _(pe):
                bank_free = cos_done if rope else (hi_done if gate else lo_done)

                def body(u, first):
                    for c, (w, t0, n) in enumerate(chunks):
                        if c in first_of:
                            pe.wait_ge(w_lo_done[w], u + 1)
                        if not first:
                            pe.wait_ge(bank_free, u * C - C + c + 1)
                        mm = product3(pe, ps[c][:, 0:n],
                                      lambda k: w_hi[w][:, k, :], lambda k: w_lo[w][:, k, :],
                                      lambda k: hn_hi[:, k, t0:t0 + n], lambda k: hn_lo[:, k, t0:t0 + n], range(KT))
                        mm.then_inc(mm_done, 1)

                body(0, True)
                with pe.Fori(1, UNITS) as u:
                    body(u, False)


def stage_values(nc, ps, w_in, hn_hi, hn_lo, v_dram):
    T = QT + 1
    GROUPS = 2
    UPG = BANK // P
    with Scratch(nc) as s:
        w_raw = s.sb("v_w_raw", [P, KT, BANK])
        w_hi, w_lo = s.sb("v_w_hi", [P, KT, BANK], F32R), s.sb("v_w_lo", [P, KT, BANK], F32R)
        out = s.sb("v_out", [P, T, UPG, 2 * P], F32R)
        w_loaded = s.sem("v_w_loaded")
        w_hi_done, w_lo_done = s.sem("v_w_hi_done"), s.sem("v_w_lo_done")
        mm_done, hi_done, lo_done = s.sem("v_mm_done"), s.sem("v_hi_done"), s.sem("v_lo_done")
        stored = s.sems("v_stored", T)
        wv = w_in.rearrange("(k p) n -> p k n", p=P)
        vd = v_dram.rearrange("(g u) t c -> g t u c", u=UPG)

        def rows(t):
            return (0, META) if t == QT else (META + t * P, P)

        with nc.Block() as block:
            @block.sync
            def _(sp):
                cols = [VA_COL, VA_COL + BANK, VB_COL, VB_COL + BANK]

                def load(n):
                    sp.wait_ge(w_lo_done, n * KT + KT)
                    sp.dma_start(w_raw[:, :, :], wv[:, :, cols[n]:cols[n] + BANK]).then_inc(w_loaded, 16)

                load(0)
                for n in range(len(cols)):
                    if n + 1 < len(cols):
                        load(n + 1)
                    for t in range(T):
                        t0, m = rows(t)
                        sp.wait_ge(lo_done, n * T + (t + 1))
                        sp.dma_start(vd[n, t0:t0 + m, :, :], words(out[0:m, t, :, :])).then_inc(stored[t], 16)
                for t in range(T):
                    sp.wait_ge(stored[t], 16 * (2 * GROUPS + 1))

            @block.scalar
            def _(act):
                act.sem_inc(mm_done, T)
                for t in range(T):
                    act.sem_inc(stored[t], 16)
                for b in range(2):
                    with act.Fori(0, GROUPS) as g:
                        n = b * GROUPS + g
                        act.wait_ge(w_loaded, n * 16 + 16)
                        act.wait_ge(mm_done, n * T + T)
                        for k in range(KT):
                            act.activation(w_hi[:, k, :], w_raw[:, k, :], ACT.Copy).then_inc(w_hi_done, 1)
                        for t in range(T):
                            t0, m = rows(t)
                            act.wait_ge(mm_done, n * T + (T + t + 1))
                            act.wait_ge(stored[t], n * 16 + 16)
                            src = ps[t % 8][0:m, :].rearrange("p (u c) -> p u c", c=P)
                            act.activation(out[0:m, t, :, 0:HD], src[:, :, 0:HD], ACT.Copy)
                            act.activation(out[0:m, t, :, 3 * HD:4 * HD], src[:, :, HD:P], ACT.Copy).then_inc(hi_done, 1)

            @block.vector
            def _(dve):
                dve.sem_inc(w_lo_done, KT)
                for b in range(2):
                    with dve.Fori(0, GROUPS) as g:
                        n = b * GROUPS + g
                        for k in range(KT):
                            dve.wait_ge(w_hi_done, n * KT + (k + 1))
                            dve.tensor_tensor(w_lo[:, k, :], w_raw[:, k, :], w_hi[:, k, :],
                                              ALU.subtract).then_inc(w_lo_done, 1)
                        for t in range(T):
                            t0, m = rows(t)
                            dve.wait_ge(hi_done, n * T + (t + 1))
                            src = ps[t % 8][0:m, :].rearrange("p (u c) -> p u c", c=P)
                            dve.tensor_tensor(out[0:m, t, :, HD:2 * HD], src[:, :, 0:HD],
                                              out[0:m, t, :, 0:HD], ALU.subtract)
                            dve.tensor_tensor(out[0:m, t, :, 2 * HD:3 * HD], src[:, :, HD:P],
                                              out[0:m, t, :, 3 * HD:4 * HD], ALU.subtract).then_inc(lo_done, 1)

            @block.tensor
            def _(pe):
                def body(n, first):
                    for t in range(T):
                        t0, m = rows(t)
                        if t == 8:
                            pe.wait_ge(lo_done, n * T + 1)
                        elif t == 0 and not first:
                            pe.wait_ge(lo_done, n * T)
                        elif not first:
                            pe.wait_ge(lo_done, n * T - T + t + 1)
                        for k in range(KT):
                            if t == 0:
                                pe.wait_ge(w_lo_done, n * KT + (KT + k + 1))
                            pe.matmul(ps[t % 8][0:m, :], hn_hi[:, k, t0:t0 + m], w_lo[:, k, :],
                                      start=(k == 0), stop=False)
                            pe.matmul(ps[t % 8][0:m, :], hn_lo[:, k, t0:t0 + m], w_hi[:, k, :],
                                      start=False, stop=False)
                            mm = pe.matmul(ps[t % 8][0:m, :], hn_hi[:, k, t0:t0 + m], w_hi[:, k, :],
                                           start=False, stop=(k == KT - 1))
                        mm.then_inc(mm_done, 1)

                body(0, True)
                with pe.Fori(1, 2 * GROUPS) as n:
                    body(n, False)


def score_chunks(i):
    w = META + P * (i + 1)
    return {1: [(0, w)], 2: [(0, w // 2), (w // 2, w - w // 2)], 3: K_CHUNKS}[-(-w // BANK)]


def turn_groups(i):
    tiles = list(range(i + 2))
    return [tiles[n:n + 4] for n in range(0, len(tiles), 4)]


CHUNKS_BEFORE = [sum(len(score_chunks(j)) for j in range(i)) for i in range(QT + 1)]
GROUPS_BEFORE = [sum(len(turn_groups(j)) for j in range(i)) for i in range(QT + 1)]
CPU = 2 * CHUNKS_BEFORE[QT]
GPH = GROUPS_BEFORE[QT]


def key_col(tile):
    return 0 if tile == 0 else META + P * (tile - 1)


def chunk_no(i, h, c):
    return 2 * CHUNKS_BEFORE[i] + h * len(score_chunks(i)) + c


def interleave(a, b):
    out, used = [], 0
    for n, x in enumerate(a):
        out.append(x)
        upto = (n + 1) * len(b) // len(a)
        out += b[used:upto]
        used = upto
    return out


def slot_order(chunks, groups):
    half = len(chunks) // 2
    g = len(groups) // 2
    return (interleave([("chunk", c) for c in chunks[:half]], [("group", x) for x in groups[:g]]),
            interleave([("chunk", c) for c in chunks[half:]], [("group", x) for x in groups[g:]]))


def groups_later(items):
    out = list(items)
    for n in range(len(out) - 1, 0, -1):
        if out[n][0] == "chunk" and out[n - 1][0] == "group":
            out[n - 1], out[n] = out[n], out[n - 1]
    return out


class UnitBuffers:

    def __init__(self, s, tag, v_parts):
        self.v_parts = v_parts
        self.QK_LOADS, self.V_LOADS = 2 + 8, 2 * len(v_parts)
        self.q = [[s.sb(f"{tag}_q{p}{h}", [P, SEQ], F32R) for h in range(2)] for p in range(2)]
        self.k = [[[s.sb(f"{tag}_k{p}{h}{x}", [P, L], F32R) for x in range(2)] for h in range(2)] for p in range(2)]
        self.v = [s.sb(f"{tag}_v{p}", [P, KEY_TILES, 2 * P], F32R) for p in range(2)]
        self.qk_loaded, self.v_loaded = s.sems(f"{tag}_qk_loaded", 2), s.sems(f"{tag}_v_loaded", 2)

    def zero_meta(self, dve, done):
        for p in range(2):
            dve.memset(self.v[p][:, 0, :].bitcast(F32), 0.0).then_inc(done, 1)

    def load(self, sp, u, p, q_dram, k_dram, v_dram, v_unit0):
        for h in range(2):
            sp.dma_start(words(self.q[p][h][:, :]), q_dram[u, h]).then_inc(self.qk_loaded[p], 16)
            for x in range(2):
                for half in range(2):
                    sp.dma_start(words(self.k[p][h][x][half * HD:(half + 1) * HD, :]), k_dram[u, h, x]).then_inc(self.qk_loaded[p], 16)
        for a, b, n in self.v_parts:
            sp.dma_start(words(self.v[p][0:META, 0, b:b + n]),
                         v_dram[u + v_unit0, 0:META, a:a + n]).then_inc(self.v_loaded[p], 16)
            sp.dma_start(words(self.v[p][:, 1:KEY_TILES, b:b + n]),
                         v_dram[u + v_unit0, META:L, a:a + n].rearrange("(j p) c -> p j c", p=P)).then_inc(self.v_loaded[p], 16)


def stage_diff(nc, ps, q_dram, k_dram, v_dram, o_dram, lams, subln_g, ident, ident_r, mask_r):
    EXP_LAG, MIX_LAG, LAG = 1, 2, 4
    S_BANKS, T_BANKS, PV_BANK, SUM_BANK = ps[0:4], ps[4:6], ps[6], ps[7]
    with Scratch(nc) as s:
        ub = UnitBuffers(s, "d", [(0, 0, HD), (3 * HD, HD, HD), (HD, P, P)])
        probs = [s.sb(f"d_probs{i}", [P, 2, META + P * (i + 1)]) for i in range(QT)]
        at_hi, at_lo = s.sb("d_at_hi", [P, 2, KEY_TILES, 2 * P], F32R), s.sb("d_at_lo", [P, 2, KEY_TILES, 2 * P], F32R)
        mx = s.sb("d_mx", [P, QT, 2, 4])
        neg_max = s.sb("d_neg_max", [P, QT, 2])
        row_sum = s.sb("d_row_sum", [P, QT, 2])
        weight = s.sb("d_weight", [P, QT, 2])
        coef = s.sb("d_coef", [P, QT])
        o_raw = s.sb("d_o_raw", [P, SEQ])
        o_sq = s.sb("d_o_sq", [P, BANK])
        o_rstd = s.sb("d_o_rstd", [P, BANK])
        o_norm = s.sb("d_o_norm", [P, BANK])
        o_hi, o_lo = s.sb("d_o_hi", [P, 2, BANK], F32R), s.sb("d_o_lo", [P, 2, BANK], F32R)
        ones = s.sb("d_ones", [P, P])
        lam_in = s.sb("d_lam_in", [1, 4, HD])
        lam_t = s.sb("d_lam_t", [1, HD])
        lam_s = s.sb("d_lam_s", [1, 8])
        neg_lam = s.sb("d_neg_lam", [P, 1])
        g8 = s.sb("d_g8", [P, 1])
        eps = s.sb("d_eps", [P, 1])
        small_loaded, prep = s.sem("d_small_loaded"), s.sem("d_prep")
        prep_exp, lam_ready, lam_spread = s.sem("d_prep_exp"), s.sem("d_lam_ready"), s.sem("d_lam_spread")
        scored, copied, shifted, exped = s.sem("d_scored"), s.sem("d_copied"), s.sem("d_shifted"), s.sem("d_exped")
        inverted, coef_done, scaled, mixed = s.sem("d_inverted"), s.sem("d_coef_done"), s.sem("d_scaled"), s.sem("d_mixed")
        turned, at_hi_done, at_lo_done = s.sem("d_turned"), s.sem("d_at_hi_done"), s.sem("d_at_lo_done")
        pv_done, o_copied, squared, summed = s.sem("d_pv_done"), s.sem("d_o_copied"), s.sem("d_squared"), s.sem("d_summed")
        normed = s.sem("d_normed")
        o_chain, o_hi_done, o_lo_done = s.sem("d_o_chain"), s.sem("d_o_hi_done"), s.sem("d_o_lo_done")
        o_stored = s.sems("d_o_stored", 2)

        def slot(i, j):
            chunks = [] if i is None else [(h, c) + kc for h in range(2) for c, kc in enumerate(score_chunks(i))]
            groups = [] if j is None else list(enumerate(turn_groups(j)))
            if not chunks:
                return [], [("group", g) for g in groups]
            return slot_order(chunks, groups)

        def back(u, i, lag, first):
            return (u, i - lag) if i >= lag else (u, None) if first else (u - 1, QT + i - lag)

        def has_before(u):
            return not (isinstance(u, int) and u == 0)

        def late(j, lag):
            return j + LAG - lag if j + LAG - lag < QT else None

        def run(eng, unit, flush):
            unit(0, 0, 0, True)
            unit(0, 1, 1, False)
            with eng.Fori(1, UNITS // 2) as v:
                unit(v, 0, v * 2, False)
                unit(v, 1, v * 2 + 1, False)
            flush(UNITS - 1)

        with nc.Block() as block:
            @block.sync
            def _(sp):
                for n, l in enumerate(lams):
                    sp.dma_start(lam_in[:, n, :], l).then_inc(small_loaded, 16)
                sp.dma_start(g8[:, :], subln_g.rearrange("o p -> p o"), allow_slow_non_contiguous=True).then_inc(small_loaded, 16)
                sp.wait_ge(prep, 2)
                ub.load(sp, 0, 0, q_dram, k_dram, v_dram, 0)
                ub.load(sp, 1, 1, q_dram, k_dram, v_dram, 0)

                def stores(u):
                    for half in range(2):
                        sp.wait_ge(o_lo_done, u * 2 + (half + 3))
                        for x, src in enumerate((o_hi, o_lo)):
                            sp.dma_start(o_dram[x, bass.ds(u * P, P), half * BANK:(half + 1) * BANK],
                                         words(src[:, half, :])).then_inc(o_stored[half], 16)

                with sp.Fori(0, UNITS // 2 - 1) as v:
                    for p in range(2):
                        sp.wait_ge(pv_done, (v * 2 + (p + 1)) * 4 + 2)
                        ub.load(sp, v * 2 + (p + 2), p, q_dram, k_dram, v_dram, 0)
                        stores(v * 2 + p)
                for p in range(2):
                    stores(UNITS - 2 + p)
                for half in range(2):
                    sp.wait_ge(o_stored[half], 32 * (UNITS + 1))

            @block.tensor
            def _(pe):
                def score(p, u, i, h, c, k0, n):
                    no = chunk_no(i, h, c)
                    bank = S_BANKS[no % 4]
                    pe.wait_ge(copied, u * CPU + (no + 1))
                    q = ub.q[p][h][:, i * P:(i + 1) * P]
                    last = c == len(score_chunks(i)) - 1
                    pe.matmul(bank[:, 0:n], q, ub.k[p][h][1][:, k0:k0 + n], start=True, stop=False)
                    mm = pe.matmul(bank[:, 0:n], q, ub.k[p][h][0][:, k0:k0 + n], start=False, stop=not last)
                    if last:
                        mm = pe.matmul(bank[:, n - P:n], ident_r[:, :], mask_r[:, :], start=False, stop=True)
                    mm.then_inc(scored, 1)

                def turn(u, i, n, tiles):
                    no = GROUPS_BEFORE[i] + n
                    if n == 0:
                        pe.wait_ge(mixed, u * QT + (i + 1))
                    pe.wait_ge(at_lo_done, u * GPH + (no + 1))
                    for x, t in enumerate(tiles):
                        mm = pe.transpose(T_BANKS[no % 2][:, x * P:(x + 1) * P],
                                          probs[i][:, 0, key_col(t):key_col(t) + P], ident[:, :])
                    mm.then_inc(turned, 1)

                def value_tile(p, u, pair, t):
                    last = 2 * pair + 2
                    at, q0 = pair % 2, P if t == last else 0
                    if t == 0:
                        pe.wait_ge(at_lo_done, u * GPH + (2 + GROUPS_BEFORE[2 * pair + 2]))
                        pe.wait_ge(o_copied, u * 4 + (pair + 1))
                    v_hi, v_lo = ub.v[p][:, t, 0:P], ub.v[p][:, t, P:2 * P]
                    o = PV_BANK[:, q0:2 * P]
                    pe.matmul(o, v_lo, at_hi[:, at, t, q0:2 * P], start=(t == 0), stop=False)
                    pe.matmul(o, v_hi, at_lo[:, at, t, q0:2 * P], start=False, stop=False)
                    mm = pe.matmul(o, v_hi, at_hi[:, at, t, q0:2 * P], start=False, stop=(t == last))
                    if t == last:
                        mm.then_inc(pv_done, 1)

                def sums(u, half):
                    pe.wait_ge(squared, u * 2 + (half + 1))
                    pe.wait_ge(o_lo_done, u * 2 + (half + 2))
                    pe.matmul(SUM_BANK[:, :], ones[:, :], o_sq[:, :], start=True, stop=True).then_inc(summed, 1)

                def step(p, u, i, lp, lu, j):
                    items = sum(slot(i, j), [])
                    tiles = []
                    if j is not None and (j > 1 or has_before(lu)):
                        vp, vu, pair = (lp, lu, j // 2 - 1) if j > 1 else (1 - lp, lu - 1, 3)
                        n_t = 2 * pair + 3
                        tiles = range(n_t // 2) if j % 2 == 0 else range(n_t // 2, n_t)
                    done = 0
                    for n, (kind, x) in enumerate(items):
                        if kind == "chunk":
                            score(p, u, i, *x)
                        else:
                            turn(lu, j, *x)
                        upto = (n + 1) * len(tiles) // len(items)
                        for t in tiles[done:upto]:
                            value_tile(vp, vu, pair, t)
                        done = upto
                    if j == 7:
                        sums(lu, 0)
                    if j == 4 and has_before(lu):
                        sums(lu - 1, 1)

                def unit(v, p, u, first):
                    pe.wait_ge(ub.qk_loaded[p], (v + 1) * (16 * ub.QK_LOADS))
                    for i in range(QT):
                        if i == LAG:
                            pe.wait_ge(ub.v_loaded[p], (v + 1) * (16 * ub.V_LOADS))
                        lu, j = back(u, i, LAG, first)
                        step(p, u, i, p if i >= LAG else 1 - p, lu, j)

                def flush(u):
                    for j in range(QT - LAG, QT):
                        step(0, 0, None, u % 2, u, j)
                    for t in range(KEY_TILES):
                        value_tile(u % 2, u, 3, t)
                    sums(u, 1)

                pe.wait_ge(prep, 5)
                run(pe, unit, flush)

            @block.vector
            def _(dve):
                def copy_scores(u, i, h, c, k0, n):
                    no = chunk_no(i, h, c)
                    dve.wait_ge(scored, u * CPU + (no + 1))
                    if c:
                        dve.wait_ge(copied, u * CPU + (no + 4))
                    dve.tensor_scalar(probs[i][:, h, k0:k0 + n], S_BANKS[no % 4][:, 0:n], 1.0,
                                      mx[:, i, h, c - 1:c] if c else None, ALU.mult, ALU.max,
                                      accum_out=mx[:, i, h, c:c + 1]).then_inc(copied, 1)

                def shift(u, i, h):
                    c = len(score_chunks(i)) - 1
                    dve.wait_ge(copied, u * CPU + (chunk_no(i, h, c) + 5))
                    dve.tensor_scalar(neg_max[:, i, h:h + 1], mx[:, i, h, c:c + 1], -SCALE, None,
                                      ALU.mult).then_inc(shifted, 1)

                def invert(u, i, h):
                    dve.wait_ge(exped, (u * QT + i) * 2 + (h + 1))
                    dve.reciprocal(weight[:, i, h:h + 1], row_sum[:, i, h:h + 1]).then_inc(inverted, 1)
                    if h:
                        dve.wait_ge(inverted, (u * QT + i) * 2 + 2)
                        dve.tensor_scalar(coef[:, i:i + 1], weight[:, i, 1:2], neg_lam[:, 0:1], None,
                                          ALU.mult).then_inc(coef_done, 1)

                def mix(u, i):
                    w = META + P * (i + 1)
                    dve.wait_ge(coef_done, u * QT + (i + 1))
                    dve.wait_ge(scaled, u * QT + (i + 1))
                    dve.scalar_tensor_tensor(out=probs[i][:, 0, 0:w], in0=probs[i][:, 1, 0:w],
                                             scalar=coef[:, i:i + 1], in1=probs[i][:, 0, 0:w],
                                             op0=ALU.mult, op1=ALU.add).then_inc(mixed, 1)

                def low(u, i, n, tiles):
                    no = GROUPS_BEFORE[i] + n
                    m, q0, at = len(tiles), (i % 2) * P, i // 2 % 2
                    dve.wait_ge(at_hi_done, u * GPH + (no + 1))
                    dve.tensor_tensor(at_lo[:, at, tiles[0]:tiles[0] + m, q0:q0 + P],
                                      T_BANKS[no % 2][:, 0:m * P].rearrange("p (t c) -> p t c", c=P),
                                      at_hi[:, at, tiles[0]:tiles[0] + m, q0:q0 + P],
                                      ALU.subtract).then_inc(at_lo_done, 1)

                def square(u, half):
                    dve.wait_ge(o_copied, u * 4 + (2 * half + 3))
                    dve.tensor_tensor(o_sq[:, :], o_raw[:, half * BANK:(half + 1) * BANK],
                                      o_raw[:, half * BANK:(half + 1) * BANK], ALU.mult).then_inc(squared, 1)

                def normalise(u, half):
                    dve.wait_ge(o_chain, (u * 2 + half) * 2 + 2)
                    dve.scalar_tensor_tensor(out=o_norm[:, :], in0=o_raw[:, half * BANK:(half + 1) * BANK],
                                             scalar=g8[:, 0:1], in1=o_rstd[:, :], op0=ALU.mult,
                                             op1=ALU.mult).then_inc(normed, 1)
                    dve.wait_ge(o_hi_done, u * 2 + (half + 1))
                    dve.wait_ge(o_stored[half], u * 32 + 32)
                    dve.tensor_tensor(o_lo[:, half, :], o_norm[:, :], o_hi[:, half, :], ALU.subtract).then_inc(o_lo_done, 1)

                def step(u, i, mu, m, lu, j):
                    for half, items in enumerate(slot(i, j)):
                        if m is not None:
                            invert(mu, m, half)
                        for kind, x in groups_later(items):
                            if kind == "chunk":
                                copy_scores(u, i, *x)
                            else:
                                low(lu, j, *x)
                        if i is not None:
                            shift(u, i, half)
                    if m is not None:
                        mix(mu, m)
                    if j == 6:
                        square(lu, 0)
                    if j is not None and has_before(lu):
                        if j == 0:
                            normalise(lu - 1, 0)
                        if j == 3:
                            square(lu - 1, 1)
                        if j == 5:
                            normalise(lu - 1, 1)

                def unit(v, p, u, first):
                    for i in range(QT):
                        lu, j = back(u, i, LAG, first)
                        step(u, i, *back(u, i, MIX_LAG, first), lu, j)

                def flush(u):
                    for j in range(QT - LAG, QT):
                        step(u, None, u, late(j, MIX_LAG), u, j)
                    normalise(u, 0)
                    square(u, 1)
                    normalise(u, 1)

                ub.zero_meta(dve, prep)
                dve.memset(ones[:, :], 1.0).then_inc(prep, 1)
                dve.memset(eps[:, :], EPS).then_inc(prep, 1)
                dve.wait_ge(small_loaded, 16 * 5)
                dve.tensor_scalar(g8[:, :], g8[:, :], 1.0 - LAM_INIT, None, ALU.mult).then_inc(prep, 1)
                for n in range(2):
                    dve.tensor_tensor(lam_in[:, 2 * n, :], lam_in[:, 2 * n, :], lam_in[:, 2 * n + 1, :],
                                      ALU.mult).then_inc(lam_ready, 1)
                    dve.wait_ge(lam_ready, 2 * n + 1)
                    dve.reduce_sum(lam_s[:, n:n + 1], lam_in[:, 2 * n, :], AXX).then_inc(lam_ready, 1)
                dve.wait_ge(prep_exp, 1)
                dve.tensor_scalar(lam_s[:, 4:5], lam_s[:, 2:3], LAM_INIT, None, ALU.add).then_inc(lam_ready, 1)
                dve.wait_ge(lam_ready, 5)
                dve.tensor_tensor(lam_s[:, 5:6], lam_s[:, 3:4], lam_s[:, 4:5], ALU.subtract).then_inc(lam_ready, 1)
                dve.wait_ge(lam_spread, 1)
                dve.sem_inc(copied, 4)
                dve.sem_inc(at_lo_done, 2)
                dve.sem_inc(o_lo_done, 2)
                run(dve, unit, flush)

            @block.scalar
            def _(act):
                def exp(u, i, h):
                    w = META + P * (i + 1)
                    act.wait_ge(shifted, (u * QT + i) * 2 + (h + 1))
                    act.activation(probs[i][:, h, 0:w], probs[i][:, h, 0:w], ACT.Exp, bias=neg_max[:, i, h:h + 1],
                                   scale=SCALE, accum_out=row_sum[:, i, h:h + 1]).then_inc(exped, 1)

                def high(u, i, n, tiles):
                    no = GROUPS_BEFORE[i] + n
                    m, q0, at = len(tiles), (i % 2) * P, i // 2 % 2
                    if n == 0 and i % 2 == 0:
                        act.wait_ge(pv_done, u * 4 + (i // 2 + 1))
                    act.wait_ge(turned, u * GPH + (no + 1))
                    act.activation(at_hi[:, at, tiles[0]:tiles[0] + m, q0:q0 + P],
                                   T_BANKS[no % 2][:, 0:m * P].rearrange("p (t c) -> p t c", c=P),
                                   ACT.Copy).then_inc(at_hi_done, 1)

                def copy_out(u, q):
                    act.wait_ge(pv_done, u * 4 + (q + 3))
                    act.wait_ge(o_lo_done, u * 2 + (q // 2 + 1))
                    act.activation(o_raw[:, q * 2 * P:(q + 1) * 2 * P], PV_BANK[:, 0:2 * P], ACT.Copy).then_inc(o_copied, 1)

                def out_rstd(u, half):
                    act.wait_ge(summed, u * 2 + (half + 1))
                    act.wait_ge(normed, u * 2 + (half + 1))
                    act.activation(o_rstd[:, :], SUM_BANK[:, :], ACT.Ln, bias=eps[:, 0:1], scale=1.0 / P).then_inc(o_chain, 1)
                    act.wait_ge(o_chain, (u * 2 + half) * 2 + 1)
                    act.activation(o_rstd[:, :], o_rstd[:, :], ACT.Exp, scale=-0.5).then_inc(o_chain, 1)

                def out_high(u, half):
                    act.wait_ge(normed, u * 2 + (half + 2))
                    act.wait_ge(o_stored[half], u * 32 + 32)
                    act.activation(o_hi[:, half, :], o_norm[:, :], ACT.Copy).then_inc(o_hi_done, 1)

                def step(eu, e, lu, j):
                    if j in (4, 6):
                        copy_out(lu, j // 2 - 2)
                    if j in (0, 2) and has_before(lu):
                        copy_out(lu - 1, j // 2 + 2)
                    for half, items in enumerate(slot(e, j)):
                        if e is not None:
                            exp(eu, e, half)
                        for kind, x in items:
                            if kind == "group":
                                high(lu, j, *x)
                    if j is not None and has_before(lu):
                        if j == 0:
                            out_rstd(lu - 1, 0)
                            out_high(lu - 1, 0)
                        if j == 5:
                            out_rstd(lu - 1, 1)
                            out_high(lu - 1, 1)

                def unit(v, p, u, first):
                    for i in range(QT):
                        lu, j = back(u, i, LAG, first)
                        step(*back(u, i, EXP_LAG, first), lu, j)

                def flush(u):
                    for j in range(QT - LAG, QT):
                        step(u, late(j, EXP_LAG), u, j)
                    copy_out(u, 2)
                    out_rstd(u, 0)
                    out_high(u, 0)
                    copy_out(u, 3)
                    out_rstd(u, 1)
                    out_high(u, 1)

                act.preload_act_table_set("natural_log_exp_and_others")
                act.sem_inc(pv_done, 2)
                act.sem_inc(o_copied, 1)
                act.sem_inc(normed, 1)
                act.wait_ge(lam_ready, 4)
                act.wait_ge(prep, 5)
                act.activation(lam_s[:, 2:4], lam_s[:, 0:2], ACT.Exp).then_inc(prep_exp, 1)
                for half in range(2):
                    act.sem_inc(o_stored[half], 32)
                run(act, unit, flush)

            @block.gpsimd
            def _(pool):
                pool.wait_ge(lam_ready, 6)
                pool.partition_broadcast(neg_lam[:, :], lam_s[0:1, 5:6]).then_inc(lam_spread, 1)
                with pool.Fori(0, UNITS) as u:
                    for i in range(QT):
                        w = META + P * (i + 1)
                        pool.wait_ge(inverted, (u * QT + i) * 2 + 1)
                        pool.tensor_tensor(probs[i][:, 0, 0:w], probs[i][:, 0, 0:w], weight[:, i, 0:1].broadcast_to([P, w]),
                                           ALU.mult).then_inc(scaled, 1)


def stage_stick(nc, ps, q_dram, k_dram, v_dram, o_dram, ident, ident_r, mask_r, oa_dram, oa_early):
    ITEMS = 2 * QT
    LAG, RING = 3, 4
    S_BANKS, T_BANKS, PV_BANKS = ps[0:4], ps[4:6], ps[6:8]
    GPU = 2 * GPH
    with Scratch(nc) as s:
        ub = UnitBuffers(s, "s", [(0, 0, 2 * P)])
        take = s.sb("s_take", [P, RING, L])
        leave = s.sb("s_leave", [P, RING, L])
        one = s.sb("s_one", [P, L])
        at_hi = s.sb("s_at_hi", [P, 2, KEY_TILES, 2 * P], F32R)
        at_lo = s.sb("s_at_lo", [P, 2, KEY_TILES, 2 * P], F32R)
        o_low = s.sb("s_o_low", [P, 2 * P])
        o_sum = s.sb("s_o_sum", [P, 2 * P])
        o_hi, o_lo = s.sb("s_o_hi", [P, 4, 2 * P], F32R), s.sb("s_o_lo", [P, 4, 2 * P], F32R)
        prep, early_loaded = s.sem("s_prep"), s.sem("s_early_loaded")
        scored, split = s.sem("s_scored"), s.sem("s_split")
        scanned, taken = s.sem("s_scanned"), s.sem("s_taken")
        turned, at_hi_done, at_lo_done = s.sem("s_turned"), s.sem("s_at_hi_done"), s.sem("s_at_lo_done")
        pv_done, o_low_done, o_summed = s.sem("s_pv_done"), s.sem("s_o_low_done"), s.sem("s_o_summed")
        o_hi_done, o_lo_done = s.sem("s_o_hi_done"), s.sem("s_o_lo_done")
        o_stored = s.sems("s_o_stored", 4)

        def group_no(n, g):
            i, h = n // 2, n % 2
            return 2 * GROUPS_BEFORE[i] + h * len(turn_groups(i)) + g

        def slot(n, j):
            chunks = [] if n is None else [("chunk", (c,) + kc) for c, kc in enumerate(score_chunks(n // 2))]
            groups = [] if j is None else [("group", x) for x in enumerate(turn_groups(j // 2))]
            return interleave(chunks, groups) if chunks else groups

        def run(eng, unit, flush):
            unit(0, 0, 0, True)
            unit(0, 1, 1, False)
            with eng.Fori(1, UNITS // 2) as v:
                unit(v, 0, v * 2, False)
                unit(v, 1, v * 2 + 1, False)
            flush(UNITS - 1)

        with nc.Block() as block:
            @block.sync
            def _(sp):
                sp.wait_ge(prep, 2)
                ub.load(sp, 0, 0, q_dram, k_dram, v_dram, UNITS)
                ub.load(sp, 1, 1, q_dram, k_dram, v_dram, UNITS)
                for n, dst in enumerate(oa_early):
                    c, x = n // 2, n % 2
                    sp.dma_start(words(dst[:, :, :]), oa_dram[x, :, c * BANK:(c + 1) * BANK].rearrange(
                        "(k p) t -> p k t", p=P)).then_inc(early_loaded, 16)

                def stores(u):
                    for q in range(4):
                        sp.wait_ge(o_lo_done, u * 4 + (q + 2))
                        for x, src in enumerate((o_hi, o_lo)):
                            sp.dma_start(o_dram[x, bass.ds(u * P, P), q * 2 * P:(q + 1) * 2 * P],
                                         words(src[:, q, :])).then_inc(o_stored[q], 16)

                with sp.Fori(0, UNITS // 2 - 1) as v:
                    for p in range(2):
                        sp.wait_ge(pv_done, (v * 2 + (p + 1)) * 8 + 2)
                        ub.load(sp, v * 2 + (p + 2), p, q_dram, k_dram, v_dram, UNITS)
                        stores(v * 2 + p)
                for p in range(2):
                    stores(UNITS - 2 + p)
                for q in range(4):
                    sp.wait_ge(o_stored[q], 32 * (UNITS + 1))
                sp.wait_ge(early_loaded, 16 * len(oa_early))

            @block.tensor
            def _(pe):
                def score(p, u, n_item, c, k0, n):
                    i, h = n_item // 2, n_item % 2
                    no = chunk_no(i, h, c)
                    bank = S_BANKS[no % 4]
                    pe.wait_ge(split, u * CPU + (no + 1))
                    q = ub.q[p][h][:, i * P:(i + 1) * P]
                    last = c == len(score_chunks(i)) - 1
                    pe.matmul(bank[:, 0:n], q, ub.k[p][h][1][:, k0:k0 + n], start=True, stop=False)
                    mm = pe.matmul(bank[:, 0:n], q, ub.k[p][h][0][:, k0:k0 + n], start=False, stop=not last)
                    if last:
                        mm = pe.matmul(bank[:, n - P:n], ident_r[:, :], mask_r[:, :], start=False, stop=True)
                    mm.then_inc(scored, 1)

                def turn(u, n_item, g, tiles):
                    if g == 0:
                        pe.wait_ge(taken, u * ITEMS + (n_item + 1))
                    no = group_no(n_item, g)
                    pe.wait_ge(at_lo_done, u * GPU + (no + 1))
                    for x, t in enumerate(tiles):
                        mm = pe.transpose(T_BANKS[no % 2][:, x * P:(x + 1) * P],
                                          take[:, n_item % RING, key_col(t):key_col(t) + P], ident[:, :])
                    mm.then_inc(turned, 1)

                def value_tile(p, u, pair, h, t):
                    last, last_item = 2 * pair + 2, 4 * pair + 2 + h
                    if t == 0:
                        pe.wait_ge(at_lo_done, u * GPU + (2 + group_no(last_item, len(turn_groups(2 * pair + 1)) - 1) + 1))
                        pe.wait_ge(o_summed, u * 4 + (pair + 1))
                    q0 = P if t == last else 0
                    w = ub.v[p][:, t, h * P:(h + 1) * P]
                    o = PV_BANKS[h][:, q0:2 * P]
                    pe.matmul(o, w, at_lo[:, h, t, q0:2 * P], start=(t == 0), stop=False)
                    mm = pe.matmul(o, w, at_hi[:, h, t, q0:2 * P], start=False, stop=(t == last))
                    if t == last:
                        mm.then_inc(pv_done, 1)

                def step(p, u, n, lp, lu, j):
                    due = None
                    if j is not None and j % 4 == 3:
                        due = (lp, lu, j // 4, 0)
                    elif j is not None and j % 4 == 0 and j > 0:
                        due = (lp, lu, j // 4 - 1, 1)
                    elif j == 0 and not (isinstance(lu, int) and lu == 0):
                        due = (1 - lp, lu - 1, 3, 1)
                    n_t, done = 2 * due[2] + 3 if due else 0, 0
                    items = slot(n, j)
                    for x_no, (kind, x) in enumerate(items):
                        if kind == "chunk":
                            score(p, u, n, *x)
                        else:
                            turn(lu, j, *x)
                        upto = max(0, 2 * (x_no + 1) - len(items)) * n_t // len(items)
                        for t in range(done, upto):
                            value_tile(*due, t)
                        done = upto

                def unit(v, p, u, first):
                    pe.wait_ge(ub.qk_loaded[p], (v + 1) * (16 * ub.QK_LOADS))
                    for n in range(ITEMS):
                        if n == LAG:
                            pe.wait_ge(ub.v_loaded[p], (v + 1) * (16 * ub.V_LOADS))
                        if n >= LAG:
                            step(p, u, n, p, u, n - LAG)
                        elif first:
                            step(p, u, n, p, u, None)
                        else:
                            step(p, u, n, 1 - p, u - 1, ITEMS - LAG + n)

                def flush(u):
                    for j in range(ITEMS - LAG, ITEMS):
                        step(0, 0, None, u % 2, u, j)
                    for t in range(KEY_TILES):
                        value_tile(u % 2, u, 3, 1, t)

                run(pe, unit, flush)

            @block.scalar
            def _(act):
                def sigmoids(u, n_item, c, k0, n):
                    i, h = n_item // 2, n_item % 2
                    no = chunk_no(i, h, c)
                    act.wait_ge(scored, u * CPU + (no + 1))
                    act.activation(leave[:, n_item % RING, k0:k0 + n], S_BANKS[no % 4][:, 0:n], ACT.Sigmoid,
                                   scale=-SCALE)
                    act.activation(take[:, n_item % RING, k0:k0 + n], S_BANKS[no % 4][:, 0:n], ACT.Sigmoid,
                                   scale=SCALE).then_inc(split, 1)

                def high(u, n_item, g, tiles):
                    i, h = n_item // 2, n_item % 2
                    q0, no, m = (i % 2) * P, group_no(n_item, g), len(tiles)
                    if g == 0 and i % 2 == 0:
                        act.wait_ge(pv_done, (u * 4 + i // 2) * 2 + (h + 1))
                    act.wait_ge(turned, u * GPU + (no + 1))
                    act.activation(at_hi[:, h, tiles[0]:tiles[0] + m, q0:q0 + P],
                                   T_BANKS[no % 2][:, 0:m * P].rearrange("p (t c) -> p t c", c=P),
                                   ACT.Copy).then_inc(at_hi_done, 1)

                def out_low(u, s_):
                    act.wait_ge(pv_done, (u * 4 + s_) * 2 + 4)
                    act.wait_ge(o_summed, u * 4 + (s_ + 1))
                    act.activation(o_low[0:HD, :], PV_BANKS[0][HD:P, 0:2 * P], ACT.Copy)
                    act.activation(o_low[HD:P, :], PV_BANKS[1][0:HD, 0:2 * P], ACT.Copy).then_inc(o_low_done, 1)

                def out_high(u, s_):
                    act.wait_ge(o_summed, u * 4 + (s_ + 2))
                    act.wait_ge(o_stored[s_], u * 32 + 32)
                    act.activation(o_hi[:, s_, :], o_sum[:, :], ACT.Copy).then_inc(o_hi_done, 1)

                def step(u, n, lu, j):
                    for kind, x in slot(n, j):
                        if kind == "chunk":
                            sigmoids(u, n, *x)
                        else:
                            high(lu, j, *x)
                    if j is not None and j % 4 == 1 and j > 1:
                        out_low(lu, j // 4 - 1)
                    if j is not None and j % 4 == 3 and j > 3:
                        out_high(lu, j // 4 - 1)

                def unit(v, p, u, first):
                    for n in range(ITEMS):
                        step(u, n, *((u, n - LAG) if n >= LAG else (u, None) if first else (u - 1, ITEMS - LAG + n)))
                        if n == LAG + 1 and not first:
                            out_low(u - 1, 3)
                        if n == LAG + 3 and not first:
                            out_high(u - 1, 3)

                def flush(u):
                    for j in range(ITEMS - LAG, ITEMS):
                        step(u, None, u, j)
                    out_low(u, 3)
                    out_high(u, 3)

                for q in range(4):
                    act.sem_inc(o_stored[q], 32)
                act.sem_inc(split, 4)
                act.sem_inc(pv_done, 2)
                run(act, unit, flush)

            @block.vector
            def _(dve):
                def scan(u, n_item):
                    i, h = n_item // 2, n_item % 2
                    w = META + P * (i + 1)
                    no = chunk_no(i, h, len(score_chunks(i)) - 1)
                    dve.wait_ge(split, u * CPU + (no + 5))
                    r = leave[:, n_item % RING, w - 1::-1] if w == L else leave[:, n_item % RING, 0:w][:, ::-1]
                    dve.tensor_tensor_scan(r, r, one[:, 0:w], 1.0, ALU.mult, ALU.mult).then_inc(scanned, 1)

                def low(u, n_item):
                    i, h = n_item // 2, n_item % 2
                    q0 = (i % 2) * P
                    for g, tiles in enumerate(turn_groups(i)):
                        no, m = group_no(n_item, g), len(tiles)
                        dve.wait_ge(at_hi_done, u * GPU + (no + 1))
                        dve.tensor_tensor(at_lo[:, h, tiles[0]:tiles[0] + m, q0:q0 + P],
                                          T_BANKS[no % 2][:, 0:m * P].rearrange("p (t c) -> p t c", c=P),
                                          at_hi[:, h, tiles[0]:tiles[0] + m, q0:q0 + P],
                                          ALU.subtract).then_inc(at_lo_done, 1)

                def out_sum(u, s_):
                    dve.wait_ge(o_low_done, u * 4 + (s_ + 1))
                    dve.wait_ge(o_lo_done, u * 4 + (s_ + 1))
                    for h in range(2):
                        a, b = h * HD, (h + 1) * HD
                        last = dve.tensor_tensor(o_sum[a:b, :], PV_BANKS[h][a:b, 0:2 * P], o_low[a:b, :], ALU.add)
                    last.then_inc(o_summed, 1)

                def out_lo(u, s_):
                    dve.wait_ge(o_hi_done, u * 4 + (s_ + 1))
                    dve.wait_ge(o_stored[s_], u * 32 + 32)
                    dve.tensor_tensor(o_lo[:, s_, :], o_sum[:, :], o_hi[:, s_, :], ALU.subtract).then_inc(o_lo_done, 1)

                def lagged(u, n):
                    low(u, n)
                    if n % 4 == 1 and n > 1:
                        out_sum(u, n // 4 - 1)
                    if n % 4 == 3 and n > 3:
                        out_lo(u, n // 4 - 1)

                def unit(v, p, u, first):
                    for n in range(ITEMS):
                        if n >= LAG:
                            lagged(u, n - LAG)
                        elif not first:
                            lagged(u - 1, ITEMS - LAG + n)
                        scan(u, n)
                        if n == LAG + 1 and not first:
                            out_sum(u - 1, 3)
                        if n == LAG + 3 and not first:
                            out_lo(u - 1, 3)

                def flush(u):
                    for n in range(ITEMS - LAG, ITEMS):
                        lagged(u, n)
                    out_sum(u, 3)
                    out_lo(u, 3)

                ub.zero_meta(dve, prep)
                dve.memset(one[:, :], 1.0).then_inc(prep, 1)
                dve.wait_ge(prep, 3)
                dve.sem_inc(at_lo_done, 2)
                dve.sem_inc(o_summed, 1)
                dve.sem_inc(o_lo_done, 1)
                run(dve, unit, flush)

            @block.gpsimd
            def _(pool):
                with pool.Fori(0, UNITS) as u:
                    for n in range(ITEMS):
                        w, r = META + P * (n // 2 + 1), n % RING
                        pool.wait_ge(scanned, u * ITEMS + (n + 1))
                        pool.tensor_tensor(take[:, r, 0:w - 1], take[:, r, 0:w - 1], leave[:, r, 1:w],
                                           ALU.mult).then_inc(taken, 1)


def stage_constants(nc, ident, ident_r, causal_r, strict_r):
    with Scratch(nc) as s:
        masks = s.sb("c_masks", [P, 2, P])
        zeroed, selected, done = s.sem("c_zeroed"), s.sem("c_selected"), s.sem("c_done")
        with nc.Block() as block:
            @block.gpsimd
            def _(pool):
                pool.memset(ident[:, :], 0.0).then_inc(zeroed, 1)
                pool.memset(masks[:, :, :], 0.0).then_inc(zeroed, 1)
                pool.wait_ge(zeroed, 2)
                pool.affine_select(out=ident[:, :], in_=ident[:, :], pattern=[[-1, P]], compare_op=ALU.not_equal,
                                   fill=1.0, base=0, channel_multiplier=1).then_inc(selected, 1)
                for m in range(2):
                    pool.affine_select(out=masks[:, m, :], in_=masks[:, m, :], pattern=[[-1, P]],
                                       compare_op=ALU.is_ge, fill=NEG, base=-m,
                                       channel_multiplier=1).then_inc(selected, 1)

            @block.vector
            def _(dve):
                dve.wait_ge(selected, 3)
                dve.tensor_copy(ident_r[:, :], ident[:, :]).then_inc(done, 1)
                dve.tensor_copy(causal_r[:, :], masks[:, 0, :]).then_inc(done, 1)
                dve.tensor_copy(strict_r[:, :], masks[:, 1, :]).then_inc(done, 1)
                dve.wait_ge(done, 3)


def stage_merge(nc, ps, w_out_a, w_out_b, w_out, o_a, ob_dram, gate_dram, oa_dram, m_dram):
    CH = 2
    VP = KT // 2
    with Scratch(nc) as s:
        o_b = [s.sb(f"m_ob{x}", [P, KT, SEQ], F32R) for x in range(2)]
        w_raw = [s.sb(f"m_w_raw{p}", [P, KT, P]) for p in range(2)]
        w_hi = [s.sb(f"m_w_hi{p}", [P, KT, P], F32R) for p in range(2)]
        w_lo = [s.sb(f"m_w_lo{p}", [P, KT, P], F32R) for p in range(2)]
        gates = [s.sb(f"m_gate{p}", [P, SEQ]) for p in range(2)]
        part = s.sb("m_part", [P, KT, SEQ])
        out_raw = s.sb("m_out_raw", [P, D])
        m_hi, m_lo = s.sb("m_hi", [P, CH, BANK], F32R), s.sb("m_lo", [P, CH, BANK], F32R)
        a_loaded, b_loaded = s.sem("m_a_loaded"), s.sem("m_b_loaded")
        w_loaded, g_loaded = s.sems("m_w_loaded", 2), s.sems("m_g_loaded", 2)
        w_hi_done, w_lo_done = s.sem("m_w_hi_done"), s.sem("m_w_lo_done")
        mm_done, gated, added = s.sem("m_mm_done"), s.sem("m_gated"), s.sem("m_added")
        hi_done, lo_done, stored = s.sem("m_hi_done"), s.sem("m_lo_done"), s.sems("m_stored", CH)
        out_loaded, out_hi_done, out_lo_done = s.sem("m_out_loaded"), s.sem("m_out_hi_done"), s.sem("m_out_lo_done")
        wv = [w.rearrange("o (k p) n -> p (o k) n", p=P) for w in (w_out_a, w_out_b)]
        out_v = w_out.rearrange("o (k p) n -> p (o k) n", p=P)
        oa_v, ob_v = (x.rearrange("x (k p) t -> x p k t", p=P) for x in (oa_dram, ob_dram))

        def tile_of(x, k, c):
            return x[:, bass.ds(k, 1), c * BANK:(c + 1) * BANK].rearrange("p o c -> p (o c)")

        def col(x, k):
            return x[:, bass.ds(k, 1), :].rearrange("p o c -> p (o c)")

        with nc.Block() as block:
            @block.sync
            def _(sp):
                def load_w(b, u, p):
                    sp.dma_start(w_raw[p][:, :, :], wv[b][:, :, bass.ds(u * P, P)]).then_inc(w_loaded[p], 16)

                def load_g(b, u, p):
                    sp.dma_start(gates[p][:, :], gate_dram[b, bass.ds(u * P, P), :]).then_inc(g_loaded[p], 16)

                def body(b, v, last):
                    for p in range(2):
                        u, n = v * 2 + p, v * 2 + (p + KT * b)
                        ahead = (b, u + 2) if not last else (1, p) if b == 0 else None
                        if ahead:
                            sp.wait_ge(w_lo_done, n + 1)
                            load_w(*ahead, p)
                        if b == 0:
                            for x in range(2):
                                sp.dma_start(words(o_b[x][:, bass.ds(u, 1), :]),
                                             ob_v[x, :, bass.ds(u, 1), :]).then_inc(b_loaded, 16)
                            sp.wait_ge(gated, n * CH + (2 * CH + CH))
                        else:
                            for c in range(CH):
                                sp.wait_ge(lo_done, u * CH + (c + 1))
                                for x, src in enumerate((m_hi, m_lo)):
                                    sp.dma_start(m_dram[x, bass.ds(u * P, P), c * BANK:(c + 1) * BANK],
                                                 words(src[:, c, :])).then_inc(stored[c], 16)
                            sp.wait_ge(added, u * CH + CH)
                        if ahead:
                            load_g(*ahead, p)
                        if b == 1 and not (last and p == 1):
                            sp.wait_ge(out_lo_done, u * 2 + 2)
                            load_out(u + 1)

                def load_out(u):
                    sp.dma_start(out_raw[:, :], out_v[:, bass.ds(u, 1), :]).then_inc(out_loaded, 16)

                load_w(0, 0, 0)
                load_g(0, 0, 0)
                load_w(0, 1, 1)
                sp.dma_start(words(o_a[1][1][:, :, :]), oa_v[1, :, :, BANK:SEQ]).then_inc(a_loaded, 16)
                load_g(0, 1, 1)
                for b in range(2):
                    with sp.Fori(0, VP - 1) as v:
                        body(b, v, False)
                    body(b, VP - 1, True)
                    if b == 0:
                        load_out(0)
                for c in range(CH):
                    sp.wait_ge(stored[c], 32 * (KT + 1))

            @block.scalar
            def _(act):
                def split_w(v, p, b):
                    act.wait_ge(w_loaded[p], v * 16 + (VP * b + 1) * 16)
                    act.wait_ge(mm_done, v * 2 * CH + (p + KT * b) * CH + CH)
                    act.activation(w_hi[p][:, :, :], w_raw[p][:, :, :], ACT.Copy).then_inc(w_hi_done, 1)

                def body(b, v, last):
                    for p in range(2):
                        if p == 0:
                            split_w(v, 1, b)
                        elif not last:
                            split_w(v + 1, 0, b)
                        if b == 1:
                            u = v * 2 + p
                            act.wait_ge(out_loaded, u * 16 + 16)
                            act.wait_ge(mm_done, KT * CH + 2 * CH)
                            for half in range(2):
                                act.activation(col(o_a[1][half], u), out_raw[:, half * BANK:(half + 1) * BANK],
                                               ACT.Copy).then_inc(out_hi_done, 1)
                            for c in range(CH):
                                act.wait_ge(added, u * CH + (c + 1))
                                act.wait_ge(stored[c], u * 32 + 32)
                                act.activation(m_hi[:, c, :], tile_of(part, u, c), ACT.Copy).then_inc(hi_done, 1)

                act.sem_inc(mm_done, 2 * CH)
                for c in range(CH):
                    act.sem_inc(stored[c], 32)
                split_w(0, 0, 0)
                with act.Fori(0, VP) as v:
                    body(0, v, False)
                with act.Fori(0, VP - 1) as v:
                    body(1, v, False)
                body(1, VP - 1, True)

            @block.vector
            def _(dve):
                def split_w(v, p, b):
                    dve.wait_ge(w_hi_done, v * 2 + (p + KT * b + 1))
                    dve.tensor_tensor(w_lo[p][:, :, :], w_raw[p][:, :, :], w_hi[p][:, :, :],
                                      ALU.subtract).then_inc(w_lo_done, 1)

                def body(b, v, last):
                    for p in range(2):
                        u, n = v * 2 + p, v * 2 + (p + KT * b)
                        if p == 0:
                            split_w(v, 1, b)
                        elif not last:
                            split_w(v + 1, 0, b)
                        if b == 1:
                            for half in range(2):
                                dve.wait_ge(out_hi_done, u * 2 + (half + 1))
                                dve.tensor_tensor(col(o_a[0][half], u), out_raw[:, half * BANK:(half + 1) * BANK],
                                                  col(o_a[1][half], u), ALU.subtract).then_inc(out_lo_done, 1)
                        dve.wait_ge(g_loaded[p], v * 16 + (VP * b + 1) * 16)
                        for c in range(CH):
                            dve.wait_ge(mm_done, n * CH + (2 * CH + c + 1))
                            gate = gates[p][:, c * BANK:(c + 1) * BANK]
                            if b == 0:
                                dve.tensor_tensor(tile_of(part, u, c), ps[2 * p + c][:, :], gate, ALU.mult).then_inc(gated, 1)
                            else:
                                dve.tensor_tensor(gate, ps[2 * p + c][:, :], gate, ALU.mult).then_inc(gated, 1)
                                dve.wait_ge(gated, n * CH + (2 * CH + c + 1))
                                dve.tensor_tensor(tile_of(part, u, c), tile_of(part, u, c), gate,
                                                  ALU.add).then_inc(added, 1)
                        if b == 1:
                            for c in range(CH):
                                dve.wait_ge(hi_done, u * CH + (c + 1))
                                dve.wait_ge(stored[c], u * 32 + 32)
                                dve.tensor_tensor(m_lo[:, c, :], tile_of(part, u, c), m_hi[:, c, :],
                                                  ALU.subtract).then_inc(lo_done, 1)

                dve.sem_inc(gated, 2 * CH)
                split_w(0, 0, 0)
                with dve.Fori(0, VP) as v:
                    body(0, v, False)
                with dve.Fori(0, VP - 1) as v:
                    body(1, v, False)
                body(1, VP - 1, True)

            @block.tensor
            def _(pe):
                for b in range(2):
                    if b == 1:
                        pe.wait_ge(b_loaded, 2 * KT * 16)
                    with pe.Fori(0, VP) as v:
                        for p in range(2):
                            n = v * 2 + (p + KT * b)
                            pe.wait_ge(w_lo_done, n + 1)
                            for c in range(CH):
                                if b == 0 and c == 1:
                                    pe.wait_ge(a_loaded, 16)
                                pe.wait_ge(gated, n * CH + (c + 1))
                                xs = ([(lambda k, x=x: o_a[c][x][:, k, :]) for x in range(2)] if b == 0 else
                                      [(lambda k, x=x: o_b[x][:, k, c * BANK:(c + 1) * BANK]) for x in range(2)])
                                product3(pe, ps[2 * p + c][:, :], lambda k: w_hi[p][:, k, :],
                                         lambda k: w_lo[p][:, k, :], xs[0], xs[1], range(KT)).then_inc(mm_done, 1)


def stage_residual(nc, ps, x, w_hi, w_lo, mlp_g, m_dram, ident, h2, hm_hi, hm_lo):
    with Scratch(nc) as s:
        m = [[s.sb(f"r_m{p}{q}", [P, KT, P], F32R) for q in range(2)] for p in range(2)]
        sq = s.sb("r_sq", [P, D])
        ssum, rstd = s.sb("r_ssum", [P, 2]), s.sb("r_rstd", [P, 2])
        y = s.sb("r_y", [P, 2, D])
        g = s.sb("r_g", [P, KT])
        x_loaded, m_loaded, g_loaded = s.sems("r_x_loaded", 2), s.sems("r_m_loaded", 2), s.sem("r_g_loaded")
        mm_done, added, squared, scaled = s.sem("r_mm_done"), s.sem("r_added"), s.sem("r_squared"), s.sem("r_scaled")
        mean_eps, rooted, inverted = s.sem("r_mean_eps"), s.sem("r_rooted"), s.sem("r_inverted")
        turned, hi_done, lo_done = s.sem("r_turned"), s.sem("r_hi_done"), s.sem("r_lo_done")
        mv = m_dram.rearrange("x (k p) t -> x p k t", p=P)
        xv = x[0].rearrange("(t p) c -> p t c", p=P)
        TP = QT // 2
        with nc.Block() as block:
            @block.sync
            def _(sp):
                def load_m(t, p):
                    for q in range(2):
                        sp.dma_start(words(m[p][q][:, :, :]), mv[q, :, :, bass.ds(t * P, P)]).then_inc(m_loaded[p], 16)

                def load_x(t, p):
                    sp.dma_start(h2[:, bass.ds(t, 1), :], xv[:, bass.ds(t, 1), :]).then_inc(x_loaded[p], 16)

                load_m(0, 0)
                load_x(0, 0)
                sp.dma_start(g[:, :], mlp_g.rearrange("o (k p) -> p (o k)", p=P),
                             allow_slow_non_contiguous=True).then_inc(g_loaded, 16)
                load_m(1, 1)
                load_x(1, 1)
                with sp.Fori(0, TP - 1) as v:
                    for p in range(2):
                        sp.wait_ge(mm_done, (v * 2 + p) * 2 + 2)
                        load_m(v * 2 + (p + 2), p)
                        sp.wait_ge(added, (v * 2 + p) * 2 + 2)
                        load_x(v * 2 + (p + 2), p)

            @block.scalar
            def _(act):
                def square(t, p):
                    act.wait_ge(added, t * 2 + 2)
                    act.activation(sq[:, :], h2[:, bass.ds(t, 1), :].rearrange("p o c -> p (o c)"), ACT.Square,
                                   accum_out=ssum[:, p:p + 1]).then_inc(squared, 1)
                    act.wait_ge(mean_eps, t + 1)
                    act.activation(rstd[:, p:p + 1], ssum[:, p:p + 1], ACT.Sqrt).then_inc(rooted, 1)

                def high(t):
                    for k in range(KT):
                        if k % 4 == 0:
                            act.wait_ge(turned, t * 2 + (k // 4 + 1))
                        act.activation(hm_hi[:, k, bass.ds(t * P, P)], ps[4 + k // 4][:, (k % 4) * P:(k % 4 + 1) * P],
                                       ACT.Copy, scale=g[:, k:k + 1]).then_inc(hi_done, 1)

                act.wait_ge(g_loaded, 16)
                square(0, 0)
                with act.Fori(0, TP - 1) as v:
                    square(v * 2 + 1, 1)
                    high(v * 2)
                    square(v * 2 + 2, 0)
                    high(v * 2 + 1)
                square(QT - 1, 1)
                high(QT - 2)
                high(QT - 1)

            @block.vector
            def _(dve):
                def add(v, t, p):
                    dve.wait_ge(x_loaded[p], v * 16 + 16)
                    for half in range(2):
                        dve.wait_ge(mm_done, t * 2 + (half + 1))
                        dst = h2[:, bass.ds(t, 1), half * BANK:(half + 1) * BANK].rearrange("p o c -> p (o c)")
                        dve.tensor_tensor(dst, ps[half][:, :], dst, ALU.add).then_inc(added, 1)

                def scale(t, p):
                    dve.wait_ge(squared, t + 1)
                    dve.tensor_scalar(ssum[:, p:p + 1], ssum[:, p:p + 1], 1.0 / D, EPS, ALU.mult, ALU.add).then_inc(mean_eps, 1)
                    dve.wait_ge(rooted, t + 1)
                    dve.reciprocal(rstd[:, p:p + 1], rstd[:, p:p + 1]).then_inc(inverted, 1)
                    dve.wait_ge(inverted, t + 1)
                    dve.tensor_scalar(y[:, p, :], h2[:, bass.ds(t, 1), :].rearrange("p o c -> p (o c)"),
                                      rstd[:, p:p + 1], None, ALU.mult).then_inc(scaled, 1)

                def low(t):
                    for k in range(KT):
                        if k % 4 == 0:
                            dve.wait_ge(hi_done, t * KT + (k + 4))
                        dve.scalar_tensor_tensor(out=hm_lo[:, k, bass.ds(t * P, P)],
                                                 in0=ps[4 + k // 4][:, (k % 4) * P:(k % 4 + 1) * P],
                                                 scalar=g[:, k:k + 1], in1=hm_hi[:, k, bass.ds(t * P, P)],
                                                 op0=ALU.mult, op1=ALU.subtract).then_inc(lo_done, 1)

                dve.wait_ge(g_loaded, 16)
                add(0, 0, 0)
                scale(0, 0)
                with dve.Fori(0, TP - 1) as v:
                    add(v, v * 2 + 1, 1)
                    scale(v * 2 + 1, 1)
                    low(v * 2)
                    add(v + 1, v * 2 + 2, 0)
                    scale(v * 2 + 2, 0)
                    low(v * 2 + 1)
                add(TP - 1, QT - 1, 1)
                scale(QT - 1, 1)
                low(QT - 2)
                low(QT - 1)

            @block.tensor
            def _(pe):
                def product(v, t, p, first):
                    pe.wait_ge(m_loaded[p], (v + 1) * 32)
                    for half in range(2):
                        if not first:
                            pe.wait_ge(added, t * 2 - 2 + (half + 1))
                        product3(pe, ps[half][:, :], lambda k: m[p][0][:, k, :], lambda k: m[p][1][:, k, :],
                                 lambda k: w_hi[half][:, k, :],
                                 lambda k: w_lo[half][:, k, :], range(KT)).then_inc(mm_done, 1)

                def turn(t, p, first=False):
                    pe.wait_ge(scaled, t + 1)
                    if not first:
                        pe.wait_ge(lo_done, t * KT)
                    for k in range(KT):
                        mm = pe.transpose(ps[4 + k // 4][:, (k % 4) * P:(k % 4 + 1) * P], y[:, p, k * P:(k + 1) * P],
                                          ident[:, :])
                        if k % 4 == 3:
                            mm.then_inc(turned, 1)

                product(0, 0, 0, True)
                product(0, 1, 1, False)
                turn(0, 0, True)
                with pe.Fori(1, TP) as v:
                    product(v, v * 2, 0, False)
                    turn(v * 2 - 1, 1)
                    product(v, v * 2 + 1, 1, False)
                    turn(v * 2, 0)
                turn(QT - 1, 1)


def stage_mlp(nc, ps, w_up, w_down, final_g, h2, hm_hi, hm_lo, wide, out):
    FT = KT // 2
    GROUPS = D_FF // (FT * P)
    CH = 2
    with Scratch(nc) as s:
        u_raw = [s.sb(f"f_u_raw{i}", [P, KT, P]) for i in range(2)]
        u_hi = [s.sb(f"f_u_hi{i}", [P, KT, P], F32R) for i in range(2)]
        u_lo = [s.sb(f"f_u_lo{i}", [P, KT, P], F32R) for i in range(2)]
        d_raw = s.sb("f_d_raw", [P, FT, BANK])
        d_hi, d_lo, r_hi, r_lo = [[w[:, i * FT:(i + 1) * FT, :] for i in range(2)] for w in wide]
        relu = s.sb("f_relu", [P, 2, BANK])
        sq = s.sb("f_sq", [P, 2, BANK])
        u_loaded, d_loaded = s.sems("f_u_loaded", 2), s.sem("f_d_loaded")
        u_hi_done, u_lo_done, d_hi_done, d_lo_done = (s.sem("f_u_hi_done"), s.sem("f_u_lo_done"),
                                                      s.sem("f_d_hi_done"), s.sem("f_d_lo_done"))
        up_done, relued, sqd, r_hi_done, r_lo_done = (s.sem("f_up_done"), s.sem("f_relued"), s.sem("f_sqd"),
                                                      s.sem("f_r_hi_done"), s.sem("f_r_lo_done"))
        down_done, added = s.sem("f_down_done"), s.sem("f_added")
        gain, squares = u_raw[0][:, :, :].rearrange("p k c -> p (k c)"), relu[:, :, :].rearrange("p n c -> p (n c)")
        ssum, rstd = s.sb("f_ssum", [P, QT]), s.sb("f_rstd", [P, QT])
        g_loaded, squared, normed, stored = s.sem("f_g_loaded"), s.sem("f_squared"), s.sem("f_normed"), s.sem("f_stored")
        mean_eps, rooted, inverted = s.sem("f_mean_eps"), s.sem("f_rooted"), s.sem("f_inverted")
        uv = w_up.rearrange("o (k p) n -> p (o k) n", p=P)
        dv = w_down.rearrange("o (g k p) n -> (o g) p k n", p=P, k=FT)
        UC = FT * CH
        DC = QT * 2
        with nc.Block() as block:
            @block.sync
            def _(sp):
                def load_u(g, f):
                    sp.dma_start(u_raw[f % 2][:, :, :], uv[:, :, bass.ds((g * FT + f) * P, P)]).then_inc(u_loaded[f % 2], 16)

                def body(g, last):
                    for f in range(FT):
                        if f < FT - 2 or not last:
                            sp.wait_ge(u_lo_done, g * FT + (f + 1))
                            load_u(g + 1 if f >= FT - 2 else g, (f + 2) % FT)
                        if f == 0:
                            sp.wait_ge(d_lo_done, g * 2 + 2)
                            sp.dma_start(d_raw[:, :, :], dv[g, :, :, 0:BANK]).then_inc(d_loaded, 16)
                        if f == 2:
                            sp.wait_ge(d_lo_done, g * 2 + 3)
                            sp.dma_start(d_raw[:, :, :], dv[g, :, :, BANK:D]).then_inc(d_loaded, 16)
                        if f == 2 and last:
                            sp.wait_ge(u_lo_done, g * FT + 3)
                            sp.dma_start(gain, final_g.rearrange("(o c) -> o c", o=1).broadcast_to([P, D])).then_inc(g_loaded, 16)

                load_u(0, 0)
                load_u(0, 1)
                with sp.Fori(0, GROUPS - 1) as g:
                    body(g, False)
                body(GROUPS - 1, True)
                for t in range(QT):
                    sp.wait_ge(normed, t + 1)
                    sp.dma_start(out[0, t * P:(t + 1) * P, :], h2[:, t, :]).then_inc(stored, 16)
                sp.wait_ge(stored, 16 * QT)

            @block.scalar
            def _(act):
                def split_u(g, f):
                    act.wait_ge(u_loaded[f % 2], (g * 2 + (f // 2 + 1)) * 16)
                    act.wait_ge(up_done, (g * FT + f) * CH + 2)
                    act.activation(u_hi[f % 2][:, :, :], u_raw[f % 2][:, :, :], ACT.Copy).then_inc(u_hi_done, 1)

                def split_d(g, half):
                    act.wait_ge(d_loaded, (g * 2 + (half + 1)) * 16)
                    act.wait_ge(down_done, (g + 1) * DC)
                    act.activation(d_hi[half][:, :, :], d_raw[:, :, :], ACT.Copy).then_inc(d_hi_done, 1)

                def rectify(g, n):
                    act.wait_ge(up_done, g * UC + (n + 5))
                    act.wait_ge(sqd, g * UC + (n + 1))
                    act.activation(relu[:, n % 2, :], ps[n % 4][:, :], ACT.Relu).then_inc(relued, 1)

                def high(g, n):
                    f, c = n // CH, n % CH
                    act.wait_ge(sqd, g * UC + (n + 3))
                    act.activation(r_hi[c][:, f, :], sq[:, n % 2, :], ACT.Copy).then_inc(r_hi_done, 1)

                act.sem_inc(up_done, 4)
                act.sem_inc(down_done, DC)
                act.sem_inc(sqd, 2)

                def body(g):
                    split_u(g, 0)
                    split_u(g, 1)
                    for n in range(UC):
                        rectify(g, n)
                        high(g, n)
                        if n in (1, 3):
                            split_u(g, n // 2 + 2)
                        if n in (2, 5):
                            split_d(g, n // 3)

                with act.Fori(0, GROUPS) as g:
                    body(g)
                for t in range(QT):
                    act.wait_ge(added, (GROUPS - 1) * DC + 2 * t + 6)
                    if t:
                        act.wait_ge(squared, t)
                    act.activation(squares, h2[:, t, :], ACT.Square, accum_out=ssum[:, t:t + 1]).then_inc(squared, 1)
                    act.wait_ge(mean_eps, t + 1)
                    act.activation(rstd[:, t:t + 1], ssum[:, t:t + 1], ACT.Sqrt).then_inc(rooted, 1)

            @block.vector
            def _(dve):
                def split_u(g, f):
                    dve.wait_ge(u_hi_done, g * FT + (f + 1))
                    dve.tensor_tensor(u_lo[f % 2][:, :, :], u_raw[f % 2][:, :, :], u_hi[f % 2][:, :, :],
                                      ALU.subtract).then_inc(u_lo_done, 1)

                def split_d(g, half):
                    dve.wait_ge(d_hi_done, g * 2 + (half + 1))
                    dve.tensor_tensor(d_lo[half][:, :, :], d_raw[:, :, :], d_hi[half][:, :, :],
                                      ALU.subtract).then_inc(d_lo_done, 1)

                def square(g, n):
                    dve.wait_ge(relued, g * UC + (n + 1))
                    dve.scalar_tensor_tensor(out=sq[:, n % 2, :], in0=ps[n % 4][:, :], scalar=0.0,
                                             in1=relu[:, n % 2, :], op0=ALU.max, op1=ALU.mult).then_inc(sqd, 1)

                def low(g, n):
                    f, c = n // CH, n % CH
                    dve.wait_ge(r_hi_done, g * UC + (n + 1))
                    dve.tensor_tensor(r_lo[c][:, f, :], sq[:, n % 2, :],
                                      r_hi[c][:, f, :], ALU.subtract).then_inc(r_lo_done, 1)

                def add(g, n):
                    t, half = n // 2, n % 2
                    dve.wait_ge(down_done, g * DC + (DC + n + 1))
                    dst = h2[:, t, half * BANK:(half + 1) * BANK]
                    dve.tensor_tensor(dst, ps[4 + n % 4][:, :], dst, ALU.add).then_inc(added, 1)

                dve.sem_inc(added, 4)
                dve.sem_inc(d_lo_done, 2)
                def norm(t):
                    dve.wait_ge(squared, t + 1)
                    dve.tensor_scalar(ssum[:, t:t + 1], ssum[:, t:t + 1], 1.0 / D, EPS, ALU.mult, ALU.add).then_inc(mean_eps, 1)
                    dve.wait_ge(rooted, t + 1)
                    dve.reciprocal(rstd[:, t:t + 1], rstd[:, t:t + 1]).then_inc(inverted, 1)
                    dve.wait_ge(inverted, t + 1)
                    dve.scalar_tensor_tensor(out=h2[:, t, :], in0=h2[:, t, :], scalar=rstd[:, t:t + 1], in1=gain,
                                             op0=ALU.mult, op1=ALU.mult).then_inc(normed, 1)

                def body(g, last):
                    split_u(g, 0)
                    split_u(g, 1)
                    for n in range(UC):
                        square(g, n)
                        low(g, n)
                        if n in (1, 3):
                            split_u(g, n // 2 + 2)
                        if n in (2, 5):
                            split_d(g, n // 3)
                    if last:
                        dve.wait_ge(g_loaded, 16)
                    for n in range(DC):
                        add(g, n)
                        if last and n % 2 and n > 1:
                            norm(n // 2 - 1)
                    if last:
                        norm(QT - 1)

                with dve.Fori(0, GROUPS - 1) as g:
                    body(g, False)
                body(GROUPS - 1, True)

            @block.tensor
            def _(pe):
                def body(g, first):
                    for n in range(UC):
                        f, c = n // CH, n % CH
                        if c == 0:
                            pe.wait_ge(u_lo_done, g * FT + (f + 1))
                        if not (first and n < 4):
                            pe.wait_ge(sqd, g * UC + (n - 1))
                        product3(pe, ps[n % 4][:, :], lambda k: u_hi[f % 2][:, k, :], lambda k: u_lo[f % 2][:, k, :],
                                 lambda k: hm_hi[:, k, c * BANK:(c + 1) * BANK],
                                 lambda k: hm_lo[:, k, c * BANK:(c + 1) * BANK], range(KT)).then_inc(up_done, 1)
                    for n in range(DC):
                        t, half = n // 2, n % 2
                        if n < 2:
                            pe.wait_ge(d_lo_done, g * 2 + (half + 3))
                        pe.wait_ge(added, g * DC + (n + 1))
                        for k in range(FT):
                            if n == 0:
                                pe.wait_ge(r_lo_done, g * UC + (k + 1) * CH)
                            x = lambda a: a[t * P // BANK][:, k, t * P % BANK:t * P % BANK + P]
                            o = ps[4 + n % 4][:, :]
                            pe.matmul(o, x(r_lo), d_hi[half][:, k, :], start=(k == 0), stop=False)
                            pe.matmul(o, x(r_hi), d_lo[half][:, k, :], start=False, stop=False)
                            mm = pe.matmul(o, x(r_hi), d_hi[half][:, k, :], start=False, stop=(k == FT - 1))
                        mm.then_inc(down_done, 1)

                body(0, True)
                with pe.Fori(1, GROUPS) as g:
                    body(g, False)


def layer(nc, a, cos, sin, out):
    with ExitStack() as keep:
        def sb(name, shape, dt=F32):
            return keep.enter_context(nc.sbuf_tensor(name, shape, dt))

        ps = [keep.enter_context(nc.psum_tensor(f"bank{i}", [P, BANK], F32)) for i in range(8)]
        ident, ident_r = sb("ident", [P, P]), sb("ident_r", [P, P], F32R)
        causal_r, strict_r = sb("causal_r", [P, P], F32R), sb("strict_r", [P, P], F32R)
        q_dram = [nc.dram_tensor(f"q_scratch{b}", (UNITS, 2, 2, HD, SEQ), F32).ap() for b in range(2)]
        k_dram = [nc.dram_tensor(f"k_scratch{b}", (UNITS, 2, 2, HD, L), F32).ap() for b in range(2)]
        v_dram = nc.dram_tensor("v_scratch", (2 * UNITS, L, 2 * P), F32).ap()
        o_dram = [nc.dram_tensor(f"o_scratch{b}", (2, D, SEQ), F32).ap() for b in range(2)]
        m_dram = nc.dram_tensor("m_scratch", (2, D, SEQ), F32).ap()
        gate_dram = nc.dram_tensor("gate_scratch", (2, D, SEQ), F32).ap()
        w_in = a["w_in"].rearrange("o k n -> (o k) n")

        stage_constants(nc, ident, ident_r, causal_r, strict_r)
        with Scratch(nc) as s:
            hn_hi, hn_lo = s.sb("hn_hi", [P, KT, L], F32R), s.sb("hn_lo", [P, KT, L], F32R)
            stage_norm(nc, ps, a["x"], a["meta_tokens"], a["norm_mix_g"], ident, hn_hi, hn_lo)

            def place_qk(b):
                def place(u, w, part, t0, n):
                    if w == 0:
                        return [(q_dram[b][u, h, part, :, t0 - META:t0 - META + n], h * HD, HD) for h in range(2)]
                    return [(k_dram[b][u, h, part, :, t0:t0 + n], h * HD, HD) for h in range(2)]
                return place

            def place_gate(u, w, part, t0, n):
                return [(gate_dram[w, bass.ds(u * P, P), t0 - META:t0 - META + n], 0, P)]

            stage_channels(nc, ps, "pa", w_in, (QA_COL, KA_COL), (Q_CHUNKS, K_CHUNKS), hn_hi, hn_lo,
                           (cos, sin), place_qk(0))
            stage_channels(nc, ps, "pb", w_in, (QB_COL, KB_COL), (Q_CHUNKS, K_CHUNKS), hn_hi, hn_lo,
                           None, place_qk(1))
            stage_channels(nc, ps, "pg", w_in, (GA_COL, GB_COL), (Q_CHUNKS, Q_CHUNKS), hn_hi, hn_lo,
                           None, place_gate, gate=True)
            stage_values(nc, ps, w_in, hn_hi, hn_lo, v_dram)
        stage_diff(nc, ps, q_dram[0], k_dram[0], v_dram, o_dram[0],
                   [a["lambda_q1"], a["lambda_k1"], a["lambda_q2"], a["lambda_k2"]], a["subln_g"],
                   ident, ident_r, causal_r)
        wide = [sb(f"wide{i}", [P, KT, BANK], F32R) for i in range(3)]
        stage_stick(nc, ps, q_dram[1], k_dram[1], v_dram, o_dram[1], ident, ident_r, strict_r, o_dram[0], wide)
        wide.append(sb("wide3", [P, KT, BANK], F32R))
        stage_merge(nc, ps, a["w_out_a"], a["w_out_b"], a["w_out"], [wide[0:2], wide[2:4]], o_dram[1], gate_dram,
                    o_dram[0], m_dram)
        h2 = sb("h2", [P, QT, D])
        with Scratch(nc) as s:
            hm_hi, hm_lo = s.sb("hm_hi", [P, KT, SEQ], F32R), s.sb("hm_lo", [P, KT, SEQ], F32R)
            stage_residual(nc, ps, a["x"], wide[2:4], wide[0:2], a["norm_mlp_g"], m_dram, ident, h2, hm_hi, hm_lo)
            stage_mlp(nc, ps, a["w_up"], a["w_down"], a["norm_final_g"], h2, hm_hi, hm_lo, wide, out)


INPUTS = ["x", "meta_tokens", "norm_mix_g", "w_in", "lambda_q1", "lambda_k1", "lambda_q2", "lambda_k2", "subln_g",
          "w_out_a", "w_out_b", "w_out", "norm_mlp_g", "w_up", "w_down", "norm_final_g"]


def rope_tables():
    inv = (np.float32(ROPE_THETA) ** (-np.arange(0, HD, 2, dtype=np.float32) / np.float32(HD))).astype(np.float32)
    ang = inv[:, None] * np.arange(L, dtype=np.float32)[None, :]
    cos, sin = np.cos(ang).astype(np.float32), np.sin(ang).astype(np.float32)
    return np.concatenate([cos] * 4, axis=0), np.concatenate([-sin, sin, -sin, sin], axis=0)


def kernel(**inputs):
    import concourse.bacc as _bacc
    from concourse.bass_utils import run_bass_kernel_spmd as _run

    nc = _bacc.Bacc("TRN2", target_bir_lowering=False, num_devices=1)
    arrays, aps = {}, {}
    for name in INPUTS:
        arrays[f"in_{name}"] = np.ascontiguousarray(inputs[name])
        aps[name] = nc.dram_tensor(f"in_{name}", arrays[f"in_{name}"].shape, F32, kind="ExternalInput").ap()
    tables = []
    for name, table in zip(("rope_cos", "rope_sin"), rope_tables()):
        arrays[name] = table
        tables.append(nc.dram_tensor(name, table.shape, F32, kind="ExternalInput").ap())
    out = nc.dram_tensor("out_0", (1, SEQ, D), F32, kind="ExternalOutput").ap()
    layer(nc, aps, tables[0], tables[1], out)
    r = _run(nc, [arrays], core_ids=[0])
    return r.results[0]["out_0"]
```
